# Optimizing a Trainium2 kernel written in Bass

```python
import jax, jax.numpy as jnp
from jax import lax
import numpy as np

D_MODEL = 2048
BATCH = 1
SEQ = 256
DEPTH = 2

N_A_LAYERS = DEPTH // 2
N_B_LAYERS = DEPTH - N_A_LAYERS
GLA_HEADS = 4
GLA_DK = D_MODEL // 2
GLA_DV = D_MODEL
GLA_HEAD_K = GLA_DK // GLA_HEADS
GLA_HEAD_V = GLA_DV // GLA_HEADS
GLA_GATE_RANK = 16
GLA_TAU = 16.0
GLA_CHUNK = 64
GLA_IN = 2 * GLA_DK + 2 * GLA_DV + GLA_GATE_RANK
MLA_HEADS = 16
MLA_Q_LORA = 512
MLA_KV_LORA = 512
MLA_NOPE = 128
MLA_ROPE = 64
MLA_V = 128
ROPE_THETA = 10000.0
Q_BLOCK = 128
D_FF = 4 * D_MODEL
RMS_EPS = 1e-6

kernel_name = 'yoco_gla_mla_hybrid'

def rmsnorm(x, g):
    xf = x.astype(jnp.float32)
    y = xf * lax.rsqrt(jnp.mean(xf * xf, axis=-1, keepdims=True) + RMS_EPS)
    return (y * g.astype(jnp.float32)).astype(x.dtype)

def rope(x, positions):
    r = x.shape[-1]
    half = r // 2
    freqs = ROPE_THETA ** (-jnp.arange(0, r, 2, dtype=jnp.float32) / r)
    ang = positions.astype(jnp.float32)[..., None] * freqs
    cos, sin = jnp.cos(ang)[:, :, None, :], jnp.sin(ang)[:, :, None, :]
    x1, x2 = x[..., :half].astype(jnp.float32), x[..., half:].astype(jnp.float32)
    return jnp.concatenate([x1 * cos - x2 * sin, x1 * sin + x2 * cos], axis=-1).astype(x.dtype)

def _to_chunks(t, n_heads):
    b, s, hd = t.shape
    return t.reshape(b, s // GLA_CHUNK, GLA_CHUNK, n_heads, hd // n_heads).transpose(1, 0, 3, 2, 4)

def gla_mix(xn, w_in, w_gate_up, b_gate, g_norm, w_out):
    bsz, seq, _ = xn.shape
    f32 = jnp.float32
    q, k, v, r, g_low = jnp.split(xn @ w_in, [GLA_DK, 2 * GLA_DK, 2 * GLA_DK + GLA_DV, 2 * GLA_DK + 2 * GLA_DV], axis=-1)
    log_a = jax.nn.log_sigmoid((g_low @ w_gate_up + b_gate).astype(f32)) / GLA_TAU
    qc = _to_chunks(q.astype(f32) * GLA_HEAD_K ** -0.5, GLA_HEADS)
    kc = _to_chunks(k.astype(f32), GLA_HEADS)
    vc = _to_chunks(v.astype(f32), GLA_HEADS)
    gc = _to_chunks(log_a, GLA_HEADS)
    causal = jnp.tril(jnp.ones((GLA_CHUNK, GLA_CHUNK), dtype=bool))

    def step(state, inp):
        qb, kb, vb, gb = inp
        b = jnp.cumsum(gb, axis=2)
        o_inter = jnp.einsum('bhcd,bhde->bhce', qb * jnp.exp(b), state)
        diff = b[:, :, :, None, :] - b[:, :, None, :, :]
        decay = jnp.exp(jnp.where(causal[:, :, None], diff, -jnp.inf))
        scores = jnp.einsum('bhid,bhjd,bhijd->bhij', qb, kb, decay)
        o_intra = jnp.einsum('bhij,bhje->bhie', scores, vb)
        b_last = b[:, :, -1:, :]
        state = state * jnp.exp(b_last)[:, :, 0, :, None] + jnp.einsum('bhcd,bhce->bhde', kb * jnp.exp(b_last - b), vb)
        return state, o_inter + o_intra

    state0 = jnp.zeros((bsz, GLA_HEADS, GLA_HEAD_K, GLA_HEAD_V), f32)
    _, o = lax.scan(step, state0, (qc, kc, vc, gc))
    o = o.transpose(1, 0, 3, 2, 4).reshape(bsz, seq, GLA_HEADS, GLA_HEAD_V)
    o = rmsnorm(o, g_norm).reshape(bsz, seq, GLA_DV).astype(xn.dtype)
    return (o * jax.nn.silu(r)) @ w_out

def mla_shared_kv(h, positions, norm_in, w_dkv, kv_norm, w_uk, w_uv):
    bsz, seq, _ = h.shape
    ckv = rmsnorm(h, norm_in) @ w_dkv
    c = rmsnorm(ckv[..., :MLA_KV_LORA], kv_norm)
    k_rope = rope(ckv[..., None, MLA_KV_LORA:], positions)[:, :, 0, :]
    k_nope = (c @ w_uk).reshape(bsz, seq, MLA_HEADS, MLA_NOPE)
    v = (c @ w_uv).reshape(bsz, seq, MLA_HEADS, MLA_V)
    return k_nope, k_rope, v

def mla_mix(xn, positions, w_dq, q_norm, w_uq, w_o, k_nope, k_rope, v):
    bsz, seq, _ = xn.shape
    cq = rmsnorm(xn @ w_dq, q_norm)
    q = (cq @ w_uq).reshape(bsz, seq, MLA_HEADS, MLA_NOPE + MLA_ROPE)
    q_nope = q[..., :MLA_NOPE]
    q_rope = rope(q[..., MLA_NOPE:], positions)
    nb = seq // Q_BLOCK
    scale = (MLA_NOPE + MLA_ROPE) ** -0.5
    key_idx = jnp.arange(seq)

    def blocks(t):
        return t.reshape(bsz, nb, Q_BLOCK, *t.shape[2:]).swapaxes(0, 1)

    def attend(inp):
        qn, qr, blk = inp
        s = jnp.einsum('bqhd,bkhd->bhqk', qn, k_nope) + jnp.einsum('bqhr,bkr->bhqk', qr, k_rope)
        q_idx = blk * Q_BLOCK + jnp.arange(Q_BLOCK)
        mask = key_idx[None, :] <= q_idx[:, None]
        p = jax.nn.softmax(jnp.where(mask, s.astype(jnp.float32) * scale, -jnp.inf), axis=-1).astype(v.dtype)
        return jnp.einsum('bhqk,bkhd->bqhd', p, v)

    o = lax.map(attend, (blocks(q_nope), blocks(q_rope), jnp.arange(nb)))
    o = o.swapaxes(0, 1).reshape(bsz, seq, MLA_HEADS * MLA_V)
    return o @ w_o

def sq_relu_mlp(xn, w1, w2):
    return jnp.square(jax.nn.relu(xn @ w1)) @ w2

def setup_inputs(seed: int = 0) -> dict:
    key = jax.random.key(seed)
    ks = jax.random.split(key, 24)
    f32 = jnp.float32

    def dense(k, shape, fan_in):
        return jax.random.normal(k, shape, f32) * fan_in ** -0.5

    def gain(k, shape):
        return 1.0 + 0.02 * jax.random.normal(k, shape, f32)

    return {
        'x': jax.random.normal(ks[0], (BATCH, SEQ, D_MODEL), f32),
        'positions': jnp.broadcast_to(jnp.arange(SEQ, dtype=jnp.int32), (BATCH, SEQ)),
        'norm_mix': gain(ks[1], (DEPTH, D_MODEL)),
        'norm_mlp': gain(ks[2], (DEPTH, D_MODEL)),
        'gla_w_in': dense(ks[3], (N_A_LAYERS, D_MODEL, GLA_IN), D_MODEL),
        'gla_w_gate_up': dense(ks[4], (N_A_LAYERS, GLA_GATE_RANK, GLA_DK), GLA_GATE_RANK),
        'gla_b_gate': 0.01 * jax.random.normal(ks[5], (N_A_LAYERS, GLA_DK), f32),
        'gla_norm': gain(ks[6], (N_A_LAYERS, GLA_HEAD_V)),
        'gla_w_out': dense(ks[7], (N_A_LAYERS, GLA_DV, D_MODEL), GLA_DV),
        'kv_norm_in': gain(ks[8], (D_MODEL,)),
        'mla_w_dkv': dense(ks[9], (D_MODEL, MLA_KV_LORA + MLA_ROPE), D_MODEL),
        'mla_kv_norm': gain(ks[10], (MLA_KV_LORA,)),
        'mla_w_uk': dense(ks[11], (MLA_KV_LORA, MLA_HEADS * MLA_NOPE), MLA_KV_LORA),
        'mla_w_uv': dense(ks[12], (MLA_KV_LORA, MLA_HEADS * MLA_V), MLA_KV_LORA),
        'mla_w_dq': dense(ks[13], (N_B_LAYERS, D_MODEL, MLA_Q_LORA), D_MODEL),
        'mla_q_norm': gain(ks[14], (N_B_LAYERS, MLA_Q_LORA)),
        'mla_w_uq': dense(ks[15], (N_B_LAYERS, MLA_Q_LORA, MLA_HEADS * (MLA_NOPE + MLA_ROPE)), MLA_Q_LORA),
        'mla_w_o': dense(ks[16], (N_B_LAYERS, MLA_HEADS * MLA_V, D_MODEL), MLA_HEADS * MLA_V),
        'mlp_w1': dense(ks[17], (DEPTH, D_MODEL, D_FF), D_MODEL),
        'mlp_w2': dense(ks[18], (DEPTH, D_FF, D_MODEL), D_FF),
        'final_norm': gain(ks[19], (D_MODEL,)),
    }

def reference(x, positions, norm_mix, norm_mlp, gla_w_in, gla_w_gate_up, gla_b_gate, gla_norm, gla_w_out,
              kv_norm_in, mla_w_dkv, mla_kv_norm, mla_w_uk, mla_w_uv,
              mla_w_dq, mla_q_norm, mla_w_uq, mla_w_o, mlp_w1, mlp_w2, final_norm):
    h = x
    shared = None
    for layer in range(DEPTH):
        if layer < N_A_LAYERS:
            a = layer
            h = h + gla_mix(rmsnorm(h, norm_mix[layer]), gla_w_in[a], gla_w_gate_up[a], gla_b_gate[a],
                            gla_norm[a], gla_w_out[a])
        else:
            if layer == N_A_LAYERS:
                shared = mla_shared_kv(h, positions, kv_norm_in, mla_w_dkv, mla_kv_norm, mla_w_uk, mla_w_uv)
            b = layer - N_A_LAYERS
            k_nope, k_rope, v = shared
            h = h + mla_mix(rmsnorm(h, norm_mix[layer]), positions, mla_w_dq[b], mla_q_norm[b], mla_w_uq[b],
                            mla_w_o[b], k_nope, k_rope, v)
        h = h + sq_relu_mlp(rmsnorm(h, norm_mlp[layer]), mlp_w1[layer], mlp_w2[layer])
    return rmsnorm(h, final_norm)


_drawn_inputs = setup_inputs


def setup_inputs(seed=0):
    import zlib

    import numpy as np

    out = dict(_drawn_inputs(seed))
    spreads = {}
    factors = {'gla_b_gate': 8.0,
     'gla_norm': 4.715,
     'kv_norm_in': 8.0,
     'mla_kv_norm': 8.0,
     'mla_q_norm': 8.0,
     'final_norm': 2.913}
    for name, (base, spread) in spreads.items():
        noise = np.random.default_rng([zlib.crc32(name.encode()), seed]).standard_normal(out[name].shape)
        drawn = base * np.exp(spread * noise) if base else spread * noise
        out[name] = __import__('jax').numpy.asarray(drawn.astype(out[name].dtype))
    for name, factor in factors.items():
        out[name] = (out[name] * factor).astype(out[name].dtype)
    return out
```

```python
from contextlib import ExitStack

import numpy as np

import concourse.bass as bass
from concourse import mybir

F32 = mybir.dt.float32
F32R = mybir.dt.float32r
I32 = mybir.dt.int32
ALU = mybir.AluOpType
ACT = mybir.ActivationFunctionType
AX = mybir.AxisListType

P = 128
S = 256
TB = S // P
D = 2048
KT = D // P
EPS = 1e-6

GH = 4
GK = D // 2
HK = GK // GH
HV = D // GH
RANK = 16
TAU = 16.0
LEVELS = [64, 32, 16, 8, 4, 2, 1]

MH = 16
LORA = 512
LT = LORA // P
NOPE = 128
ROPE = 64
QH = NOPE + ROPE
PAIRS = MH // 2
THETA = 10000.0
MLA_SCALE = float(QH) ** -0.5
MASKED = -1e30

D_FF = 4 * D
SLAB = 2048
SLABS = D_FF // SLAB

ROUND = 1.5 * 2.0 ** 23
TWO_PI = [6.28125, 0.0019350051879882812, 2.0 * np.pi - 6.28125 - 0.0019350051879882812]

HC = 256
HK4 = 4
HF = HK4 * HC
RING = 4
UNITS = KT // HK4
PANEL = 2 * UNITS
PANELS = D // (2 * HC)
HEAD_HALVES = 3 * PANEL
H_GLA, G_GLA = 0, 0
H_OUT, G_OUT = H_GLA + GH * HEAD_HALVES, G_GLA + GH * 6
H_MLP0, G_MLP0 = H_OUT + PANELS * PANEL, G_OUT + PANELS * 2
SLAB_HALVES, SLAB_GROUPS = 2 * PANELS * PANEL, 4 * PANELS
H_DKV, G_DKV = H_MLP0 + SLABS * SLAB_HALVES, G_MLP0 + SLABS * SLAB_GROUPS
H_DQ, G_DQ = H_DKV + PANEL, G_DKV + 2
H_PAIR, G_PAIR = H_DQ + PANEL, G_DQ + 2
H_WO, G_WO = H_PAIR + PAIRS * 4, G_PAIR + PAIRS * 4
H_MLP1, G_MLP1 = H_WO + PANELS * PANEL, G_WO + PANELS * 2
C_GLA = 0
C_MLP0 = C_GLA + GH * 6
UP_GROUPS = SLABS * PANELS * 2
C_DKV = C_MLP0 + UP_GROUPS
C_DQ = C_DKV + 2
C_PAIR = C_DQ + 2
C_MLP1 = C_PAIR + PAIRS * 4
X_GLA, X_MLP0, X_KV, X_Q, X_C, X_CQ, X_MLP1 = 0, 16, 32, 48, 64, 68, 72
N_MIX0, N_MIX1, N_MLP0, N_MLP1, N_KVIN, N_FIN, N_GLA, N_C, N_CQ = 0, 16, 32, 48, 64, 80, 96, 100, 104
N_GAINS = 108
R_OUT, R_MLP0 = 0, 2 * PANELS
R_WO = R_MLP0 + SLABS * PANELS * 2
R_MLP1 = R_WO + 2 * PANELS
(ST_MIX0, ST_MLP0, ST_MIX1, ST_C, ST_CQ, ST_MLP1, ST_FIN) = range(7)
PLACES = [[0, 1, 2, 3, 5, 6, 7], [0, 1, 2, 3, 4, 5, 6]]
SUFFIX, PREFIX = 4, 7


def constants():
    s, t = np.arange(P)[:, None], np.arange(P)[None, :]
    sums = {}
    masks = []
    for m in LEVELS:
        mid = (t // (2 * m)) * 2 * m + m
        upper = (t % (2 * m)) >= m
        sums[m] = np.where(upper, (s >= mid) & (s <= t), (s > t) & (s < mid))
        same = (s // (2 * m)) == (t // (2 * m))
        masks.append(same & ((t % (2 * m)) >= m) & ((s % (2 * m)) < m))
    masks.append(s == t)
    suffix, prefix = s > t, s <= t
    order = [sums[m] for m in LEVELS[:4]] + [suffix] + [sums[m] for m in LEVELS[4:]] + [prefix]
    rot = np.zeros((P, P))
    half = ROPE // 2
    for b in range(0, P, ROPE):
        for d in range(half):
            rot[b + d + half, b + d] = -1.0
            rot[b + d, b + d + half] = 1.0
    causal = np.zeros((P, 3 * P))
    later = np.where(t > s, MASKED, 0.0)
    causal[:, 0:P] = later
    causal[:, 2 * P:] = later
    freqs = (THETA ** (-np.arange(0, ROPE, 2, dtype=np.float64) / ROPE)).astype(np.float32)
    pad = np.zeros((P, P))
    pad[:, RANK] = 1.0
    return {
        "c_sums": np.stack(order, 1).reshape(P, 9 * P).astype(np.float32),
        "c_masks": np.stack(masks, 1).reshape(P, 8 * P).astype(np.float32),
        "c_ident": np.eye(P, dtype=np.float32),
        "c_rot": rot.astype(np.float32),
        "c_causal": causal.astype(np.float32),
        "c_freqs": np.tile(freqs, P // half)[:, None].copy(),
        "c_bias_row": pad.astype(np.float32),
    }


def build(nc, t, out):
    ctx = ExitStack()
    with ctx:
        def sb(name, shape, dt=F32):
            return ctx.enter_context(nc.sbuf_tensor(name, shape, dt))

        def sem(name):
            return ctx.enter_context(nc.semaphore(name))

        resid = sb("resid", [P, KT, S])
        xa = sb("xa", [P, KT, 2, S], F32R)
        xb = sb("xb", [P, KT, 2, S], F32R)
        stage = sb("stage", [P, RING, HF])
        wts = sb("wts", [P, RING, HK4, 2, HC], F32R)
        temps = sb("temps", [P, 16 * S])
        sqs = sb("sqs", [P, S])
        rstd = sb("rstd", [P, S + TB])
        ident = sb("ident", [P, P])
        ones = sb("ones", [P, P])
        gains = sb("gains", [P, N_GAINS])
        power = sb("power", [P, 1])
        scratch = sb("scratch", [P, 11136])
        scratch_r = sb("scratch_r", [P, 4096], F32R)

        def carve(tensor, at=0):
            end = [at]

            def take(*dims):
                n = int(np.prod(dims))
                v = tensor[:, end[0]:end[0] + n]
                end[0] += n
                assert end[0] <= tensor.shape[1]
                if len(dims) == 1:
                    return v
                names = "abcd"[:len(dims)]
                return v.rearrange(f"p ({' '.join(names)}) -> p {' '.join(names)}",
                                   **dict(zip(names, dims)))

            return take

        take = carve(temps)
        corr, total = take(2, 2, S), take(2, 2, S)
        sq_a, sq_b = take(4, S), take(4, S)
        x_nat = temps[:, :].rearrange("p (b d) -> p b d", b=TB)

        take = carve(scratch)
        dec = take(2, 8, P)
        qdec = take(2, 8, P)
        q_sb, k_sb = take(2, S), take(2, S)
        v_sb = take(TB, HV)
        r_sb, e_sb, o_sb = take(4, S), take(4, S), take(4, S)
        masks = take(8, P)
        kx = take(2, P)
        att = take(3 * P)
        rstd_o = take(S)
        w_up = scratch[:, 0:GK]
        z_sb = scratch[:, 2048:2048 + TB * GK]
        g_sb = scratch[:, 0:TB * GK]
        sums_in = scratch[:, 4096:4096 + 9 * P]
        low_nat = r_sb[:, 0, :].rearrange("p (b c) -> p b c", b=TB)
        low_t = r_sb[:, 1, :]
        side_in0 = r_sb[:, 2, :]
        low_tmp = r_sb[:, 3, :]
        gains_in = e_sb[:, 0, 0:P]
        take = carve(scratch_r)
        gate = take(TB, 2, HK)
        sums = take(9, P)
        side0 = take(2, KT * RANK)

        take = carve(scratch)
        kt_sb, vt_sb = take(2, 2, S), take(2, TB, S)
        cos, sin = take(S), take(S)
        causal = take(3 * P)
        rot = take(P)
        lat = take(LT, S)
        keys_r = take(2, S)
        qn_sb = take(2, 2, S)
        qr_sb = take(2, S)
        raw_r, cos_r, sin_r = take(S), take(S), take(S)
        sc_sb, pr_sb, pt_sb = take(2, 3 * P), take(2, 3 * P), take(2, 3 * P)
        mx, nmx, den, rden = take(4), take(4), take(4), take(4)
        freqs = take(2)
        rstd_c = take(S)
        side_in1 = take(KT * ROPE)
        kr_nat = sc_sb[:, 0, 0:TB * P].rearrange("p (b c) -> p b c", b=TB)
        kr_tmp = pr_sb[:, 0, 0:TB * ROPE].rearrange("p (b c) -> p b c", b=TB)
        ang, turns, pos_i = pt_sb[:, 0, 0:S], pt_sb[:, 1, 0:S], cos.bitcast(I32)
        take = carve(scratch_r)
        xc, xq = take(LT, 2, S), take(LT, 2, S)
        side1 = scratch_r[:, 2048:4096].rearrange("p (h n) -> p h n", h=2)

        take = carve(scratch)
        act, sq_h = take(2, 2, S), take(2, 2, S)
        o_nat = take(TB, D)
        y_sb = scratch[:, 6144:6144 + KT * S].rearrange("p (t s) -> p t s", t=KT)

        ps = ctx.enter_context(nc.psum_tensor("ps", [P, 8, 512], F32))

        s_ident, s_xin = sem("s_ident"), sem("s_xin")
        s_gin, s_side0, s_up, s_masks, s_sums = (
            sem(n) for n in ("s_gin", "s_side0", "s_up", "s_masks", "s_sums"))
        s_side1, s_causal, s_rotm, s_freqs, s_pos = (
            sem(n) for n in ("s_side1", "s_causal", "s_rotm", "s_freqs", "s_pos"))
        s_landed = [sem(f"s_landed{i}") for i in range(RING)]
        s_high = sem("s_high")
        s_split = sem("s_split")
        s_mult = sem("s_mult")
        s_read = sem("s_read")
        s_corr = sem("s_corr")
        s_main = sem("s_main")
        s_xhi, s_x = sem("s_xhi"), sem("s_x")
        s_sqs = sem("s_sqs")
        s_stat = sem("s_stat")
        s_mean = sem("s_mean")
        s_rstd = sem("s_rstd")
        s_act, s_acthi, s_acts = sem("s_act"), sem("s_acthi"), sem("s_acts")
        s_hid = sem("s_hid")
        s_dve, s_pool = sem("s_dve"), sem("s_pool")
        s_ones, s_pad, s_tr, s_trc, s_gtr, s_gains = (
            sem(n) for n in ("s_ones", "s_pad", "s_tr", "s_trc", "s_gtr", "s_gains"))
        s_sidehi, s_sidelo, s_low, s_lownat, s_lowt, s_lowtc = (
            sem(n) for n in ("s_sidehi", "s_sidelo", "s_low", "s_lownat", "s_lowt", "s_lowtc"))
        s_z, s_zact, s_g, s_ghi, s_glo, s_sumsr = (
            sem(n) for n in ("s_z", "s_zact", "s_g", "s_ghi", "s_glo", "s_sumsr"))
        s_y, s_fin, s_finc, s_out = (sem(n) for n in ("s_y", "s_fin", "s_finc", "s_out"))
        s_gcur = sem("s_gcur")
        s_sum = sem("s_sum")
        s_dec = sem("s_dec")
        s_q, s_k, s_r = sem("s_q"), sem("s_k"), sem("s_r")
        s_v = sem("s_v")
        s_qd, s_kd = sem("s_qd"), sem("s_kd")
        s_kx = sem("s_kx")
        s_sc = sem("s_sc")
        s_msk = sem("s_msk")
        s_att = sem("s_att")
        s_o, s_osq, s_ocp, s_ost, s_ostd, s_orstd = (
            sem(n) for n in ("s_o", "s_osq", "s_ocp", "s_ost", "s_ostd", "s_orstd"))
        s_er, s_eone, s_erec = sem("s_er"), sem("s_eone"), sem("s_erec")
        s_gated = sem("s_gated")
        s_lat, s_laty, s_krn, s_krt, s_krc, s_krot, s_krz = (
            sem(n) for n in ("s_lat", "s_laty", "s_krn", "s_krt", "s_krc", "s_krot", "s_krz"))
        s_ang, s_trig, s_keysr = sem("s_ang"), sem("s_trig"), sem("s_keysr")
        s_raw, s_rot, s_cosr, s_sinr, s_qr = (
            sem(n) for n in ("s_raw", "s_rot", "s_cosr", "s_sinr", "s_qr"))
        s_dots, s_ms, s_max, s_nmx, s_exp, s_rden, s_pr = (
            sem(n) for n in ("s_dots", "s_ms", "s_max", "s_nmx", "s_exp", "s_rden", "s_pr"))
        s_pt, s_ptc, s_ov, s_ohi, s_ox = (
            sem(n) for n in ("s_pt", "s_ptc", "s_ov", "s_ohi", "s_ox"))

        def by_chunk(w):
            return w.rearrange("(t p) n -> p t n", p=P)

        w_in, w_out = by_chunk(t["gla_w_in"][0]), by_chunk(t["gla_w_out"][0])
        w1 = [by_chunk(t["mlp_w1"][i]) for i in range(2)]
        w2 = [by_chunk(t["mlp_w2"][i]) for i in range(2)]
        w_dkv, w_dq = by_chunk(t["mla_w_dkv"]), by_chunk(t["mla_w_dq"][0])
        w_uk, w_uv, w_o = by_chunk(t["mla_w_uk"]), by_chunk(t["mla_w_uv"]), by_chunk(t["mla_w_o"][0])
        w_uq = t["mla_w_uq"][0].rearrange("(t p) (h c) -> p t h c", p=P, c=QH)
        x_dram = t["x"][0].rearrange("(b p) d -> p b d", p=P)
        out_dram = out[0].rearrange("(b p) d -> p b d", p=P)

        block = ctx.enter_context(nc.Block())

        @block.sync
        def _(sp):
            def load(h, j, src, n=HF):
                slot = j % RING
                sp.wait_ge(s_split, h + j + 1)
                dst = stage[:, slot, 0:n]
                if len(src.shape) == 3:
                    dst = dst.rearrange("p (t n) -> p t n", t=src.shape[1])
                    sp.dma_start(dst, src).then_inc(s_landed[slot], 16)
                else:
                    dst = dst.rearrange("p (t h n) -> p t h n", t=src.shape[1], h=src.shape[2])
                    for hd in range(2):
                        sp.dma_start(dst[:, :, hd], src[:, :, hd]).then_inc(s_landed[slot], 16)

            def panel(h, w, row, col0, col1):
                for u in range(UNITS):
                    for c, col in enumerate((col0, col1)):
                        load(h, 2 * u + c, w[:, bass.ds(row + HK4 * u, HK4), bass.ds(col, HC)])

            def plain_panels(h, w):
                with sp.Fori(0, PANELS) as p:
                    panel(h + p * PANEL, w, 0, p * 2 * HC, p * 2 * HC + HC)

            def mlp(layer, h0):
                with sp.Fori(0, SLABS) as s:
                    h = h0 + s * SLAB_HALVES
                    with sp.Fori(0, PANELS) as p:
                        col = s * SLAB + p * 2 * HC
                        panel(h + p * PANEL, w1[layer], 0, col, col + HC)
                    with sp.Fori(0, PANELS) as p:
                        panel(h + PANELS * PANEL + p * PANEL, w2[layer], s * KT,
                              p * 2 * HC, p * 2 * HC + HC)

            with sp.Fori(0, GH) as i:
                h = H_GLA + i * HEAD_HALVES
                panel(h, w_in, 0, i * HK, GK + i * HK)
                v0 = 2 * GK + i * HV
                panel(h + PANEL, w_in, 0, v0, v0 + HC)
                r0 = 2 * GK + D + i * HV
                panel(h + 2 * PANEL, w_in, 0, r0, r0 + HC)
            plain_panels(H_OUT, w_out)
            sp.wait_ge(s_gated, 5 * GH + 1)
            sp.dma_start(side_in1.rearrange("p (t n) -> p t n", t=KT),
                         w_dkv[:, :, LORA:LORA + ROPE]).then_inc(s_side1, 16)
            sp.dma_start(causal, t["c_causal"]).then_inc(s_causal, 16)
            sp.dma_start(rot, t["c_rot"]).then_inc(s_rotm, 16)
            sp.dma_start(freqs[:, 0:1], t["c_freqs"]).then_inc(s_freqs, 16)
            sp.dma_start(pos_i, t["positions"][0:1, :].broadcast_to([P, S])).then_inc(s_pos, 16)
            mlp(0, H_MLP0)
            panel(H_DKV, w_dkv, 0, 0, HC)
            panel(H_DQ, w_dq, 0, 0, HC)
            with sp.Fori(0, PAIRS) as i:
                h = H_PAIR + i * 4
                load(h, 0, w_uk[:, :, bass.ds(i * HC, HC)])
                load(h, 1, w_uv[:, :, bass.ds(i * HC, HC)])
                load(h, 2, w_uq[:, :, bass.ds(i * 2, 2), 0:NOPE])
                load(h, 3, w_uq[:, :, bass.ds(i * 2, 2), NOPE:QH], n=HF // 2)
            plain_panels(H_WO, w_o)
            mlp(1, H_MLP1)
            for n in range(8):
                b, c = n // 4, n % 4
                sp.wait_ge(s_finc, n + 1)
                sp.dma_start(out_dram[:, b, c * 512:(c + 1) * 512],
                             o_nat[:, b, c * 512:(c + 1) * 512]).then_inc(s_out, 16)
            sp.wait_ge(s_out, 8 * 16)

        @block.gpsimd
        def _(pool):
            steps = [0]

            def step(ins):
                steps[0] += 1
                ins.then_inc(s_pool, 1)
                pool.wait_ge(s_pool, steps[0])

            def squares(st, src, chunks, dst=rstd[:, 0:S]):
                if st:
                    pool.wait_ge(s_stat, st)
                step(pool.tensor_tensor(sq_a, src[:, 0:4, :], src[:, 0:4, :], ALU.mult))
                for c in range(4, chunks, 4):
                    part = src[:, c:c + 4, :]
                    step(pool.tensor_tensor(sq_b, part, part, ALU.mult))
                    step(pool.tensor_tensor(sq_a, sq_a, sq_b, ALU.add))
                step(pool.tensor_tensor(sq_a[:, 0:2, :], sq_a[:, 0:2, :], sq_a[:, 2:4, :], ALU.add))
                pool.tensor_tensor(sqs[:, :], sq_a[:, 0, :], sq_a[:, 1, :], ALU.add)\
                    .then_inc(s_sqs, 1)
                pool.wait_ge(s_mean, st + 1)
                pool.tensor_tensor(dst, dst, power[:, 0:1].broadcast_to(list(dst.shape)), ALU.pow)\
                    .then_inc(s_rstd, 1)

            def mlp(k0):
                with pool.Fori(0, SLABS) as s:
                    with pool.Fori(0, PANELS) as p:
                        for c in range(2):
                            k = k0 + s * (PANELS * 2) + p * 2 + c
                            pool.wait_ge(s_act, k + 1)
                            pool.wait_ge(s_hid, k + 1)
                            pool.tensor_tensor(sq_h[:, c], act[:, c], act[:, c], ALU.mult)\
                                .then_inc(s_acts, 1)
                            pool.wait_ge(s_acts, k + 1)
                            pool.wait_ge(s_acthi, k + 1)
                            hid = xb[:, bass.ds(p * 4 + 2 * c, 2)]
                            pool.tensor_tensor(hid[:, :, 1, :], sq_h[:, c],
                                               hid[:, :, 0, :].bitcast(F32), ALU.subtract)\
                                .then_inc(s_hid, 1)

            pool.sem_inc(s_hid, 2)
            for free in (s_orstd, s_pr, s_gated):
                pool.sem_inc(free, 1)
            step(pool.memset(power[:, :], -0.5))
            pool.memset(ones[:, :], 1.0).then_inc(s_ones, 1)
            step(pool.memset(low_nat, 0.0))
            step(pool.memset(low_nat[:, :, RANK:RANK + 1], 1.0))
            pool.memset(w_up, 0.0).then_inc(s_pad, 1)
            pool.wait_ge(s_trc, 8)
            squares(ST_MIX0, resid, KT, rstd[:, :])

            with pool.Fori(0, GH) as i:
                for b in range(TB):
                    pool.wait_ge(s_dec, 4 * i + 2 * b + 3)
                    pool.wait_ge(s_k, i + 1)
                    pool.wait_ge(s_qd, 2 * i + b + 1)
                    if b == 0:
                        pool.tensor_tensor(kx, dec[:, :, SUFFIX, :], k_sb[:, :, 0:P], ALU.mult)\
                            .then_inc(s_kx, 1)
                        pool.wait_ge(s_kx, i + 1)
                    for d in range(2):
                        keys = k_sb[:, d:d + 1, b * P:(b + 1) * P].broadcast_to([P, 8, P])
                        ins = pool.tensor_tensor(dec[:, d], dec[:, d], keys, ALU.mult)
                    ins.then_inc(s_kd, 1)
                pool.wait_ge(s_ostd, i + 1)
                pool.tensor_tensor(rstd_o, rstd_o, power[:, 0:1].broadcast_to([P, S]), ALU.pow)\
                    .then_inc(s_orstd, 1)
                pool.wait_ge(s_orstd, i + 2)
                g = 5 * i
                pool.wait_ge(s_erec, i + 1)
                pool.tensor_tensor(r_sb, r_sb, e_sb, ALU.mult).then_inc(s_gated, 1)
                pool.wait_ge(s_gated, g + 2)
                pool.wait_ge(s_ocp, i + 2)
                pool.tensor_tensor(o_sb, o_sb, r_sb, ALU.mult).then_inc(s_gated, 1)
                pool.wait_ge(s_gated, g + 3)
                per_token = rstd_o.rearrange("p (o s) -> p o s", o=1).broadcast_to([P, 4, S])
                head = xb[:, bass.ds(4 * i, 4)]
                pool.tensor_tensor(head[:, :, 0, :], o_sb, per_token, ALU.mult).then_inc(s_gated, 1)
                pool.wait_ge(s_gated, g + 4)
                pool.tensor_tensor(o_sb, o_sb, per_token, ALU.mult).then_inc(s_gated, 1)
                pool.wait_ge(s_gated, g + 5)
                pool.tensor_tensor(head[:, :, 1, :], o_sb, head[:, :, 0, :].bitcast(F32),
                                   ALU.subtract).then_inc(s_gated, 1)

            pool.wait_ge(s_read, G_MLP0 + 2)
            squares(ST_MLP0, resid, KT)
            mlp(0)
            pool.wait_ge(s_read, G_DKV + 2)
            squares(ST_MIX1, resid, KT, rstd[:, :])
            pool.memset(keys_r, 0.0).then_inc(s_krz, 1)
            pool.wait_ge(s_lat, 2)
            squares(ST_C, lat, LT, rstd_c)
            pool.wait_ge(s_lat, 4)
            squares(ST_CQ, lat, LT, rstd_c)

            def slot(i, b, proj=True, attn=True):
                if attn:
                    pool.wait_ge(s_rden, i)
                    for h in range(2):
                        for blk in range(2):
                            part = pr_sb[:, h, 0:P] if blk == 0 else pr_sb[:, h, P:3 * P]
                            col = 2 * blk + h
                            by = rden[:, col:col + 1].broadcast_to(list(part.shape))
                            ins = pool.tensor_tensor(part, part, by, ALU.mult)
                    ins.then_inc(s_pr, 1)
                if proj:
                    pool.wait_ge(s_raw, i + 1)
                    pool.wait_ge(s_qr, i)
                    pool.tensor_tensor(cos_r, raw_r, cos, ALU.mult).then_inc(s_cosr, 1)
                    pool.wait_ge(s_cosr, i + 1)
                    pool.wait_ge(s_sinr, i + 1)
                    pool.tensor_tensor(qr_sb[:, b, :], cos_r, sin_r, ALU.add).then_inc(s_qr, 1)

            slot(0, 0, attn=False)
            with pool.Fori(0, PAIRS // 2 - 1) as m:
                slot(m * 2 + 1, 1)
                slot(m * 2 + 2, 0)
            slot(PAIRS - 1, 1)
            slot(PAIRS, 0, proj=False)

            pool.wait_ge(s_read, G_MLP1 + 2)
            squares(ST_MLP1, resid, KT)
            mlp(UP_GROUPS)
            pool.wait_ge(s_read, G_MLP1 + SLABS * SLAB_GROUPS + 2)
            squares(ST_FIN, resid, KT, rstd[:, :])

        @block.scalar
        def _(act_e):
            sc = act_e

            pair_loads = [0]

            def high(h, j, n=HF, pairs=None):
                slot = j % RING
                more = 16 * (pair_loads[0] if pairs is None else pairs) if slot >= 2 else 0
                sc.wait_ge(s_landed[slot], h * (16 // RING) + (16 * (j // RING + 1) + more))
                sc.wait_ge(s_mult, h + j + 1)
                src = stage[:, slot, 0:n].rearrange("p (t n) -> p t n", n=HC)
                sc.activation(wts[:, slot, 0:n // HC, 0, :], src, ACT.Copy).then_inc(s_high, 1)

            def copy_corr(h, j, c, banks=2):
                sc.wait_ge(s_mult, h + j + 1 + RING)
                sc.activation(corr[:, c, 0:banks, :], ps[:, 2 * c:2 * c + banks, S:2 * S], ACT.Copy)\
                    .then_inc(s_corr, 1)

            def convert(src, gain, dst, c0, c1):
                for c in range(c0, c1):
                    sc.activation(dst[:, c, 0, :], src[:, c, :], ACT.Copy,
                                  scale=gains[:, gain + c:gain + c + 1]).then_inc(s_xhi, 1)

            def first_panel(h, gain, dst):
                for u in range(UNITS):
                    convert(resid, gain, dst, HK4 * u, HK4 * u + HK4)
                    high(h, 2 * u + 2)
                    high(h, 2 * u + 3)

            def highs(h, j0, j1):
                for j in range(j0, j1):
                    high(h, j)

            def up(h, p, k):
                for c in range(2):
                    copy_corr(h, PANEL - 2 + c, c)
                    sc.wait_ge(s_act, k + c + 1)
                    hid = xb[:, bass.ds(p * 4 + 2 * c, 2), 0, :]
                    sc.activation(hid, act[:, c], ACT.Square).then_inc(s_acthi, 1)

            def mlp(h0, k0, gain, last):
                first_panel(h0, gain, xa)
                up(h0, 0, k0)
                with sc.Fori(1, PANELS) as p:
                    highs(h0 + p * PANEL, 2, PANEL + 2)
                    up(h0 + p * PANEL, p, k0 + p * 2)
                with sc.Fori(PANELS, 2 * PANELS) as p:
                    highs(h0 + p * PANEL, 2, PANEL + 2)
                with sc.Fori(1, SLABS - 1 if last else SLABS) as s:
                    h = h0 + s * SLAB_HALVES
                    k = k0 + s * (2 * PANELS)
                    with sc.Fori(0, PANELS) as p:
                        highs(h + p * PANEL, 2, PANEL + 2)
                        up(h + p * PANEL, p, k + p * 2)
                    with sc.Fori(PANELS, 2 * PANELS) as p:
                        highs(h + p * PANEL, 2, PANEL + 2)
                if last:
                    h = h0 + (SLABS - 1) * SLAB_HALVES
                    k = k0 + (SLABS - 1) * (2 * PANELS)
                    with sc.Fori(0, PANELS) as p:
                        highs(h + p * PANEL, 2, PANEL + 2)
                        up(h + p * PANEL, p, k + p * 2)
                    with sc.Fori(PANELS, 2 * PANELS - 1) as p:
                        highs(h + p * PANEL, 2, PANEL + 2)
                    highs(h + (2 * PANELS - 1) * PANEL, 2, PANEL)

            for free in (s_dec, s_ocp, s_ptc):
                sc.sem_inc(free, 1)
            sc.dma_start(ident[:, :], t["c_ident"]).then_inc(s_ident, 16)
            for b in range(TB):
                sc.dma_start(x_nat[:, b, :], x_dram[:, b, :]).then_inc(s_xin, 16)
            row = 0
            for w in (t["norm_mix"], t["norm_mlp"], t["kv_norm_in"], t["final_norm"], t["gla_norm"],
                      t["mla_kv_norm"], t["mla_q_norm"]):
                flat = w if len(w.shape) == 1 else w.rearrange("a b -> (a b)")
                n = flat.shape[0] // P
                sc.dma_start(gains_in[row:row + n, :], flat.rearrange("(r c) -> r c", c=P))\
                    .then_inc(s_gin, 16)
                row += n
            sc.dma_start(side_in0.rearrange("p (t n) -> p t n", t=KT),
                         w_in[:, :, 2 * GK + 2 * D:]).then_inc(s_side0, 16)
            sc.dma_start(sums_in, t["c_sums"]).then_inc(s_sums, 16)
            sc.dma_start(masks, t["c_masks"].rearrange("p (l n) -> p l n", l=8))\
                .then_inc(s_masks, 16)
            sc.wait_ge(s_pad, 1)
            sc.dma_start(w_up[0:RANK, :], t["gla_w_gate_up"][0]).then_inc(s_up, 16)
            sc.dma_start(w_up[RANK:RANK + 1, :], t["gla_b_gate"]).then_inc(s_up, 16)

            sc.wait_ge(s_gains, 1)
            sc.wait_ge(s_trc, 8)
            convert(resid, N_MIX0, xa, 0, KT)
            sc.wait_ge(s_side0, 16)
            sc.activation(side0[:, 0, :], side_in0, ACT.Copy).then_inc(s_sidehi, 1)
            sc.wait_ge(s_sums, 16)
            sc.activation(sums.rearrange("p a b -> p (a b)"), sums_in, ACT.Copy)\
                .then_inc(s_sumsr, 1)
            highs(H_GLA, 0, 2)
            sc.wait_ge(s_z, 1)
            z_ps = ps[:, 4:8, :].rearrange("p b n -> p (b n)")
            sc.activation(z_sb, z_ps, ACT.Abs).then_inc(s_zact, 1)
            sc.wait_ge(s_zact, 1)
            sc.activation(z_sb, z_sb, ACT.Exp, scale=-1.0).then_inc(s_zact, 1)
            sc.wait_ge(s_zact, 2)
            sc.activation(z_sb, z_sb, ACT.Ln, bias=1.0).then_inc(s_zact, 1)
            sc.wait_ge(s_g, 1)
            g_by_head = g_sb.rearrange("p (b h n) -> p h b n", b=TB, h=GH)
            for i in range(GH):
                sc.activation(xb[:, 4 * i:4 * i + 2, 0, :], g_by_head[:, i], ACT.Copy)\
                    .then_inc(s_ghi, 1)
            sc.wait_ge(s_glo, GH)

            with sc.Fori(0, GH) as i:
                h = H_GLA + i * HEAD_HALVES

                def decays(b, d):
                    r = 2 * b + d
                    sc.wait_ge(s_sum, 4 * i + r + 1)
                    sc.activation(dec[:, d].rearrange("p (g l) n -> p g (l n)", g=2), ps[:, 4:6, :],
                                  ACT.Exp, scale=1.0 / TAU).then_inc(s_dec, 1)

                sc.activation(gate, xb[:, bass.ds(4 * i, 2)].bitcast(F32), ACT.Copy)\
                    .then_inc(s_gcur, 1)
                highs(h, 2, 8)
                decays(0, 0)
                highs(h, 8, 10)
                decays(0, 1)
                copy_corr(h, 6, 0)
                copy_corr(h, 7, 1)
                highs(h, 10, 18)
                decays(1, 0)
                copy_corr(h, 14, 0)
                copy_corr(h, 15, 1)
                decays(1, 1)
                highs(h, 18, 26)
                sc.wait_ge(s_o, i + 1)
                o_ps = ps[:, 6:8, :].rearrange("p b (e s) -> p (b e) s", e=2)
                sc.activation(sq_b, o_ps, ACT.Square).then_inc(s_osq, 1)
                sc.wait_ge(s_gated, 5 * i + 1)
                for e in range(4):
                    ins = sc.activation(o_sb[:, e, :], o_ps[:, e, :], ACT.Copy,
                                        scale=gains[:, N_GLA + e:N_GLA + e + 1])
                ins.then_inc(s_ocp, 1)
                copy_corr(h, 22, 0)
                copy_corr(h, 23, 1)
                sc.wait_ge(s_r, 2 * i + 2)
                sc.activation(e_sb, r_sb, ACT.Exp, scale=-1.0).then_inc(s_er, 1)

            with sc.Fori(0, PANELS) as p:
                highs(H_OUT + p * PANEL, 2, PANEL + 2)
            sc.wait_ge(s_read, G_MLP0 + 2)
            mlp(H_MLP0, 0, N_MLP0, False)

            sc.wait_ge(s_read, G_DKV + 2)
            first_panel(H_DKV, N_KVIN, xa)
            copy_corr(H_DKV, PANEL - 2, 0)
            copy_corr(H_DKV, PANEL - 1, 1)
            sc.wait_ge(s_side1, 16)
            sc.activation(side1[:, 0, :], side_in1, ACT.Copy).then_inc(s_sidehi, 1)
            first_panel(H_DQ, N_MIX1, xb)
            copy_corr(H_DQ, PANEL - 2, 0)
            copy_corr(H_DQ, PANEL - 1, 1)

            def convert_lat(n, dst):
                sc.wait_ge(s_laty, n)
                for c in range(LT):
                    sc.activation(dst[:, c, 0, :], lat[:, c, :], ACT.Copy).then_inc(s_xhi, 1)

            convert_lat(1, xc)
            sc.wait_ge(s_ang, 2)
            sc.activation(sin, sin, ACT.Sin).then_inc(s_trig, 1)
            sc.activation(cos, cos, ACT.Sin).then_inc(s_trig, 1)
            convert_lat(2, xq)

            def slot(i, proj=True, attn=True):
                h = H_PAIR + i * 4
                if proj:
                    high(h, 2, pairs=i + 1)
                    copy_corr(h, 0, 0)
                    high(h, 3, n=HF // 2, pairs=i + 1)
                if attn:
                    sc.wait_ge(s_nmx, i)
                    for hd in range(2):
                        for blk in range(2):
                            col = 2 * blk + hd
                            a, z = (0, P) if blk == 0 else (P, 3 * P)
                            ins = sc.activation(pr_sb[:, hd, a:z], sc_sb[:, hd, a:z], ACT.Exp,
                                                bias=nmx[:, col:col + 1], scale=MLA_SCALE,
                                                accum_out=den[:, col:col + 1])
                    ins.then_inc(s_exp, 1)
                if proj:
                    copy_corr(h, 1, 1)
                    high(h, 4)
                    copy_corr(h, 2, 0)
                    high(h, 5)
                if attn:
                    sc.wait_ge(s_pt, i)
                    sc.activation(pt_sb, ps[:, 4:6, 0:3 * P], ACT.Copy).then_inc(s_ptc, 1)
                if proj:
                    copy_corr(h, 3, 1, banks=1)
                if attn:
                    sc.wait_ge(s_ov, i)
                    sc.activation(xb[:, bass.ds(2 * i - 2, 2), 0, :],
                                  ps[:, 6, :].rearrange("p (h s) -> p h s", h=2), ACT.Copy)\
                        .then_inc(s_ohi, 1)

            slot(0, attn=False)
            with sc.Fori(1, PAIRS) as i:
                slot(i)
            slot(PAIRS, proj=False)
            pair_loads[0] = PAIRS

            with sc.Fori(0, PANELS) as p:
                highs(H_WO + p * PANEL, 2, PANEL + 2)
            sc.wait_ge(s_read, G_MLP1 + 2)
            mlp(H_MLP1, UP_GROUPS, N_MLP1, True)
            sc.wait_ge(s_read, G_MLP1 + SLABS * SLAB_GROUPS + 2)
            for c in range(KT):
                sc.activation(y_sb[:, c, :], resid[:, c, :], ACT.Copy,
                              scale=gains[:, N_FIN + c:N_FIN + c + 1]).then_inc(s_y, 1)

        @block.tensor
        def _(pe):
            def begin(h, j, g=None):
                pe.wait_ge(s_split, h + j + 1 + RING)
                if g is not None:
                    pe.wait_ge(s_read, g + 1)

            def weights(j, c, part, col):
                return wts[:, j % RING, c, part, col:col + P]

            def products(bank, n, main, rest, first, last):
                corr_at = slice(n // 2, n)
                if last:
                    pe.matmul(bank[:, corr_at], *rest, start=False, stop=False)
                ins = pe.matmul(bank[:, 0:n], *main, start=first, stop=last)
                if not last:
                    ins = pe.matmul(bank[:, corr_at], *rest, start=False, stop=False)
                return ins

            def half_t(j, c2, x, x0, first, last):
                for n in range(2):
                    for c in range(HK4):
                        ins = products(ps[:, 2 * c2 + n], 2 * S,
                                       (weights(j, c, 0, n * P), x[:, x0 + c]),
                                       (weights(j, c, 1, n * P), x[:, x0 + c, 0, :]),
                                       first and c == 0, last and c == HK4 - 1)
                ins.then_inc(s_mult, 1)

            def half_n(j, c2, x, x0, first, last):
                for b in range(TB):
                    tok = slice(b * P, (b + 1) * P)
                    for c in range(HK4):
                        ins = products(ps[:, 2 * c2 + b], 2 * HC,
                                       (x[:, x0 + c, 0, tok], wts[:, j % RING, c]),
                                       (x[:, x0 + c, 1, tok], wts[:, j % RING, c, 0, :]),
                                       first and c == 0, last and c == HK4 - 1)
                ins.then_inc(s_mult, 1)

            def panel(h, g, x, ready=None, half=half_t, after=None):
                for u in range(UNITS):
                    if ready:
                        ready(u)
                    for c2 in range(2):
                        j = 2 * u + c2
                        begin(h, j, g + c2 if u == 0 else None)
                        half(j, c2, x, HK4 * u, u == 0, u == UNITS - 1)
                        if after and j in after:
                            after[j]()

            def stat(st, columns):
                pe.wait_ge(s_sqs, st + 1)
                if st:
                    pe.wait_ge(s_rstd, st)
                ins = pe.matmul(ps[:, 7, 0:S], ones[:, :], sqs[:, :], start=True, stop=True)
                for b in range(TB if columns else 0):
                    ins = pe.matmul(ps[:, 7, S + b:S + b + 1], sqs[:, b * P:(b + 1) * P],
                                    ones[:, 0:1], start=True, stop=True)
                ins.then_inc(s_stat, 1)

            def inputs(x0):
                return lambda u: pe.wait_ge(s_x, x0 + HK4 * (u + 1))

            def hidden(k):
                return lambda u: pe.wait_ge(s_hid, k + 2 * (u + 1) + 2)

            def mlp(h0, g0, k0, x0, st):
                panel(h0, g0, xa, inputs(x0), after={5: lambda: stat(st, False)})
                with pe.Fori(1, PANELS) as p:
                    panel(h0 + p * PANEL, g0 + p * 2, xa)
                with pe.Fori(PANELS, 2 * PANELS) as p:
                    panel(h0 + p * PANEL, g0 + p * 2, xb, hidden(k0))
                with pe.Fori(1, SLABS) as s:
                    h = h0 + s * SLAB_HALVES
                    g = g0 + s * SLAB_GROUPS
                    with pe.Fori(0, PANELS) as p:
                        panel(h + p * PANEL, g + p * 2, xa)
                    with pe.Fori(PANELS, 2 * PANELS) as p:
                        panel(h + p * PANEL, g + p * 2, xb, hidden(k0 + s * (2 * PANELS)))

            pe.sem_inc(s_mult, RING)
            pe.wait_ge(s_ident, 16)
            pe.wait_ge(s_xin, 16 * TB)
            for bank in range(8):
                for n in range(4):
                    c, b = 2 * bank + n // 2, n % 2
                    ins = pe.transpose(ps[:, bank, n * P:(n + 1) * P],
                                       x_nat[:, b, c * P:(c + 1) * P], ident[:, :])
                ins.then_inc(s_tr, 1)
            pe.wait_ge(s_gin, 16 * 7)
            pe.wait_ge(s_trc, 1)
            pe.transpose(ps[:, 0, 0:N_GAINS], gains_in[0:N_GAINS, :], ident[0:N_GAINS, 0:N_GAINS])\
                .then_inc(s_gtr, 1)
            pe.wait_ge(s_ones, 1)
            pe.wait_ge(s_trc, 8)
            pe.wait_ge(s_sidelo, 1)
            pe.wait_ge(s_x, X_GLA + KT)
            for b in range(TB):
                for c in range(KT):
                    cols = slice(c * RANK, (c + 1) * RANK)
                    tok = slice(b * P, (b + 1) * P)
                    ins = products(ps[:, 4 + b], 2 * RANK, (xa[:, c, 0, tok], side0[:, :, cols]),
                                   (xa[:, c, 1, tok], side0[:, 0, cols]), c == 0, c == KT - 1)
            ins.then_inc(s_low, 1)
            stat(ST_MIX0, True)
            pe.wait_ge(s_lownat, 1)
            for b in range(TB):
                ins = pe.transpose(ps[:, 6, b * P:(b + 1) * P], low_nat[:, b, :], ident[:, :])
            ins.then_inc(s_lowt, 1)
            pe.wait_ge(s_lowtc, 1)
            pe.wait_ge(s_mean, ST_MIX0 + 1)
            pe.wait_ge(s_up, 32)
            pe.wait_ge(s_gains, 1)
            for b in range(TB):
                for n in range(2):
                    ins = pe.matmul(ps[:, 4 + 2 * b + n, :], low_t[:, b * P:(b + 1) * P],
                                    w_up[:, n * 512:(n + 1) * 512], start=True, stop=True)
            ins.then_inc(s_z, 1)
            pe.wait_ge(s_sumsr, 1)

            with pe.Fori(0, GH) as i:
                h = H_GLA + i * HEAD_HALVES
                g = G_GLA + i * 6

                def gate_sums(b, d):
                    r = 2 * b + d
                    if r == 0:
                        pe.wait_ge(s_gcur, i + 1)
                        pe.wait_ge(s_orstd, i + 1)
                    pe.wait_ge(s_dec, 4 * i + r + 1)
                    for n in range(2):
                        at = 4 * n + (b if n else 0)
                        for part in range(2):
                            ins = pe.matmul(ps[:, 4 + n, :], gate[:, b, part, d * P:(d + 1) * P],
                                            sums[:, at:at + 4, :], start=part == 0, stop=part == 1)
                    ins.then_inc(s_sum, 1)

                def scores(b):
                    pe.wait_ge(s_qd, 2 * i + b + 1)
                    pe.wait_ge(s_kd, 2 * i + b + 1)
                    if b == 0:
                        pe.wait_ge(s_ocp, i + 1)
                    else:
                        pe.wait_ge(s_att, 2 * i + 1)
                    tok = slice(b * P, (b + 1) * P)
                    for n in range(8):
                        at = PLACES[b][n] if n < 7 else None
                        for d in range(2):
                            lhs = dec[:, d, at, :] if n < 7 else k_sb[:, d, tok]
                            rhs = qdec[:, d, at, :] if n < 7 else q_sb[:, d, tok]
                            ins = pe.matmul(ps[:, 6 + n // 4, (n % 4) * P:(n % 4 + 1) * P], lhs, rhs,
                                            start=d == 0, stop=d == 1)
                    if b == 1:
                        for d in range(2):
                            ins = pe.matmul(ps[:, 4, 0:P], kx[:, d, :], qdec[:, d, PREFIX, :],
                                            start=d == 0, stop=d == 1)
                    ins.then_inc(s_sc, 1)

                def output():
                    pe.wait_ge(s_att, 2 * i + 2)
                    pe.wait_ge(s_v, 2 * i + 2)
                    for e in range(4):
                        bank, col = 6 + e // 2, (e % 2) * S
                        feat = slice(e * P, (e + 1) * P)
                        pe.matmul(ps[:, bank, col:col + P], v_sb[:, 0, feat], att[:, 0:P],
                                  start=True, stop=True)
                        pe.matmul(ps[:, bank, col + P:col + S], v_sb[:, 0, feat], att[:, P:S],
                                  start=True, stop=False)
                        ins = pe.matmul(ps[:, bank, col + P:col + S], v_sb[:, 1, feat],
                                        att[:, S:3 * P], start=False, stop=True)
                    ins.then_inc(s_o, 1)

                panel(h, g, xa, after={3: lambda: gate_sums(0, 0), 5: lambda: gate_sums(0, 1)})
                panel(h + PANEL, g + 2, xa, half=half_n,
                      after={3: lambda: scores(0), 5: lambda: gate_sums(1, 0),
                             7: lambda: gate_sums(1, 1)})
                panel(h + 2 * PANEL, g + 4, xa, after={1: lambda: scores(1), 5: output})
                pe.wait_ge(s_osq, i + 1)
                for e in range(4):
                    ins = pe.matmul(ps[:, 5, 0:S], ones[:, :], sq_b[:, e, :], start=e == 0,
                                    stop=e == 3)
                ins.then_inc(s_ost, 1)

            with pe.Fori(0, PANELS) as p:
                panel(H_OUT + p * PANEL, G_OUT + p * 2, xb,
                      lambda u: pe.wait_ge(s_gated, 5 * (u + 1) + 1))
            mlp(H_MLP0, G_MLP0, 0, X_MLP0, ST_MLP0)

            panel(H_DKV, G_DKV, xa, inputs(X_KV), after={5: lambda: stat(ST_MIX1, True)})
            pe.wait_ge(s_sidelo, 2)
            for b in range(TB):
                for c in range(KT):
                    cols = slice(c * ROPE, (c + 1) * ROPE)
                    tok = slice(b * P, (b + 1) * P)
                    ins = products(ps[:, 4 + b], 2 * ROPE, (xa[:, c, 0, tok], side1[:, :, cols]),
                                   (xa[:, c, 1, tok], side1[:, 0, cols]), c == 0, c == KT - 1)
            ins.then_inc(s_low, 1)
            panel(H_DQ, G_DQ, xb, inputs(X_Q), after={3: lambda: stat(ST_C, False)})

            def keys(i):
                h, g = H_PAIR + i * 4, G_PAIR + i * 4
                begin(h, 0, g)
                half_t(0, 0, xc, 0, True, True)

            def values(i):
                h, g = H_PAIR + i * 4, G_PAIR + i * 4
                begin(h, 1, g + 1)
                half_n(1, 1, xc, 0, True, True)

            def queries(i):
                h, g = H_PAIR + i * 4, G_PAIR + i * 4
                begin(h, 2, g + 2)
                half_t(2, 0, xq, 0, True, True)

            def rotary_queries(i):
                h, g = H_PAIR + i * 4, G_PAIR + i * 4
                begin(h, 3, g + 3)
                for c in range(LT):
                    cols = (c % 2) * P
                    ins = products(ps[:, 2], 2 * S, (weights(3, c // 2, 0, cols), xq[:, c]),
                                   (weights(3, c // 2, 1, cols), xq[:, c, 0, :]),
                                   c == 0, c == LT - 1)
                ins.then_inc(s_mult, 1)

            def rotate(i):
                pe.wait_ge(s_raw, i + 1)
                pe.wait_ge(s_sinr, i)
                pe.matmul(ps[:, 7, 0:S], rot, raw_r, start=True, stop=True).then_inc(s_rot, 1)

            def dots(i, b):
                pe.wait_ge(s_read, G_PAIR + i * 4 + 2)
                pe.wait_ge(s_qr, i)
                pe.wait_ge(s_ptc, i)
                for hd in range(2):
                    for blk in range(2):
                        n = (blk + 1) * P
                        dst = ps[:, 4 + hd, blk * P:blk * P + n]
                        tok = slice(blk * P, (blk + 1) * P)
                        pe.matmul(dst, qn_sb[:, b, hd, tok], kt_sb[:, b, hd, 0:n], start=True,
                                  stop=False)
                        ins = pe.matmul(dst, qr_sb[:, b, tok], keys_r[:, hd, 0:n], start=False,
                                        stop=True)
                ins.then_inc(s_dots, 1)

            def turn(i):
                pe.wait_ge(s_pr, i + 1)
                for hd in range(2):
                    for n in range(3):
                        ins = pe.transpose(ps[:, 4 + hd, n * P:(n + 1) * P],
                                           pr_sb[:, hd, n * P:(n + 1) * P], ident[:, :])
                ins.then_inc(s_pt, 1)

            def weigh(i, b):
                pe.wait_ge(s_ptc, i + 1)
                pe.wait_ge(s_ox, i)
                for hd in range(2):
                    feat = slice(hd * P, (hd + 1) * P)
                    at = hd * S
                    pe.matmul(ps[:, 6, at:at + P], vt_sb[:, b, 0, feat], pt_sb[:, hd, 0:P],
                              start=True, stop=True)
                    pe.matmul(ps[:, 6, at + P:at + S], vt_sb[:, b, 0, feat], pt_sb[:, hd, P:S],
                              start=True, stop=False)
                    ins = pe.matmul(ps[:, 6, at + P:at + S], vt_sb[:, b, 1, feat],
                                    pt_sb[:, hd, S:3 * P], start=False, stop=True)
                ins.then_inc(s_ov, 1)

            pe.wait_ge(s_x, X_C + LT)
            keys(0)
            values(0)
            stat(ST_CQ, False)
            pe.wait_ge(s_krn, 1)
            for b in range(TB):
                ins = pe.transpose(ps[:, 6, b * P:(b + 1) * P], kr_nat[:, b, :], ident[:, :])
            ins.then_inc(s_krt, 1)
            pe.wait_ge(s_krc, 1)
            pe.wait_ge(s_rotm, 16)
            pe.wait_ge(s_rstd, ST_CQ + 1)
            pe.matmul(ps[:, 7, 0:S], rot, raw_r, start=True, stop=True).then_inc(s_krot, 1)
            pe.wait_ge(s_x, X_CQ + LT)
            queries(0)
            rotary_queries(0)
            pe.wait_ge(s_keysr, 2)
            rotate(0)

            def slot(i, b):
                keys(i)
                dots(i, 1 - b)
                values(i)
                queries(i)
                turn(i)
                rotary_queries(i)
                weigh(i, 1 - b)
                rotate(i)

            with pe.Fori(0, PAIRS // 2 - 1) as m:
                slot(m * 2 + 1, 1)
                slot(m * 2 + 2, 0)
            slot(PAIRS - 1, 1)
            dots(PAIRS, 1)
            turn(PAIRS)
            weigh(PAIRS, 1)

            with pe.Fori(0, PANELS) as p:
                panel(H_WO + p * PANEL, G_WO + p * 2, xb,
                      lambda u: pe.wait_ge(s_ox, 2 * (u + 1) + 1))
            mlp(H_MLP1, G_MLP1, UP_GROUPS, X_MLP1, ST_MLP1)

            for n in range(8):
                b, c0 = n // 4, (n % 4) * 4
                pe.wait_ge(s_y, KT if n else KT)
                if n == 7:
                    stat(ST_FIN, True)
                    pe.wait_ge(s_rstd, ST_FIN + 1)
                for c in range(4):
                    ins = pe.transpose(ps[:, n, c * P:(c + 1) * P],
                                       y_sb[:, c0 + c, b * P:(b + 1) * P], ident[:, :])
                ins.then_inc(s_fin, 1)

        @block.vector
        def _(dve):
            steps = [0]

            def step(ins):
                steps[0] += 1
                ins.then_inc(s_dve, 1)
                dve.wait_ge(s_dve, steps[0])

            def low(h, j, n=HF):
                slot = j % RING
                dve.wait_ge(s_high, h + j + 1)
                src = stage[:, slot, 0:n].rearrange("p (t n) -> p t n", n=HC)
                dve.tensor_tensor(wts[:, slot, 0:n // HC, 1, :], src,
                                  wts[:, slot, 0:n // HC, 0, :].bitcast(F32), ALU.subtract)\
                    .then_inc(s_split, 1)

            def lows(h, j0, j1):
                for j in range(j0, j1):
                    low(h, j)

            def convert(src, gain, dst, x0, c0, c1):
                for c in range(c0, c1):
                    dve.wait_ge(s_xhi, x0 + c + 1)
                    dve.scalar_tensor_tensor(out=dst[:, c, 1, :], in0=src[:, c, :],
                                             scalar=gains[:, gain + c:gain + c + 1],
                                             in1=dst[:, c, 0, :].bitcast(F32),
                                             op0=ALU.mult, op1=ALU.subtract).then_inc(s_x, 1)

            def factors(st, features, columns=False, dst=None):
                dve.wait_ge(s_stat, st + 1)
                n = S + TB if columns else S
                to = rstd[:, 0:n] if dst is None else dst
                dve.tensor_scalar(to, ps[:, 7, 0:n], 1.0 / features, EPS, ALU.mult, ALU.add)\
                    .then_inc(s_mean, 1)
                dve.wait_ge(s_rstd, st + 1)

            def first_panel(h, gain, dst, x0, after=None):
                for u in range(UNITS):
                    convert(resid, gain, dst, x0, HK4 * u, HK4 * u + HK4)
                    low(h, 2 * u + 2)
                    low(h, 2 * u + 3)
                    if after and u in after:
                        after[u]()

            def sum_group(g, n, c, dst=None, banks=2):
                dve.wait_ge(s_corr, n + 1)
                to = total[:, c, 0:banks, :] if dst is None else dst
                dve.tensor_tensor(to, ps[:, 2 * c:2 * c + banks, 0:S], corr[:, c, 0:banks, :],
                                  ALU.add).then_inc(s_read, 1)

            def per_token(banks, factor=None):
                f = rstd[:, 0:S] if factor is None else factor
                return f.rearrange("p (o s) -> p o s", o=1).broadcast_to([P, banks, S])

            def up(g, p, k, cc):
                for c in range(2):
                    dve.wait_ge(s_hid, k + c + 1)
                    sum_group(g + c, cc + c, c)
                    dve.wait_ge(s_read, g + c + 3)
                    dve.scalar_tensor_tensor(out=act[:, c], in0=total[:, c], scalar=0.0,
                                             in1=per_token(2), op0=ALU.max, op1=ALU.mult)\
                        .then_inc(s_act, 1)

            def down(h, p, r):
                for c in range(2):
                    dve.wait_ge(s_mult, h + PANEL - 2 + c + 1 + RING)
                    to = resid[:, bass.ds(p * 4 + 2 * c, 2), :]
                    banks = ps[:, 2 * c:2 * c + 2]
                    dve.tensor_tensor(to, banks[:, :, 0:S], to, ALU.add).then_inc(s_main, 1)
                    dve.wait_ge(s_main, r + c + 1)
                    dve.tensor_tensor(to, banks[:, :, S:2 * S], to, ALU.add).then_inc(s_read, 1)

            def down_panels(h0, r0):
                with dve.Fori(0, PANELS) as p:
                    lows(h0 + p * PANEL, 2, PANEL + 2)
                    down(h0 + p * PANEL, p, r0 + p * 2)

            def mlp(h0, g0, k0, c0, r0, x0, gain, st, last):
                first_panel(h0, gain, xa, x0)
                factors(st, D)
                up(g0, 0, k0, c0)
                with dve.Fori(1, PANELS) as p:
                    lows(h0 + p * PANEL, 2, PANEL + 2)
                    up(g0 + p * 2, p, k0 + p * 2, c0 + p * 2)
                down_panels(h0 + PANELS * PANEL, r0)
                with dve.Fori(1, SLABS - 1 if last else SLABS) as s:
                    h, g = h0 + s * SLAB_HALVES, g0 + s * SLAB_GROUPS
                    n = s * (2 * PANELS)
                    with dve.Fori(0, PANELS) as p:
                        lows(h + p * PANEL, 2, PANEL + 2)
                        up(g + p * 2, p, k0 + n + p * 2, c0 + n + p * 2)
                    down_panels(h + PANELS * PANEL, r0 + n)
                if last:
                    h, g = h0 + (SLABS - 1) * SLAB_HALVES, g0 + (SLABS - 1) * SLAB_GROUPS
                    n = (SLABS - 1) * 2 * PANELS
                    with dve.Fori(0, PANELS) as p:
                        lows(h + p * PANEL, 2, PANEL + 2)
                        up(g + p * 2, p, k0 + n + p * 2, c0 + n + p * 2)
                    h += PANELS * PANEL
                    with dve.Fori(0, PANELS - 1) as p:
                        lows(h + p * PANEL, 2, PANEL + 2)
                        down(h + p * PANEL, p, r0 + n + p * 2)
                    h += (PANELS - 1) * PANEL
                    lows(h, 2, PANEL)
                    down(h, PANELS - 1, r0 + n + 2 * (PANELS - 1))

            dve.sem_inc(s_split, RING)
            dve.sem_inc(s_read, 2)
            dve.sem_inc(s_ox, 1)
            for bank in range(8):
                dve.wait_ge(s_tr, bank + 1)
                dve.tensor_copy(resid[:, 2 * bank:2 * bank + 2, :],
                                ps[:, bank, :].rearrange("p (c s) -> p c s", c=2))\
                    .then_inc(s_trc, 1)
            dve.wait_ge(s_gtr, 1)
            dve.tensor_copy(gains[:, :], ps[:, 0, 0:N_GAINS]).then_inc(s_gains, 1)
            dve.wait_ge(s_gains, 1)
            convert(resid, N_MIX0, xa, X_GLA, 0, KT)
            dve.wait_ge(s_sidehi, 1)
            dve.tensor_tensor(side0[:, 1, :], side_in0, side0[:, 0, :].bitcast(F32), ALU.subtract)\
                .then_inc(s_sidelo, 1)
            lows(H_GLA, 0, 2)
            dve.wait_ge(s_low, 1)
            lt = low_tmp[:, 0:TB * RANK].rearrange("p (b c) -> p b c", b=TB)
            step(dve.tensor_copy(lt, ps[:, 4:6, RANK:2 * RANK]))
            step(dve.tensor_tensor(lt, ps[:, 4:6, 0:RANK], lt, ALU.add))
            factors(ST_MIX0, D, columns=True)
            dve.wait_ge(s_pad, 1)
            for b in range(TB):
                ins = dve.tensor_scalar(low_nat[:, b, 0:RANK], lt[:, b, :],
                                        rstd[:, S + b:S + b + 1], None, ALU.mult)
            ins.then_inc(s_lownat, 1)
            dve.wait_ge(s_lowt, 1)
            dve.tensor_copy(low_t, ps[:, 6, 0:S]).then_inc(s_lowtc, 1)
            dve.wait_ge(s_zact, 3)
            z_ps = ps[:, 4:8, :].rearrange("p b n -> p (b n)")
            dve.scalar_tensor_tensor(out=g_sb, in0=z_ps, scalar=0.0, in1=z_sb, op0=ALU.min,
                                     op1=ALU.subtract).then_inc(s_g, 1)
            g_by_head = g_sb.rearrange("p (b h n) -> p h b n", b=TB, h=GH)
            for i in range(GH):
                dve.wait_ge(s_ghi, i + 1)
                part = xb[:, 4 * i:4 * i + 2]
                dve.tensor_tensor(part[:, :, 1, :], g_by_head[:, i], part[:, :, 0, :].bitcast(F32),
                                  ALU.subtract).then_inc(s_glo, 1)
            dve.wait_ge(s_glo, GH)
            dve.wait_ge(s_masks, 16)

            with dve.Fori(0, GH) as i:
                h = H_GLA + i * HEAD_HALVES
                g = G_GLA + i * 6
                cc = C_GLA + i * 6

                def scaled_queries(b):
                    for d in range(2):
                        dve.wait_ge(s_dec, 4 * i + 2 * b + d + 2)
                        q = q_sb[:, d:d + 1, b * P:(b + 1) * P].broadcast_to([P, 8, P])
                        ins = dve.tensor_tensor(qdec[:, d], dec[:, d], q, ALU.mult)
                    ins.then_inc(s_qd, 1)

                def masked(b, dst):
                    dve.wait_ge(s_sc, 2 * i + b + 1)
                    tmp = sq_a.rearrange("p a (l n) -> p (a l) n", l=2)
                    dve.tensor_tensor(tmp, ps[:, 6:8, :].rearrange("p a (l n) -> p (a l) n", l=4),
                                      masks, ALU.mult).then_inc(s_msk, 1)
                    dve.wait_ge(s_msk, 2 * i + b + 1)
                    return dve.tensor_reduce(dst, tmp.rearrange("p l n -> p n l"), AX.X, ALU.add)

                lows(h, 2, 10)
                for c, (to, scale, done) in enumerate(((q_sb, float(HK) ** -0.5, s_q),
                                                       (k_sb, 1.0, s_k))):
                    sum_group(g + c, cc + c, c)
                    dve.wait_ge(s_read, g + c + 3)
                    dve.scalar_tensor_tensor(out=to, in0=total[:, c], scalar=scale,
                                             in1=per_token(2), op0=ALU.mult, op1=ALU.mult)\
                        .then_inc(done, 1)
                dve.wait_ge(s_q, i + 1)
                scaled_queries(0)
                lows(h, 10, 16)
                masked(0, att[:, 0:P]).then_inc(s_att, 1)
                lows(h, 16, 18)
                for c in range(2):
                    sum_group(g + 2 + c, cc + 2 + c, c)
                    dve.wait_ge(s_read, g + 2 + c + 3)
                    for b in range(TB):
                        ins = dve.tensor_scalar(v_sb[:, b, c * HC:(c + 1) * HC], total[:, c, b, :],
                                                rstd[:, S + b:S + b + 1], None, ALU.mult)
                    ins.then_inc(s_v, 1)
                scaled_queries(1)
                lows(h, 18, 22)
                masked(1, att[:, S:3 * P])
                dve.tensor_copy(att[:, P:S], ps[:, 4, 0:P]).then_inc(s_att, 1)
                lows(h, 22, 26)
                dve.wait_ge(s_gated, 5 * i + 1)
                for c in range(2):
                    sum_group(g + 4 + c, cc + 4 + c, c)
                    dve.wait_ge(s_read, g + 4 + c + 3)
                    dve.tensor_tensor(r_sb[:, 2 * c:2 * c + 2, :], total[:, c], per_token(2),
                                      ALU.mult).then_inc(s_r, 1)
                dve.wait_ge(s_ost, i + 1)
                dve.tensor_scalar(rstd_o, ps[:, 5, 0:S], 1.0 / HV, EPS, ALU.mult, ALU.add)\
                    .then_inc(s_ostd, 1)
                dve.wait_ge(s_er, i + 1)
                dve.tensor_scalar(e_sb, e_sb, 1.0, None, ALU.add).then_inc(s_eone, 1)
                dve.wait_ge(s_eone, i + 1)
                dve.reciprocal(e_sb, e_sb).then_inc(s_erec, 1)

            down_panels(H_OUT, R_OUT)
            mlp(H_MLP0, G_MLP0, 0, C_MLP0, R_MLP0, X_MLP0, N_MLP0, ST_MLP0, False)

            first_panel(H_DKV, N_KVIN, xa, X_KV)
            factors(ST_MIX1, D, columns=True)

            def latent(g, cc, n):
                for c in range(2):
                    sum_group(g + c, cc + c, c)
                    dve.wait_ge(s_read, g + c + 3)
                    dve.tensor_tensor(lat[:, 2 * c:2 * c + 2, :], total[:, c], per_token(2),
                                      ALU.mult).then_inc(s_lat, 1)
                    dve.wait_ge(s_lat, n + c + 1)

            def normed(st, gain, dst, x0, n):
                factors(st, LORA, dst=rstd_c)
                for c in range(LT):
                    ins = dve.scalar_tensor_tensor(out=lat[:, c, :], in0=lat[:, c, :],
                                                   scalar=gains[:, gain + c:gain + c + 1],
                                                   in1=rstd_c, op0=ALU.mult, op1=ALU.mult)
                ins.then_inc(s_laty, 1)
                dve.wait_ge(s_laty, n)
                for c in range(LT):
                    dve.wait_ge(s_xhi, x0 + c + 1)
                    dve.tensor_tensor(dst[:, c, 1, :], lat[:, c, :], dst[:, c, 0, :].bitcast(F32),
                                      ALU.subtract).then_inc(s_x, 1)

            latent(G_DKV, C_DKV, 0)
            dve.wait_ge(s_sidehi, 2)
            dve.tensor_tensor(side1[:, 1, :], side_in1, side1[:, 0, :].bitcast(F32), ALU.subtract)\
                .then_inc(s_sidelo, 1)
            first_panel(H_DQ, N_MIX1, xb, X_Q)
            dve.wait_ge(s_low, 2)
            step(dve.tensor_copy(kr_tmp, ps[:, 4:6, ROPE:2 * ROPE]))
            step(dve.tensor_tensor(kr_tmp, ps[:, 4:6, 0:ROPE], kr_tmp, ALU.add))
            for b in range(TB):
                for n in range(2):
                    ins = dve.tensor_scalar(kr_nat[:, b, n * ROPE:(n + 1) * ROPE], kr_tmp[:, b, :],
                                            rstd[:, S + b:S + b + 1], None, ALU.mult)
            ins.then_inc(s_krn, 1)
            normed(ST_C, N_C, xc, X_C, 1)
            dve.wait_ge(s_x, X_C + LT)
            latent(G_DQ, C_DQ, 2)
            dve.wait_ge(s_freqs, 16)
            dve.wait_ge(s_pos, 16)
            step(dve.tensor_copy(ang, pos_i))
            step(dve.tensor_scalar(ang, ang, freqs[:, 0:1], None, ALU.mult))
            step(dve.tensor_scalar(turns, ang, 1.0 / (2.0 * np.pi), ROUND, ALU.mult, ALU.add))
            step(dve.tensor_scalar(turns, turns, ROUND, None, ALU.subtract))
            for part in TWO_PI:
                step(dve.scalar_tensor_tensor(out=ang, in0=turns, scalar=-part, in1=ang,
                                              op0=ALU.mult, op1=ALU.add))
            step(dve.tensor_scalar(sin, ang, float(np.float32(np.pi)), -float(np.float32(np.pi)),
                                   ALU.min, ALU.max))
            step(dve.scalar_tensor_tensor(out=cos, in0=sin, scalar=-1.0, in1=sin, op0=ALU.mult,
                                          op1=ALU.max))
            dve.tensor_scalar(cos, cos, -1.0, float(np.pi / 2), ALU.mult, ALU.add)\
                .then_inc(s_ang, 2)
            normed(ST_CQ, N_CQ, xq, X_CQ, 2)
            dve.wait_ge(s_krt, 1)
            dve.tensor_copy(raw_r, ps[:, 6, 0:S]).then_inc(s_krc, 1)
            dve.wait_ge(s_trig, 2)
            dve.wait_ge(s_krc, 1)
            step(dve.tensor_tensor(cos_r, raw_r, cos, ALU.mult))
            dve.wait_ge(s_krot, 1)
            step(dve.tensor_tensor(sin_r, ps[:, 7, 0:S], sin, ALU.mult))
            dve.wait_ge(s_krz, 1)
            for n in range(2):
                rows = slice(n * ROPE, (n + 1) * ROPE)
                dve.tensor_tensor(keys_r[rows, n, :], cos_r[rows, :], sin_r[rows, :], ALU.add)\
                    .then_inc(s_keysr, 1)
            dve.wait_ge(s_keysr, 2)
            dve.wait_ge(s_causal, 16)

            def slot(i, b, proj=True, attn=True):
                h, g, cc = H_PAIR + i * 4, G_PAIR + i * 4, C_PAIR + i * 4
                if proj:
                    low(h, 2)
                    sum_group(g, cc, 0, dst=kt_sb[:, b])
                if attn:
                    dve.wait_ge(s_dots, i)
                    mask = causal.rearrange("p (o n) -> p o n", o=1).broadcast_to([P, 2, 3 * P])
                    dve.tensor_tensor(sc_sb, ps[:, 4:6, 0:3 * P], mask, ALU.add).then_inc(s_ms, 1)
                    dve.wait_ge(s_ms, i)
                    dve.tensor_reduce(mx[:, 0:2], sc_sb[:, :, 0:P], AX.X, ALU.max)
                    dve.tensor_reduce(mx[:, 2:4], sc_sb[:, :, P:3 * P], AX.X, ALU.max)\
                        .then_inc(s_max, 1)
                    dve.wait_ge(s_max, i)
                    dve.tensor_scalar(nmx, mx, -MLA_SCALE, None, ALU.mult).then_inc(s_nmx, 1)
                if proj:
                    low(h, 3, n=HF // 2)
                    sum_group(g + 1, cc + 1, 1, dst=vt_sb[:, b])
                    low(h, 4)
                if attn:
                    dve.wait_ge(s_exp, i)
                    dve.wait_ge(s_pr, i)
                    dve.reciprocal(rden, den).then_inc(s_rden, 1)
                if proj:
                    sum_group(g + 2, cc + 2, 0, dst=qn_sb[:, b])
                    low(h, 5)
                    dve.wait_ge(s_qr, i)
                    sum_group(g + 3, cc + 3, 1, dst=raw_r.rearrange("p (o s) -> p o s", o=1),
                              banks=1)
                    dve.wait_ge(s_read, g + 3 + 3)
                    dve.sem_inc(s_raw, 1)
                if attn:
                    dve.wait_ge(s_ohi, i)
                    pair = xb[:, bass.ds(2 * i - 2, 2)]
                    dve.tensor_tensor(pair[:, :, 1, :],
                                      ps[:, 6, :].rearrange("p (h s) -> p h s", h=2),
                                      pair[:, :, 0, :].bitcast(F32), ALU.subtract).then_inc(s_ox, 1)
                if proj:
                    dve.wait_ge(s_rot, i + 1)
                    dve.tensor_tensor(sin_r, ps[:, 7, 0:S], sin, ALU.mult).then_inc(s_sinr, 1)

            slot(0, 0, attn=False)
            with dve.Fori(0, PAIRS // 2 - 1) as m:
                slot(m * 2 + 1, 1)
                slot(m * 2 + 2, 0)
            slot(PAIRS - 1, 1)
            slot(PAIRS, 0, proj=False)

            down_panels(H_WO, R_WO)
            mlp(H_MLP1, G_MLP1, UP_GROUPS, C_MLP1, R_MLP1, X_MLP1, N_MLP1, ST_MLP1, True)
            factors(ST_FIN, D, columns=True)
            for n in range(8):
                b, c = n // 4, n % 4
                dve.wait_ge(s_fin, n + 1)
                dve.tensor_scalar(o_nat[:, b, c * 512:(c + 1) * 512], ps[:, n, :],
                                  rstd[:, S + b:S + b + 1], None, ALU.mult).then_inc(s_finc, 1)


_INS = ["x", "positions", "norm_mix", "norm_mlp", "gla_w_in", "gla_w_gate_up", "gla_b_gate",
        "gla_norm", "gla_w_out", "kv_norm_in", "mla_w_dkv", "mla_kv_norm", "mla_w_uk", "mla_w_uv",
        "mla_w_dq", "mla_q_norm", "mla_w_uq", "mla_w_o", "mlp_w1", "mlp_w2", "final_norm"]


def kernel(**inputs):
    import concourse.bacc as bacc
    from concourse.bass_utils import run_bass_kernel_spmd

    nc = bacc.Bacc("TRN2", target_bir_lowering=False, num_devices=1)
    arrays, tensors = {}, {}
    given = {name: inputs[name] for name in _INS}
    for name, a in (*given.items(), *constants().items()):
        a = np.ascontiguousarray(a)
        arrays[f"in_{name}"] = a
        tensors[name] = nc.dram_tensor(f"in_{name}", a.shape, mybir.dt.from_np(a.dtype),
                                       kind="ExternalInput").ap()
    out = nc.dram_tensor("out", (1, S, D), F32, kind="ExternalOutput").ap()
    build(nc, tensors, out)
    return run_bass_kernel_spmd(nc, [arrays], core_ids=[0]).results[0]["out"]
```

```python
from contextlib import ExitStack

import numpy as np

import concourse.bass as bass
from concourse import mybir

F32 = mybir.dt.float32
F32R = mybir.dt.float32r
I32 = mybir.dt.int32
ALU = mybir.AluOpType
ACT = mybir.ActivationFunctionType
AX = mybir.AxisListType

P = 128
S = 256
TB = S // P
D = 2048
KT = D // P
EPS = 1e-6

GH = 4
GK = D // 2
HK = GK // GH
HV = D // GH
RANK = 16
TAU = 16.0
LEVELS = [64, 32, 16, 8, 4, 2, 1]

MH = 16
LORA = 512
LT = LORA // P
NOPE = 128
ROPE = 64
QH = NOPE + ROPE
PAIRS = MH // 2
THETA = 10000.0
MLA_SCALE = float(QH) ** -0.5
MASKED = -1e30

D_FF = 4 * D
SLAB = 2048
SLABS = D_FF // SLAB

ROUND = 1.5 * 2.0 ** 23
TWO_PI = [6.28125, 0.0019350051879882812, 2.0 * np.pi - 6.28125 - 0.0019350051879882812]

HC = 256
HK4 = 4
HF = HK4 * HC
RING = 4
UNITS = KT // HK4
PANEL = 2 * UNITS
PANELS = D // (2 * HC)
HEAD_HALVES = 3 * PANEL
H_GLA, G_GLA = 0, 0
H_OUT, G_OUT = H_GLA + GH * HEAD_HALVES, G_GLA + GH * 6
H_MLP0, G_MLP0 = H_OUT + PANELS * PANEL, G_OUT + PANELS * 2
SLAB_HALVES, SLAB_GROUPS = 2 * PANELS * PANEL, 4 * PANELS
H_DKV, G_DKV = H_MLP0 + SLABS * SLAB_HALVES, G_MLP0 + SLABS * SLAB_GROUPS
H_DQ, G_DQ = H_DKV + PANEL, G_DKV + 2
H_PAIR, G_PAIR = H_DQ + PANEL, G_DQ + 2
H_WO, G_WO = H_PAIR + PAIRS * 4, G_PAIR + PAIRS * 4
H_MLP1, G_MLP1 = H_WO + PANELS * PANEL, G_WO + PANELS * 2
H_END, G_END = H_MLP1 + SLABS * SLAB_HALVES, G_MLP1 + SLABS * SLAB_GROUPS
C_GLA = 0
C_MLP0 = C_GLA + GH * 6
UP_GROUPS = SLABS * PANELS * 2
C_DKV = C_MLP0 + UP_GROUPS
C_DQ = C_DKV + 2
C_PAIR = C_DQ + 2
C_MLP1 = C_PAIR + PAIRS * 4
X_GLA, X_MLP0, X_KV, X_Q, X_C, X_CQ, X_MLP1 = 0, 16, 32, 48, 64, 68, 72
N_MIX0, N_MIX1, N_MLP0, N_MLP1, N_KVIN, N_FIN, N_GLA, N_C, N_CQ = 0, 16, 32, 48, 64, 80, 96, 100, 104
N_GAINS = 108
R_OUT, R_MLP0 = 0, 2 * PANELS
R_WO = R_MLP0 + SLABS * PANELS * 2
R_MLP1 = R_WO + 2 * PANELS
(ST_MIX0, ST_MLP0, ST_MIX1, ST_C, ST_CQ, ST_MLP1, ST_FIN) = range(7)
PLACES = [[0, 1, 2, 3, 5, 6, 7], [0, 1, 2, 3, 4, 5, 6]]
SUFFIX, PREFIX = 4, 7


def constants():
    s, t = np.arange(P)[:, None], np.arange(P)[None, :]
    sums = {}
    masks = []
    for m in LEVELS:
        mid = (t // (2 * m)) * 2 * m + m
        upper = (t % (2 * m)) >= m
        sums[m] = np.where(upper, (s >= mid) & (s <= t), (s > t) & (s < mid))
        same = (s // (2 * m)) == (t // (2 * m))
        masks.append(same & ((t % (2 * m)) >= m) & ((s % (2 * m)) < m))
    masks.append(s == t)
    suffix, prefix = s > t, s <= t
    order = [sums[m] for m in LEVELS[:4]] + [suffix] + [sums[m] for m in LEVELS[4:]] + [prefix]
    rot = np.zeros((P, P))
    half = ROPE // 2
    for b in range(0, P, ROPE):
        for d in range(half):
            rot[b + d + half, b + d] = -1.0
            rot[b + d, b + d + half] = 1.0
    causal = np.zeros((P, 3 * P))
    later = np.where(t > s, MASKED, 0.0)
    causal[:, 0:P] = later
    causal[:, 2 * P:] = later
    freqs = (THETA ** (-np.arange(0, ROPE, 2, dtype=np.float64) / ROPE)).astype(np.float32)
    pad = np.zeros((P, P))
    pad[:, RANK] = 1.0
    return {
        "c_sums": np.stack(order, 1).reshape(P, 9 * P).astype(np.float32),
        "c_masks": np.stack(masks, 1).reshape(P, 8 * P).astype(np.float32),
        "c_ident": np.eye(P, dtype=np.float32),
        "c_rot": rot.astype(np.float32),
        "c_causal": causal.astype(np.float32),
        "c_freqs": np.tile(freqs, P // half)[:, None].copy(),
        "c_bias_row": pad.astype(np.float32),
    }


def build(nc, t, out):
    ctx = ExitStack()
    with ctx:
        def sb(name, shape, dt=F32):
            return ctx.enter_context(nc.sbuf_tensor(name, shape, dt))

        def sem(name):
            return ctx.enter_context(nc.semaphore(name))

        resid = sb("resid", [P, KT, S])
        xa = sb("xa", [P, KT, 2, S], F32R)
        xb = sb("xb", [P, KT, 2, S], F32R)
        stage = sb("stage", [P, RING, HF])
        wts = sb("wts", [P, RING, HK4, 2, HC], F32R)
        temps = sb("temps", [P, 16 * S])
        sqs = sb("sqs", [P, S + TB])
        rstd = sb("rstd", [P, S + TB])
        ident = sb("ident", [P, P])
        ones = sb("ones", [P, P])
        gains = sb("gains", [P, N_GAINS])
        eps = sb("eps", [P, 2])
        scratch = sb("scratch", [P, 11136])
        scratch_r = sb("scratch_r", [P, 4096], F32R)

        def carve(tensor, at=0):
            end = [at]

            def take(*dims):
                n = int(np.prod(dims))
                v = tensor[:, end[0]:end[0] + n]
                end[0] += n
                assert end[0] <= tensor.shape[1]
                if len(dims) == 1:
                    return v
                names = "abcd"[:len(dims)]
                return v.rearrange(f"p ({' '.join(names)}) -> p {' '.join(names)}",
                                   **dict(zip(names, dims)))

            return take

        root = sqs
        take = carve(temps)
        corr, total = take(2, 2, S), take(2, 2, S)
        sq_a, sq_b = take(4, S), take(4, S)
        x_nat = temps[:, :].rearrange("p (b d) -> p b d", b=TB)

        take = carve(scratch)
        dec = take(2, 8, P)
        qdec = take(2, 8, P)
        q_sb, k_sb = take(2, S), take(2, S)
        v_sb = take(TB, HV)
        r_sb, e_sb, o_sb = take(4, S), take(4, S), take(4, S)
        masks = take(8, P)
        kx = take(2, P)
        att = take(3 * P)
        rstd_o, root_o = take(S), root[:, 0:S]
        w_up = scratch[:, 0:GK]
        z_sb = scratch[:, 2048:2048 + TB * GK]
        g_sb = scratch[:, 0:TB * GK]
        sums_in = scratch[:, 4096:4096 + 9 * P]
        low_nat = r_sb[:, 0, :].rearrange("p (b c) -> p b c", b=TB)
        low_t = r_sb[:, 1, :]
        side_in0 = r_sb[:, 2, :]
        low_tmp = r_sb[:, 3, :]
        gains_in = e_sb[:, 0, 0:P]
        take = carve(scratch_r)
        gate = take(TB, 2, HK)
        sums = take(9, P)
        side0 = take(2, KT * RANK)

        take = carve(scratch)
        kt_sb, vt_sb = take(2, 2, S), take(2, TB, S)
        cos, sin = take(S), take(S)
        causal = take(3 * P)
        rot = take(P)
        lat = take(LT, S)
        keys_r = take(2, S)
        qn_sb = take(2, 2, S)
        qr_sb = take(2, S)
        raw_r, cos_r, sin_r = take(S), take(S), take(S)
        sc_sb, pr_sb, pt_sb = take(2, 3 * P), take(2, 3 * P), take(2, 3 * P)
        mx, nmx, den, rden = take(4), take(4), take(4), take(4)
        freqs = take(2)
        rstd_c = take(S)
        side_in1 = take(KT * ROPE)
        kr_nat = sc_sb[:, 0, 0:TB * P].rearrange("p (b c) -> p b c", b=TB)
        kr_tmp = pr_sb[:, 0, 0:TB * ROPE].rearrange("p (b c) -> p b c", b=TB)
        ang, turns, pos_i = pt_sb[:, 0, 0:S], pt_sb[:, 1, 0:S], cos.bitcast(I32)
        take = carve(scratch_r)
        xc, xq = take(LT, 2, S), take(LT, 2, S)
        side1 = scratch_r[:, 2048:4096].rearrange("p (h n) -> p h n", h=2)

        take = carve(scratch)
        act, sq_h = take(2, 2, S), take(2, 2, S)
        o_nat = take(TB, D)
        y_sb = scratch[:, 6144:6144 + KT * S].rearrange("p (t s) -> p t s", t=KT)

        ps = ctx.enter_context(nc.psum_tensor("ps", [P, 8, 512], F32))

        s_ident, s_xin = sem("s_ident"), [sem(f"s_xin{i}") for i in range(4)]
        s_gin, s_side0, s_up, s_masks, s_sums = (
            sem(n) for n in ("s_gin", "s_side0", "s_up", "s_masks", "s_sums"))
        s_side1, s_causal, s_rotm, s_freqs, s_pos = (
            sem(n) for n in ("s_side1", "s_causal", "s_rotm", "s_freqs", "s_pos"))
        s_landed = [sem(f"s_landed{i}") for i in range(RING)]
        s_high = sem("s_high")
        s_split = sem("s_split")
        s_mult = sem("s_mult")
        s_read = sem("s_read")
        s_corr = sem("s_corr")
        s_main = sem("s_main")
        s_xhi, s_x = sem("s_xhi"), sem("s_x")
        s_sqs = sem("s_sqs")
        s_stat = sem("s_stat")
        s_root = sem("s_root")
        s_rstd = sem("s_rstd")
        s_act, s_acthi, s_acts = sem("s_act"), sem("s_acthi"), sem("s_acts")
        s_hid = sem("s_hid")
        s_dve, s_pool = sem("s_dve"), sem("s_pool")
        s_ones, s_eps, s_pad, s_tr, s_trc, s_gtr, s_gains = (
            sem(n) for n in ("s_ones", "s_eps", "s_pad", "s_tr", "s_trc", "s_gtr", "s_gains"))
        s_sidehi, s_sidelo, s_low, s_lownat, s_lowt, s_lowtc = (
            sem(n) for n in ("s_sidehi", "s_sidelo", "s_low", "s_lownat", "s_lowt", "s_lowtc"))
        s_z, s_zact, s_g, s_ghi, s_glo, s_sumsr = (
            sem(n) for n in ("s_z", "s_zact", "s_g", "s_ghi", "s_glo", "s_sumsr"))
        s_y, s_ysq, s_fin, s_finc, s_out = (
            sem(n) for n in ("s_y", "s_ysq", "s_fin", "s_finc", "s_out"))
        s_gcur = sem("s_gcur")
        s_sum = sem("s_sum")
        s_dec = sem("s_dec")
        s_q, s_k, s_r = sem("s_q"), sem("s_k"), sem("s_r")
        s_v = sem("s_v")
        s_qd, s_kd = sem("s_qd"), sem("s_kd")
        s_kx = sem("s_kx")
        s_sc = sem("s_sc")
        s_msk = sem("s_msk")
        s_att = sem("s_att")
        s_o, s_osq, s_ocp, s_ost, s_oroot, s_orstd = (
            sem(n) for n in ("s_o", "s_osq", "s_ocp", "s_ost", "s_oroot", "s_orstd"))
        s_tanh, s_silu, s_scaled, s_full, s_fullhi = (
            sem(n) for n in ("s_tanh", "s_silu", "s_scaled", "s_full", "s_fullhi"))
        s_gated = sem("s_gated")
        s_lat, s_laty, s_krn, s_krt, s_krc, s_krot, s_krz = (
            sem(n) for n in ("s_lat", "s_laty", "s_krn", "s_krt", "s_krc", "s_krot", "s_krz"))
        s_ang, s_trig, s_keysr = sem("s_ang"), sem("s_trig"), sem("s_keysr")
        s_raw, s_rot, s_cosr, s_sinr, s_qr = (
            sem(n) for n in ("s_raw", "s_rot", "s_cosr", "s_sinr", "s_qr"))
        s_dots, s_ms, s_max, s_nmx, s_exp, s_rden, s_pr = (
            sem(n) for n in ("s_dots", "s_ms", "s_max", "s_nmx", "s_exp", "s_rden", "s_pr"))
        s_pt, s_ptc, s_ov, s_ohi, s_ox = (
            sem(n) for n in ("s_pt", "s_ptc", "s_ov", "s_ohi", "s_ox"))

        def by_chunk(w):
            return w.rearrange("(t p) n -> p t n", p=P)

        w_in, w_out = by_chunk(t["gla_w_in"][0]), by_chunk(t["gla_w_out"][0])
        w1 = [by_chunk(t["mlp_w1"][i]) for i in range(2)]
        w2 = [by_chunk(t["mlp_w2"][i]) for i in range(2)]
        w_dkv, w_dq = by_chunk(t["mla_w_dkv"]), by_chunk(t["mla_w_dq"][0])
        w_uk, w_uv, w_o = by_chunk(t["mla_w_uk"]), by_chunk(t["mla_w_uv"]), by_chunk(t["mla_w_o"][0])
        w_uq = t["mla_w_uq"][0].rearrange("(t p) (h c) -> p t h c", p=P, c=QH)
        x_dram = t["x"][0].rearrange("(b p) d -> p b d", p=P)
        out_dram = out[0].rearrange("(b p) d -> p b d", p=P)

        block = ctx.enter_context(nc.Block())

        @block.sync
        def _(sp):
            def load(h, j, src, n=HF):
                slot = j % RING
                sp.wait_ge(s_split, h + j + 1)
                dst = stage[:, slot, 0:n]
                if len(src.shape) == 3:
                    dst = dst.rearrange("p (t n) -> p t n", t=src.shape[1])
                    sp.dma_start(dst, src).then_inc(s_landed[slot], 16)
                else:
                    dst = dst.rearrange("p (t h n) -> p t h n", t=src.shape[1], h=src.shape[2])
                    for hd in range(2):
                        sp.dma_start(dst[:, :, hd], src[:, :, hd]).then_inc(s_landed[slot], 16)

            def panel(h, w, row, col0, col1):
                for u in range(UNITS):
                    for c, col in enumerate((col0, col1)):
                        load(h, 2 * u + c, w[:, bass.ds(row + HK4 * u, HK4), bass.ds(col, HC)])

            def plain_panels(h, w):
                with sp.Fori(0, PANELS) as p:
                    panel(h + p * PANEL, w, 0, p * 2 * HC, p * 2 * HC + HC)

            def mlp(layer, h0):
                with sp.Fori(0, SLABS) as s:
                    h = h0 + s * SLAB_HALVES
                    with sp.Fori(0, PANELS) as p:
                        col = s * SLAB + p * 2 * HC
                        panel(h + p * PANEL, w1[layer], 0, col, col + HC)
                    with sp.Fori(0, PANELS) as p:
                        panel(h + PANELS * PANEL + p * PANEL, w2[layer], s * KT,
                              p * 2 * HC, p * 2 * HC + HC)

            with sp.Fori(0, GH) as i:
                h = H_GLA + i * HEAD_HALVES
                panel(h, w_in, 0, i * HK, GK + i * HK)
                v0 = 2 * GK + i * HV
                panel(h + PANEL, w_in, 0, v0, v0 + HC)
                r0 = 2 * GK + D + i * HV
                panel(h + 2 * PANEL, w_in, 0, r0, r0 + HC)
            plain_panels(H_OUT, w_out)
            sp.wait_ge(s_gated, GH)
            sp.dma_start(side_in1.rearrange("p (t n) -> p t n", t=KT),
                         w_dkv[:, :, LORA:LORA + ROPE]).then_inc(s_side1, 16)
            sp.dma_start(causal, t["c_causal"]).then_inc(s_causal, 16)
            sp.dma_start(rot, t["c_rot"]).then_inc(s_rotm, 16)
            sp.dma_start(freqs[:, 0:1], t["c_freqs"]).then_inc(s_freqs, 16)
            sp.dma_start(pos_i, t["positions"][0:1, :].broadcast_to([P, S])).then_inc(s_pos, 16)
            mlp(0, H_MLP0)
            panel(H_DKV, w_dkv, 0, 0, HC)
            panel(H_DQ, w_dq, 0, 0, HC)
            with sp.Fori(0, PAIRS) as i:
                h = H_PAIR + i * 4
                load(h, 0, w_uk[:, :, bass.ds(i * HC, HC)])
                load(h, 1, w_uv[:, :, bass.ds(i * HC, HC)])
                load(h, 2, w_uq[:, :, bass.ds(i * 2, 2), 0:NOPE])
                load(h, 3, w_uq[:, :, bass.ds(i * 2, 2), NOPE:QH], n=HF // 2)
            plain_panels(H_WO, w_o)
            mlp(1, H_MLP1)
            for n in range(8):
                b, c = n // 4, n % 4
                sp.wait_ge(s_finc, n + 1)
                sp.dma_start(out_dram[:, b, c * 512:(c + 1) * 512],
                             o_nat[:, b, c * 512:(c + 1) * 512]).then_inc(s_out, 16)
            sp.wait_ge(s_out, 8 * 16)

        @block.gpsimd
        def _(pool):
            steps = [0]

            def step(ins):
                steps[0] += 1
                ins.then_inc(s_pool, 1)
                pool.wait_ge(s_pool, steps[0])

            def squares(st, src, chunks, ready=None):
                for c in range(0, chunks, 4):
                    if ready:
                        ready(c)
                    part = src[:, c:c + 4, :]
                    step(pool.tensor_tensor(sq_b if c else sq_a, part, part, ALU.mult))
                    if c:
                        step(pool.tensor_tensor(sq_a, sq_a, sq_b, ALU.add))
                step(pool.tensor_tensor(sq_a[:, 0:2, :], sq_a[:, 0:2, :], sq_a[:, 2:4, :], ALU.add))
                if st:
                    pool.wait_ge(s_rstd, st)
                pool.tensor_tensor(sqs[:, 0:S], sq_a[:, 0, :], sq_a[:, 1, :], ALU.add)\
                    .then_inc(s_sqs, 1)

            def final(g):
                return lambda c: pool.wait_ge(s_read, g + c // 2 + 2 + 2)

            def mlp(k0):
                with pool.Fori(0, SLABS) as s:
                    with pool.Fori(0, PANELS) as p:
                        for c in range(2):
                            k = k0 + s * (PANELS * 2) + p * 2 + c
                            pool.wait_ge(s_act, k + 1)
                            pool.wait_ge(s_hid, k + 1)
                            pool.tensor_tensor(sq_h[:, c], act[:, c], act[:, c], ALU.mult)\
                                .then_inc(s_acts, 1)
                            pool.wait_ge(s_acts, k + 1)
                            pool.wait_ge(s_acthi, k + 1)
                            hid = xb[:, bass.ds(p * 4 + 2 * c, 2)]
                            pool.tensor_tensor(hid[:, :, 1, :], sq_h[:, c],
                                               hid[:, :, 0, :].bitcast(F32), ALU.subtract)\
                                .then_inc(s_hid, 1)

            pool.sem_inc(s_hid, 2)
            pool.sem_inc(s_pr, 1)
            for n in range(2):
                pool.memset(eps[:, n:n + 1], (1.0, 4.0)[n] * EPS).then_inc(s_eps, 1)
            pool.memset(ones[:, :], 1.0).then_inc(s_ones, 1)
            step(pool.memset(low_nat, 0.0))
            step(pool.memset(low_nat[:, :, RANK:RANK + 1], 1.0))
            pool.memset(w_up, 0.0).then_inc(s_pad, 1)
            pool.wait_ge(s_trc, 8)
            squares(ST_MIX0, resid, KT)

            with pool.Fori(0, GH) as i:
                for b in range(TB):
                    pool.wait_ge(s_dec, 4 * i + 2 * b + 3)
                    pool.wait_ge(s_k, i + 1)
                    pool.wait_ge(s_qd, 2 * i + b + 1)
                    if b == 0:
                        pool.tensor_tensor(kx, dec[:, :, SUFFIX, :], k_sb[:, :, 0:P], ALU.mult)\
                            .then_inc(s_kx, 1)
                        pool.wait_ge(s_kx, i + 1)
                    for d in range(2):
                        keys = k_sb[:, d:d + 1, b * P:(b + 1) * P].broadcast_to([P, 8, P])
                        ins = pool.tensor_tensor(dec[:, d], dec[:, d], keys, ALU.mult)
                    ins.then_inc(s_kd, 1)

            squares(ST_MLP0, resid, KT, final(G_OUT))
            mlp(0)
            squares(ST_MIX1, resid, KT, final(G_DKV - 2 * PANELS))
            pool.memset(keys_r, 0.0).then_inc(s_krz, 1)
            pool.wait_ge(s_lat, 2)
            squares(ST_C, lat, LT)
            pool.wait_ge(s_lat, 4)
            squares(ST_CQ, lat, LT)

            def slot(i, b, proj=True, attn=True):
                if attn:
                    pool.wait_ge(s_rden, i)
                    for h in range(2):
                        for blk in range(2):
                            part = pr_sb[:, h, 0:P] if blk == 0 else pr_sb[:, h, P:3 * P]
                            col = 2 * blk + h
                            by = rden[:, col:col + 1].broadcast_to(list(part.shape))
                            ins = pool.tensor_tensor(part, part, by, ALU.mult)
                    ins.then_inc(s_pr, 1)
                if proj:
                    pool.wait_ge(s_raw, i + 1)
                    pool.wait_ge(s_qr, i)
                    pool.tensor_tensor(cos_r, raw_r, cos, ALU.mult).then_inc(s_cosr, 1)
                    pool.wait_ge(s_cosr, i + 1)
                    pool.wait_ge(s_sinr, i + 1)
                    pool.tensor_tensor(qr_sb[:, b, :], cos_r, sin_r, ALU.add).then_inc(s_qr, 1)

            slot(0, 0, attn=False)
            with pool.Fori(0, PAIRS // 2 - 1) as m:
                slot(m * 2 + 1, 1)
                slot(m * 2 + 2, 0)
            slot(PAIRS - 1, 1)
            slot(PAIRS, 0, proj=False)

            squares(ST_MLP1, resid, KT, final(G_WO))
            mlp(UP_GROUPS)
            for c in range(0, 12, 4):
                final(G_END - 2 * PANELS)(c)
                part = resid[:, c:c + 4, :]
                step(pool.tensor_tensor(sq_b if c else sq_a, part, part, ALU.mult))
                if c:
                    step(pool.tensor_tensor(sq_a, sq_a, sq_b, ALU.add))
            pool.sem_inc(s_sqs, 1)

        @block.scalar
        def _(act_e):
            sc = act_e

            pair_loads = [0]

            def high(h, j, n=HF, pairs=None):
                slot = j % RING
                more = 16 * (pair_loads[0] if pairs is None else pairs) if slot >= 2 else 0
                sc.wait_ge(s_landed[slot], h * (16 // RING) + (16 * (j // RING + 1) + more))
                sc.wait_ge(s_mult, h + j + 1)
                src = stage[:, slot, 0:n].rearrange("p (t n) -> p t n", n=HC)
                sc.activation(wts[:, slot, 0:n // HC, 0, :], src, ACT.Copy).then_inc(s_high, 1)

            def copy_corr(h, j, c, banks=2):
                sc.wait_ge(s_mult, h + j + 1 + RING)
                sc.activation(corr[:, c, 0:banks, :], ps[:, 2 * c:2 * c + banks, S:2 * S], ACT.Copy)\
                    .then_inc(s_corr, 1)

            def convert(src, gain, dst, c0, c1):
                for c in range(c0, c1):
                    sc.activation(dst[:, c, 0, :], src[:, c, :], ACT.Copy,
                                  scale=gains[:, gain + c:gain + c + 1]).then_inc(s_xhi, 1)

            def last_panel(h, g, gain):
                for j in range(2, PANEL + 2):
                    high(h, j)
                    if j < 8:
                        c = 2 * (j - 2)
                        sc.wait_ge(s_read, g + c // 2 + 1 + 2)
                        convert(resid, gain, xa, c, c + 2)

            def take_root(st, features, columns=False):
                sc.wait_ge(s_stat, st + 1)
                if st:
                    sc.wait_ge(s_rstd, st)
                n = S + TB if columns else S
                sc.activation(root[:, 0:n], ps[:, 7, 0:n], ACT.Sqrt, scale=1.0 / features,
                              bias=eps[:, 0:1]).then_inc(s_root, 1)

            def first_panel(h, g, gain, st, columns=False, more=None):
                for j in range(2, PANEL + 2):
                    high(h, j)
                    if j < 4:
                        c = KT - 4 + 2 * (j - 2)
                        sc.wait_ge(s_read, g - 2 + (j - 2) + 1 + 2)
                        convert(resid, gain, xa, c, c + 2)
                    if more:
                        more(j)
                    if j == 8:
                        take_root(st, D, columns)

            def highs(h, j0, j1):
                for j in range(j0, j1):
                    high(h, j)

            def up(h, p, k):
                for c in range(2):
                    copy_corr(h, PANEL - 2 + c, c)
                    sc.wait_ge(s_act, k + c + 1)
                    hid = xb[:, bass.ds(p * 4 + 2 * c, 2), 0, :]
                    sc.activation(hid, act[:, c], ACT.Square).then_inc(s_acthi, 1)

            def mlp(h0, g0, k0, gain, st, end):
                first_panel(h0, g0, gain, st)
                up(h0, 0, k0)
                with sc.Fori(1, PANELS) as p:
                    highs(h0 + p * PANEL, 2, PANEL + 2)
                    up(h0 + p * PANEL, p, k0 + p * 2)
                with sc.Fori(PANELS, 2 * PANELS) as p:
                    highs(h0 + p * PANEL, 2, PANEL + 2)
                with sc.Fori(1, SLABS - 1) as s:
                    h = h0 + s * SLAB_HALVES
                    k = k0 + s * (2 * PANELS)
                    with sc.Fori(0, PANELS) as p:
                        highs(h + p * PANEL, 2, PANEL + 2)
                        up(h + p * PANEL, p, k + p * 2)
                    with sc.Fori(PANELS, 2 * PANELS) as p:
                        highs(h + p * PANEL, 2, PANEL + 2)
                h = h0 + (SLABS - 1) * SLAB_HALVES
                k = k0 + (SLABS - 1) * (2 * PANELS)
                with sc.Fori(0, PANELS) as p:
                    highs(h + p * PANEL, 2, PANEL + 2)
                    up(h + p * PANEL, p, k + p * 2)
                with sc.Fori(PANELS, 2 * PANELS - 1) as p:
                    highs(h + p * PANEL, 2, PANEL + 2)
                end(h + (2 * PANELS - 1) * PANEL, g0 + SLABS * SLAB_GROUPS - 2 * PANELS)

            for free in (s_dec, s_ocp, s_ptc):
                sc.sem_inc(free, 1)
            sc.dma_start(ident[:, :], t["c_ident"]).then_inc(s_ident, 16)
            for n in range(4):
                cols = slice(n * 512, (n + 1) * 512)
                sc.dma_start(x_nat[:, :, cols], x_dram[:, :, cols]).then_inc(s_xin[n], 16)
            row = 0
            for w in (t["norm_mix"], t["norm_mlp"], t["kv_norm_in"], t["final_norm"], t["gla_norm"],
                      t["mla_kv_norm"], t["mla_q_norm"]):
                flat = w if len(w.shape) == 1 else w.rearrange("a b -> (a b)")
                n = flat.shape[0] // P
                sc.dma_start(gains_in[row:row + n, :], flat.rearrange("(r c) -> r c", c=P))\
                    .then_inc(s_gin, 16)
                row += n
            sc.dma_start(side_in0.rearrange("p (t n) -> p t n", t=KT),
                         w_in[:, :, 2 * GK + 2 * D:]).then_inc(s_side0, 16)
            sc.dma_start(sums_in, t["c_sums"]).then_inc(s_sums, 16)
            sc.dma_start(masks, t["c_masks"].rearrange("p (l n) -> p l n", l=8))\
                .then_inc(s_masks, 16)
            sc.wait_ge(s_pad, 1)
            sc.dma_start(w_up[0:RANK, :], t["gla_w_gate_up"][0]).then_inc(s_up, 16)
            sc.dma_start(w_up[RANK:RANK + 1, :], t["gla_b_gate"]).then_inc(s_up, 16)

            def gates():
                sc.wait_ge(s_z, 1)
                z_ps = ps[:, 4:8, :].rearrange("p b n -> p (b n)")
                sc.activation(z_sb, z_ps, ACT.Abs).then_inc(s_zact, 1)
                sc.wait_ge(s_zact, 1)
                sc.activation(z_sb, z_sb, ACT.Exp, scale=-1.0).then_inc(s_zact, 1)
                sc.wait_ge(s_zact, 2)
                sc.activation(z_sb, z_sb, ACT.Ln, bias=1.0).then_inc(s_zact, 1)
                sc.wait_ge(s_g, 1)
                g_by_head = g_sb.rearrange("p (b h n) -> p h b n", b=TB, h=GH)
                for i in range(GH):
                    sc.activation(xb[:, 4 * i:4 * i + 2, 0, :], g_by_head[:, i], ACT.Copy)\
                        .then_inc(s_ghi, 1)
                sc.wait_ge(s_glo, GH)

            def head_gate(i):
                sc.activation(gate, xb[:, bass.ds(4 * i, 2)].bitcast(F32), ACT.Copy)\
                    .then_inc(s_gcur, 1)

            def decays(i, b, d):
                sc.wait_ge(s_sum, 4 * i + 2 * b + d + 1)
                sc.activation(dec[:, d].rearrange("p (g l) n -> p g (l n)", g=2), ps[:, 4:6, :],
                              ACT.Exp, scale=1.0 / TAU).then_inc(s_dec, 1)

            def head_output(i, first=False):
                sc.wait_ge(s_o, i + 1)
                o_ps = ps[:, 6:8, :].rearrange("p b (e s) -> p (b e) s", e=2)
                sc.activation(sq_b, o_ps, ACT.Square).then_inc(s_osq, 1)
                if not first:
                    sc.wait_ge(s_gated, i)
                for e in range(4):
                    ins = sc.activation(o_sb[:, e, :], o_ps[:, e, :], ACT.Copy,
                                        scale=gains[:, N_GLA + e:N_GLA + e + 1])
                ins.then_inc(s_ocp, 1)

            def gating(h, i):
                highs(h, 2, 4)
                sc.wait_ge(s_r, 2 * i)
                sc.activation(e_sb, r_sb, ACT.Tanh, scale=0.5).then_inc(s_tanh, 1)
                sc.wait_ge(s_ost, i)
                sc.activation(root_o, ps[:, 5, 0:S], ACT.Sqrt, scale=4.0 / HV, bias=eps[:, 1:2])\
                    .then_inc(s_oroot, 1)
                highs(h, 4, 6)
                sc.wait_ge(s_full, i)
                sc.activation(xb[:, bass.ds(4 * i - 4, 4), 0, :], o_sb, ACT.Copy)\
                    .then_inc(s_fullhi, 1)

            sc.wait_ge(s_gains, 1)
            for u in range(UNITS):
                sc.wait_ge(s_trc, 2 * u + 2)
                convert(resid, N_MIX0, xa, HK4 * u, HK4 * u + HK4)
                high(H_GLA, u)
            sc.wait_ge(s_side0, 16)
            sc.activation(side0[:, 0, :], side_in0, ACT.Copy).then_inc(s_sidehi, 1)
            sc.wait_ge(s_sums, 16)
            sc.activation(sums.rearrange("p a b -> p (a b)"), sums_in, ACT.Copy)\
                .then_inc(s_sumsr, 1)
            highs(H_GLA, 4, 10)
            copy_corr(H_GLA, 6, 0)
            copy_corr(H_GLA, 7, 1)
            sc.wait_ge(s_eps, 2)
            highs(H_GLA, 10, 12)
            take_root(ST_MIX0, D, True)
            highs(H_GLA, 12, 14)
            gates()
            head_gate(0)
            highs(H_GLA, 14, 18)
            copy_corr(H_GLA, 14, 0)
            copy_corr(H_GLA, 15, 1)
            highs(H_GLA, 18, 20)
            decays(0, 0, 0)
            decays(0, 0, 1)
            highs(H_GLA, 20, 23)
            decays(0, 1, 0)
            decays(0, 1, 1)
            highs(H_GLA, 23, 26)
            copy_corr(H_GLA, 22, 0)
            copy_corr(H_GLA, 23, 1)
            head_output(0, True)

            with sc.Fori(1, GH) as i:
                h = H_GLA + i * HEAD_HALVES
                head_gate(i)
                gating(h, i)
                highs(h, 6, 8)
                decays(i, 0, 0)
                highs(h, 8, 10)
                decays(i, 0, 1)
                copy_corr(h, 6, 0)
                copy_corr(h, 7, 1)
                highs(h, 10, 18)
                decays(i, 1, 0)
                copy_corr(h, 14, 0)
                copy_corr(h, 15, 1)
                decays(i, 1, 1)
                highs(h, 18, 26)
                head_output(i)
                copy_corr(h, 22, 0)
                copy_corr(h, 23, 1)

            gating(H_OUT, GH)
            highs(H_OUT, 6, PANEL + 2)
            with sc.Fori(1, PANELS - 1) as p:
                highs(H_OUT + p * PANEL, 2, PANEL + 2)
            last_panel(H_OUT + (PANELS - 1) * PANEL, G_OUT, N_MLP0)
            mlp(H_MLP0, G_MLP0, 0, N_MLP0, ST_MLP0, lambda h, g: last_panel(h, g, N_KVIN))

            def queries_in(j):
                if j >= 5:
                    convert(resid, N_MIX1, xb, 4 * (j - 5), min(4 * (j - 5) + 4, KT))

            first_panel(H_DKV, G_DKV, N_KVIN, ST_MIX1, True, queries_in)
            copy_corr(H_DKV, PANEL - 2, 0)
            copy_corr(H_DKV, PANEL - 1, 1)
            sc.wait_ge(s_side1, 16)
            sc.activation(side1[:, 0, :], side_in1, ACT.Copy).then_inc(s_sidehi, 1)
            highs(H_DQ, 2, 8)
            take_root(ST_C, LORA)

            def convert_lat(n, dst):
                sc.wait_ge(s_laty, n)
                for c in range(LT):
                    sc.activation(dst[:, c, 0, :], lat[:, c, :], ACT.Copy).then_inc(s_xhi, 1)

            convert_lat(1, xc)
            highs(H_DQ, 8, PANEL + 2)
            copy_corr(H_DQ, PANEL - 2, 0)
            copy_corr(H_DQ, PANEL - 1, 1)
            sc.wait_ge(s_ang, 2)
            sc.activation(sin, sin, ACT.Sin).then_inc(s_trig, 1)
            sc.activation(cos, cos, ACT.Sin).then_inc(s_trig, 1)
            take_root(ST_CQ, LORA)
            convert_lat(2, xq)

            def slot(i, proj=True, attn=True):
                h = H_PAIR + i * 4
                if proj:
                    high(h, 2, pairs=i + 1)
                    copy_corr(h, 0, 0)
                    high(h, 3, n=HF // 2, pairs=i + 1)
                if attn:
                    sc.wait_ge(s_nmx, i)
                    for hd in range(2):
                        for blk in range(2):
                            col = 2 * blk + hd
                            a, z = (0, P) if blk == 0 else (P, 3 * P)
                            ins = sc.activation(pr_sb[:, hd, a:z], sc_sb[:, hd, a:z], ACT.Exp,
                                                bias=nmx[:, col:col + 1], scale=MLA_SCALE,
                                                accum_out=den[:, col:col + 1])
                    ins.then_inc(s_exp, 1)
                if proj:
                    copy_corr(h, 1, 1)
                    high(h, 4)
                    copy_corr(h, 2, 0)
                    high(h, 5)
                if attn:
                    sc.wait_ge(s_pt, i)
                    sc.activation(pt_sb, ps[:, 4:6, 0:3 * P], ACT.Copy).then_inc(s_ptc, 1)
                if proj:
                    copy_corr(h, 3, 1, banks=1)
                if attn:
                    sc.wait_ge(s_ov, i)
                    sc.activation(xb[:, bass.ds(2 * i - 2, 2), 0, :],
                                  ps[:, 6, :].rearrange("p (h s) -> p h s", h=2), ACT.Copy)\
                        .then_inc(s_ohi, 1)

            slot(0, attn=False)
            with sc.Fori(1, PAIRS) as i:
                slot(i)
            slot(PAIRS, proj=False)
            pair_loads[0] = PAIRS

            with sc.Fori(0, PANELS - 1) as p:
                highs(H_WO + p * PANEL, 2, PANEL + 2)
            last_panel(H_WO + (PANELS - 1) * PANEL, G_WO, N_MLP1)

            def result(c0, c1):
                for c in range(c0, c1, 2):
                    sc.wait_ge(s_read, G_END - 2 * PANELS + c // 2 + 1 + 2)
                    for n in range(c, c + 2):
                        sc.activation(y_sb[:, n, :], resid[:, n, :], ACT.Copy,
                                      scale=gains[:, N_FIN + n:N_FIN + n + 1]).then_inc(s_y, 1)

            def end(h, g):
                for j in range(2, PANEL):
                    high(h, j)
                    result(2 * (j - 2), 2 * (j - 2) + 2)

            mlp(H_MLP1, G_MLP1, UP_GROUPS, N_MLP1, ST_MLP1, end)
            sc.wait_ge(s_read, G_END + 2)
            sc.wait_ge(s_sqs, ST_FIN + 1)
            sc.activation(sq_b, resid[:, KT - 4:KT, :], ACT.Square).then_inc(s_ysq, 1)
            result(KT - 4, KT)
            sc.wait_ge(s_stat, ST_FIN + 1)
            sc.wait_ge(s_rstd, ST_FIN)
            sc.activation(root[:, S:S + TB], ps[:, 7, S:S + TB], ACT.Sqrt, scale=1.0 / D,
                          bias=eps[:, 0:1]).then_inc(s_root, 1)

        @block.tensor
        def _(pe):
            def begin(h, j, g=None):
                pe.wait_ge(s_split, h + j + 1 + RING)
                if g is not None:
                    pe.wait_ge(s_read, g + 1)

            def weights(j, c, part, col):
                return wts[:, j % RING, c, part, col:col + P]

            def products(bank, n, main, rest, first, last):
                corr_at = slice(n // 2, n)
                if last:
                    pe.matmul(bank[:, corr_at], *rest, start=False, stop=False)
                ins = pe.matmul(bank[:, 0:n], *main, start=first, stop=last)
                if not last:
                    ins = pe.matmul(bank[:, corr_at], *rest, start=False, stop=False)
                return ins

            def half_t(j, c2, x, x0, first, last):
                for n in range(2):
                    for c in range(HK4):
                        ins = products(ps[:, 2 * c2 + n], 2 * S,
                                       (weights(j, c, 0, n * P), x[:, x0 + c]),
                                       (weights(j, c, 1, n * P), x[:, x0 + c, 0, :]),
                                       first and c == 0, last and c == HK4 - 1)
                ins.then_inc(s_mult, 1)

            def half_n(j, c2, x, x0, first, last):
                for b in range(TB):
                    tok = slice(b * P, (b + 1) * P)
                    for c in range(HK4):
                        ins = products(ps[:, 2 * c2 + b], 2 * HC,
                                       (x[:, x0 + c, 0, tok], wts[:, j % RING, c]),
                                       (x[:, x0 + c, 1, tok], wts[:, j % RING, c, 0, :]),
                                       first and c == 0, last and c == HK4 - 1)
                ins.then_inc(s_mult, 1)

            def panel(h, g, x, ready=None, half=half_t, after=None):
                for u in range(UNITS):
                    if ready:
                        ready(u)
                    for c2 in range(2):
                        j = 2 * u + c2
                        begin(h, j, g + c2 if u == 0 else None)
                        half(j, c2, x, HK4 * u, u == 0, u == UNITS - 1)
                        if after and j in after:
                            after[j]()

            def stat(st, columns):
                pe.wait_ge(s_sqs, st + 1)
                if st:
                    pe.wait_ge(s_root, st)
                ins = pe.matmul(ps[:, 7, 0:S], ones[:, :], sqs[:, 0:S], start=True, stop=True)
                for b in range(TB if columns else 0):
                    ins = pe.matmul(ps[:, 7, S + b:S + b + 1], sqs[:, b * P:(b + 1) * P],
                                    ones[:, 0:1], start=True, stop=True)
                ins.then_inc(s_stat, 1)

            def inputs(x0):
                return lambda u: pe.wait_ge(s_x, x0 + HK4 * (u + 1))

            def hidden(k):
                return lambda u: pe.wait_ge(s_hid, k + 2 * (u + 1) + 2)

            def mlp(h0, g0, k0, x0, st):
                panel(h0, g0, xa, inputs(x0), after={4: lambda: stat(st, False)})
                with pe.Fori(1, PANELS) as p:
                    panel(h0 + p * PANEL, g0 + p * 2, xa)
                with pe.Fori(PANELS, 2 * PANELS) as p:
                    panel(h0 + p * PANEL, g0 + p * 2, xb, hidden(k0))
                with pe.Fori(1, SLABS) as s:
                    h = h0 + s * SLAB_HALVES
                    g = g0 + s * SLAB_GROUPS
                    with pe.Fori(0, PANELS) as p:
                        panel(h + p * PANEL, g + p * 2, xa)
                    with pe.Fori(PANELS, 2 * PANELS) as p:
                        panel(h + p * PANEL, g + p * 2, xb, hidden(k0 + s * (2 * PANELS)))

            pe.sem_inc(s_mult, RING)
            pe.wait_ge(s_ident, 16)
            for bank in range(8):
                if bank % 2 == 0:
                    pe.wait_ge(s_xin[bank // 2], 16)
                for n in range(4):
                    c, b = 2 * bank + n // 2, n % 2
                    ins = pe.transpose(ps[:, bank, n * P:(n + 1) * P],
                                       x_nat[:, b, c * P:(c + 1) * P], ident[:, :])
                ins.then_inc(s_tr, 1)
            pe.wait_ge(s_gin, 16 * 7)
            pe.wait_ge(s_trc, 5)
            pe.transpose(ps[:, 4, 0:N_GAINS], gains_in[0:N_GAINS, :], ident[0:N_GAINS, 0:N_GAINS])\
                .then_inc(s_gtr, 1)

            def low_rank():
                pe.wait_ge(s_sidelo, 1)
                pe.wait_ge(s_trc, 8)
                for b in range(TB):
                    for c in range(KT):
                        cols = slice(c * RANK, (c + 1) * RANK)
                        tok = slice(b * P, (b + 1) * P)
                        ins = products(ps[:, 4 + b], 2 * RANK,
                                       (xa[:, c, 0, tok], side0[:, :, cols]),
                                       (xa[:, c, 1, tok], side0[:, 0, cols]), c == 0, c == KT - 1)
                ins.then_inc(s_low, 1)
                pe.wait_ge(s_ones, 1)
                stat(ST_MIX0, True)

            def low_transposed():
                pe.wait_ge(s_lownat, 1)
                for b in range(TB):
                    ins = pe.transpose(ps[:, 6, b * P:(b + 1) * P], low_nat[:, b, :], ident[:, :])
                ins.then_inc(s_lowt, 1)

            def gates_in():
                pe.wait_ge(s_lowtc, 1)
                pe.wait_ge(s_root, ST_MIX0 + 1)
                pe.wait_ge(s_up, 32)
                for b in range(TB):
                    for n in range(2):
                        ins = pe.matmul(ps[:, 4 + 2 * b + n, :], low_t[:, b * P:(b + 1) * P],
                                        w_up[:, n * 512:(n + 1) * 512], start=True, stop=True)
                ins.then_inc(s_z, 1)

            def gate_sums(i, b, d):
                r = 2 * b + d
                if r == 0:
                    pe.wait_ge(s_gcur, i + 1)
                    if not isinstance(i, int):
                        pe.wait_ge(s_oroot, i)
                pe.wait_ge(s_dec, 4 * i + r + 1)
                for n in range(2):
                    at = 4 * n + (b if n else 0)
                    for part in range(2):
                        ins = pe.matmul(ps[:, 4 + n, :], gate[:, b, part, d * P:(d + 1) * P],
                                        sums[:, at:at + 4, :], start=part == 0, stop=part == 1)
                ins.then_inc(s_sum, 1)

            def scores(i, b):
                pe.wait_ge(s_qd, 2 * i + b + 1)
                pe.wait_ge(s_kd, 2 * i + b + 1)
                if b == 0:
                    pe.wait_ge(s_ocp, i + 1)
                else:
                    pe.wait_ge(s_att, 2 * i + 1)
                tok = slice(b * P, (b + 1) * P)
                for n in range(8):
                    at = PLACES[b][n] if n < 7 else None
                    for d in range(2):
                        lhs = dec[:, d, at, :] if n < 7 else k_sb[:, d, tok]
                        rhs = qdec[:, d, at, :] if n < 7 else q_sb[:, d, tok]
                        ins = pe.matmul(ps[:, 6 + n // 4, (n % 4) * P:(n % 4 + 1) * P], lhs, rhs,
                                        start=d == 0, stop=d == 1)
                if b == 1:
                    for d in range(2):
                        ins = pe.matmul(ps[:, 4, 0:P], kx[:, d, :], qdec[:, d, PREFIX, :],
                                        start=d == 0, stop=d == 1)
                ins.then_inc(s_sc, 1)

            def output(i):
                pe.wait_ge(s_att, 2 * i + 2)
                pe.wait_ge(s_v, 2 * i + 2)
                for e in range(4):
                    bank, col = 6 + e // 2, (e % 2) * S
                    feat = slice(e * P, (e + 1) * P)
                    pe.matmul(ps[:, bank, col:col + P], v_sb[:, 0, feat], att[:, 0:P],
                              start=True, stop=True)
                    pe.matmul(ps[:, bank, col + P:col + S], v_sb[:, 0, feat], att[:, P:S],
                              start=True, stop=False)
                    ins = pe.matmul(ps[:, bank, col + P:col + S], v_sb[:, 1, feat],
                                    att[:, S:3 * P], start=False, stop=True)
                ins.then_inc(s_o, 1)
            def output_squares(i):
                pe.wait_ge(s_osq, i + 1)
                for e in range(4):
                    ins = pe.matmul(ps[:, 5, 0:S], ones[:, :], sq_b[:, e, :], start=e == 0,
                                    stop=e == 3)
                ins.then_inc(s_ost, 1)

            panel(H_GLA, G_GLA, xa, inputs(X_GLA), after={7: low_rank})
            pe.wait_ge(s_sumsr, 1)
            panel(H_GLA + PANEL, G_GLA + 2, xa, half=half_n,
                  after={1: low_transposed, 2: gates_in})
            panel(H_GLA + 2 * PANEL, G_GLA + 4, xa,
                  after={1: lambda: gate_sums(0, 0, 0), 2: lambda: gate_sums(0, 0, 1),
                         4: lambda: (scores(0, 0), gate_sums(0, 1, 0)),
                         5: lambda: gate_sums(0, 1, 1), 7: lambda: scores(0, 1)})
            output(0)
            output_squares(0)

            with pe.Fori(1, GH) as i:
                h = H_GLA + i * HEAD_HALVES
                g = G_GLA + i * 6
                panel(h, g, xa, after={3: lambda: gate_sums(i, 0, 0), 5: lambda: gate_sums(i, 0, 1)})
                panel(h + PANEL, g + 2, xa, half=half_n,
                      after={3: lambda: scores(i, 0), 5: lambda: gate_sums(i, 1, 0),
                             7: lambda: gate_sums(i, 1, 1)})
                panel(h + 2 * PANEL, g + 4, xa,
                      after={1: lambda: scores(i, 1), 5: lambda: output(i)})
                output_squares(i)

            with pe.Fori(0, PANELS) as p:
                panel(H_OUT + p * PANEL, G_OUT + p * 2, xb,
                      lambda u: pe.wait_ge(s_gated, u + 1))
            mlp(H_MLP0, G_MLP0, 0, X_MLP0, ST_MLP0)

            panel(H_DKV, G_DKV, xa, inputs(X_KV), after={4: lambda: stat(ST_MIX1, True)})
            panel(H_DQ, G_DQ, xb, inputs(X_Q), after={3: lambda: stat(ST_C, False)})
            pe.wait_ge(s_sidelo, 2)
            for b in range(TB):
                for c in range(KT):
                    cols = slice(c * ROPE, (c + 1) * ROPE)
                    tok = slice(b * P, (b + 1) * P)
                    ins = products(ps[:, 4 + b], 2 * ROPE, (xa[:, c, 0, tok], side1[:, :, cols]),
                                   (xa[:, c, 1, tok], side1[:, 0, cols]), c == 0, c == KT - 1)
            ins.then_inc(s_low, 1)

            def keys(i):
                h, g = H_PAIR + i * 4, G_PAIR + i * 4
                begin(h, 0, g)
                half_t(0, 0, xc, 0, True, True)

            def values(i):
                h, g = H_PAIR + i * 4, G_PAIR + i * 4
                begin(h, 1, g + 1)
                half_n(1, 1, xc, 0, True, True)

            def queries(i):
                h, g = H_PAIR + i * 4, G_PAIR + i * 4
                begin(h, 2, g + 2)
                half_t(2, 0, xq, 0, True, True)

            def rotary_queries(i):
                h, g = H_PAIR + i * 4, G_PAIR + i * 4
                begin(h, 3, g + 3)
                for c in range(LT):
                    cols = (c % 2) * P
                    ins = products(ps[:, 2], 2 * S, (weights(3, c // 2, 0, cols), xq[:, c]),
                                   (weights(3, c // 2, 1, cols), xq[:, c, 0, :]),
                                   c == 0, c == LT - 1)
                ins.then_inc(s_mult, 1)

            def rotate(i):
                pe.wait_ge(s_raw, i + 1)
                pe.wait_ge(s_sinr, i)
                pe.matmul(ps[:, 7, 0:S], rot, raw_r, start=True, stop=True).then_inc(s_rot, 1)

            def dots(i, b):
                pe.wait_ge(s_read, G_PAIR + i * 4 + 2)
                pe.wait_ge(s_qr, i)
                pe.wait_ge(s_ptc, i)
                for hd in range(2):
                    for blk in range(2):
                        n = (blk + 1) * P
                        dst = ps[:, 4 + hd, blk * P:blk * P + n]
                        tok = slice(blk * P, (blk + 1) * P)
                        pe.matmul(dst, qn_sb[:, b, hd, tok], kt_sb[:, b, hd, 0:n], start=True,
                                  stop=False)
                        ins = pe.matmul(dst, qr_sb[:, b, tok], keys_r[:, hd, 0:n], start=False,
                                        stop=True)
                ins.then_inc(s_dots, 1)

            def turn(i):
                pe.wait_ge(s_pr, i + 1)
                for hd in range(2):
                    for n in range(3):
                        ins = pe.transpose(ps[:, 4 + hd, n * P:(n + 1) * P],
                                           pr_sb[:, hd, n * P:(n + 1) * P], ident[:, :])
                ins.then_inc(s_pt, 1)

            def weigh(i, b):
                pe.wait_ge(s_ptc, i + 1)
                pe.wait_ge(s_ox, i)
                for hd in range(2):
                    feat = slice(hd * P, (hd + 1) * P)
                    at = hd * S
                    pe.matmul(ps[:, 6, at:at + P], vt_sb[:, b, 0, feat], pt_sb[:, hd, 0:P],
                              start=True, stop=True)
                    pe.matmul(ps[:, 6, at + P:at + S], vt_sb[:, b, 0, feat], pt_sb[:, hd, P:S],
                              start=True, stop=False)
                    ins = pe.matmul(ps[:, 6, at + P:at + S], vt_sb[:, b, 1, feat],
                                    pt_sb[:, hd, S:3 * P], start=False, stop=True)
                ins.then_inc(s_ov, 1)

            pe.wait_ge(s_x, X_C + LT)
            keys(0)
            values(0)
            stat(ST_CQ, False)
            pe.wait_ge(s_krn, 1)
            for b in range(TB):
                ins = pe.transpose(ps[:, 6, b * P:(b + 1) * P], kr_nat[:, b, :], ident[:, :])
            ins.then_inc(s_krt, 1)
            pe.wait_ge(s_krc, 1)
            pe.wait_ge(s_rotm, 16)
            pe.wait_ge(s_root, ST_CQ + 1)
            pe.matmul(ps[:, 7, 0:S], rot, raw_r, start=True, stop=True).then_inc(s_krot, 1)
            pe.wait_ge(s_x, X_CQ + LT)
            queries(0)
            rotary_queries(0)
            pe.wait_ge(s_keysr, 2)
            rotate(0)

            def slot(i, b):
                keys(i)
                dots(i, 1 - b)
                values(i)
                queries(i)
                turn(i)
                rotary_queries(i)
                weigh(i, 1 - b)
                rotate(i)

            with pe.Fori(0, PAIRS // 2 - 1) as m:
                slot(m * 2 + 1, 1)
                slot(m * 2 + 2, 0)
            slot(PAIRS - 1, 1)
            dots(PAIRS, 1)
            turn(PAIRS)
            weigh(PAIRS, 1)

            with pe.Fori(0, PANELS) as p:
                panel(H_WO + p * PANEL, G_WO + p * 2, xb,
                      lambda u: pe.wait_ge(s_ox, 2 * (u + 1) + 1))
            mlp(H_MLP1, G_MLP1, UP_GROUPS, X_MLP1, ST_MLP1)

            for n, ready in enumerate(((s_sqs, ST_FIN + 1), (s_ysq, 1))):
                pe.wait_ge(*ready)
            pe.wait_ge(s_root, ST_FIN)
            for b in range(TB):
                for n in range(8):
                    src = (sq_a, sq_b)[n // 4][:, n % 4, b * P:(b + 1) * P]
                    ins = pe.matmul(ps[:, 7, S + b:S + b + 1], src, ones[:, 0:1], start=n == 0,
                                    stop=n == 7)
            ins.then_inc(s_stat, 1)
            for n in range(8):
                b, c0 = n // 4, (n % 4) * 4
                pe.wait_ge(s_y, KT)
                if n == 7:
                    pe.wait_ge(s_root, ST_FIN + 1)
                for c in range(4):
                    ins = pe.transpose(ps[:, n, c * P:(c + 1) * P],
                                       y_sb[:, c0 + c, b * P:(b + 1) * P], ident[:, :])
                ins.then_inc(s_fin, 1)

        @block.vector
        def _(dve):
            steps = [0]

            def step(ins):
                steps[0] += 1
                ins.then_inc(s_dve, 1)
                dve.wait_ge(s_dve, steps[0])

            def low(h, j, n=HF):
                slot = j % RING
                dve.wait_ge(s_high, h + j + 1)
                src = stage[:, slot, 0:n].rearrange("p (t n) -> p t n", n=HC)
                dve.tensor_tensor(wts[:, slot, 0:n // HC, 1, :], src,
                                  wts[:, slot, 0:n // HC, 0, :].bitcast(F32), ALU.subtract)\
                    .then_inc(s_split, 1)

            def lows(h, j0, j1):
                for j in range(j0, j1):
                    low(h, j)

            def convert(src, gain, dst, x0, c0, c1):
                for c in range(c0, c1):
                    dve.wait_ge(s_xhi, x0 + c + 1)
                    dve.scalar_tensor_tensor(out=dst[:, c, 1, :], in0=src[:, c, :],
                                             scalar=gains[:, gain + c:gain + c + 1],
                                             in1=dst[:, c, 0, :].bitcast(F32),
                                             op0=ALU.mult, op1=ALU.subtract).then_inc(s_x, 1)

            def factors(st, columns=False, dst=None):
                dve.wait_ge(s_root, st + 1)
                n = S + TB if columns else S
                dve.reciprocal(rstd[:, 0:n] if dst is None else dst, root[:, 0:n])\
                    .then_inc(s_rstd, 1)
                dve.wait_ge(s_rstd, st + 1)

            def last_panel(h, p, r, gain, x0):
                for j in range(2, PANEL + 2):
                    low(h, j)
                    if j < 8:
                        convert(resid, gain, xa, x0, 2 * (j - 2), 2 * (j - 2) + 2)
                down(h, p, r)

            def first_panel(h, gain, x0, more=None):
                for j in range(2, PANEL + 2):
                    low(h, j)
                    if j < 4:
                        c = KT - 4 + 2 * (j - 2)
                        convert(resid, gain, xa, x0, c, c + 2)
                    if more:
                        more(j)

            def sum_group(g, n, c, dst=None, banks=2):
                dve.wait_ge(s_corr, n + 1)
                to = total[:, c, 0:banks, :] if dst is None else dst
                dve.tensor_tensor(to, ps[:, 2 * c:2 * c + banks, 0:S], corr[:, c, 0:banks, :],
                                  ALU.add).then_inc(s_read, 1)

            def per_token(banks, factor=None):
                f = rstd[:, 0:S] if factor is None else factor
                return f.rearrange("p (o s) -> p o s", o=1).broadcast_to([P, banks, S])

            def up(g, p, k, cc):
                for c in range(2):
                    dve.wait_ge(s_hid, k + c + 1)
                    sum_group(g + c, cc + c, c)
                    dve.wait_ge(s_read, g + c + 3)
                    dve.scalar_tensor_tensor(out=act[:, c], in0=total[:, c], scalar=0.0,
                                             in1=per_token(2), op0=ALU.max, op1=ALU.mult)\
                        .then_inc(s_act, 1)

            def down(h, p, r):
                for c in range(2):
                    dve.wait_ge(s_mult, h + PANEL - 2 + c + 1 + RING)
                    to = resid[:, bass.ds(p * 4 + 2 * c, 2), :]
                    banks = ps[:, 2 * c:2 * c + 2]
                    dve.tensor_tensor(to, banks[:, :, 0:S], to, ALU.add).then_inc(s_main, 1)
                    dve.wait_ge(s_main, r + c + 1)
                    dve.tensor_tensor(to, banks[:, :, S:2 * S], to, ALU.add).then_inc(s_read, 1)

            def down_panels(h0, r0, count=PANELS, start=0):
                with dve.Fori(start, count) as p:
                    lows(h0 + p * PANEL, 2, PANEL + 2)
                    down(h0 + p * PANEL, p, r0 + p * 2)

            def mlp(h0, g0, k0, c0, r0, x0, gain, st, end):
                first_panel(h0, gain, x0)
                factors(st)
                up(g0, 0, k0, c0)
                with dve.Fori(1, PANELS) as p:
                    lows(h0 + p * PANEL, 2, PANEL + 2)
                    up(g0 + p * 2, p, k0 + p * 2, c0 + p * 2)
                down_panels(h0 + PANELS * PANEL, r0)
                with dve.Fori(1, SLABS - 1) as s:
                    h, g = h0 + s * SLAB_HALVES, g0 + s * SLAB_GROUPS
                    n = s * (2 * PANELS)
                    with dve.Fori(0, PANELS) as p:
                        lows(h + p * PANEL, 2, PANEL + 2)
                        up(g + p * 2, p, k0 + n + p * 2, c0 + n + p * 2)
                    down_panels(h + PANELS * PANEL, r0 + n)
                h, g = h0 + (SLABS - 1) * SLAB_HALVES, g0 + (SLABS - 1) * SLAB_GROUPS
                n = (SLABS - 1) * 2 * PANELS
                with dve.Fori(0, PANELS) as p:
                    lows(h + p * PANEL, 2, PANEL + 2)
                    up(g + p * 2, p, k0 + n + p * 2, c0 + n + p * 2)
                down_panels(h + PANELS * PANEL, r0 + n, PANELS - 1)
                end(h + (2 * PANELS - 1) * PANEL, r0 + n + 2 * (PANELS - 1))

            dve.sem_inc(s_split, RING)
            dve.sem_inc(s_read, 2)
            dve.sem_inc(s_ox, 1)
            for bank in range(8):
                dve.wait_ge(s_tr, bank + 1)
                dve.tensor_copy(resid[:, 2 * bank:2 * bank + 2, :],
                                ps[:, bank, :].rearrange("p (c s) -> p c s", c=2))\
                    .then_inc(s_trc, 1)
            dve.wait_ge(s_gtr, 1)
            dve.tensor_copy(gains[:, :], ps[:, 4, 0:N_GAINS]).then_inc(s_gains, 1)
            dve.wait_ge(s_gains, 1)
            for u in range(UNITS):
                convert(resid, N_MIX0, xa, X_GLA, HK4 * u, HK4 * u + HK4)
                low(H_GLA, u)
            dve.wait_ge(s_sidehi, 1)
            dve.tensor_tensor(side0[:, 1, :], side_in0, side0[:, 0, :].bitcast(F32), ALU.subtract)\
                .then_inc(s_sidelo, 1)

            def queries_keys(i):
                for c in range(2):
                    sum_group(G_GLA + i * 6 + c, C_GLA + i * 6 + c, c)

            def scale_queries_keys(i):
                for c, (to, scale, done) in enumerate(((q_sb, float(HK) ** -0.5, s_q),
                                                       (k_sb, 1.0, s_k))):
                    dve.wait_ge(s_read, G_GLA + i * 6 + c + 3)
                    dve.scalar_tensor_tensor(out=to, in0=total[:, c], scalar=scale,
                                             in1=per_token(2), op0=ALU.mult, op1=ALU.mult)\
                        .then_inc(done, 1)
                dve.wait_ge(s_q, i + 1)

            def gates():
                dve.wait_ge(s_low, 1)
                lt = low_tmp[:, 0:TB * RANK].rearrange("p (b c) -> p b c", b=TB)
                step(dve.tensor_copy(lt, ps[:, 4:6, RANK:2 * RANK]))
                step(dve.tensor_tensor(lt, ps[:, 4:6, 0:RANK], lt, ALU.add))
                factors(ST_MIX0, columns=True)
                dve.wait_ge(s_pad, 1)
                for b in range(TB):
                    ins = dve.tensor_scalar(low_nat[:, b, 0:RANK], lt[:, b, :],
                                            rstd[:, S + b:S + b + 1], None, ALU.mult)
                ins.then_inc(s_lownat, 1)
                dve.wait_ge(s_sumsr, 1)
                scale_queries_keys(0)
                dve.wait_ge(s_lowt, 1)
                dve.tensor_copy(low_t, ps[:, 6, 0:S]).then_inc(s_lowtc, 1)

            def split_gates():
                dve.wait_ge(s_zact, 3)
                z_ps = ps[:, 4:8, :].rearrange("p b n -> p (b n)")
                dve.scalar_tensor_tensor(out=g_sb, in0=z_ps, scalar=0.0, in1=z_sb, op0=ALU.min,
                                         op1=ALU.subtract).then_inc(s_g, 1)
                g_by_head = g_sb.rearrange("p (b h n) -> p h b n", b=TB, h=GH)
                for i in range(GH):
                    dve.wait_ge(s_ghi, i + 1)
                    part = xb[:, 4 * i:4 * i + 2]
                    dve.tensor_tensor(part[:, :, 1, :], g_by_head[:, i],
                                      part[:, :, 0, :].bitcast(F32), ALU.subtract)\
                        .then_inc(s_glo, 1)
                dve.wait_ge(s_glo, GH)
                dve.wait_ge(s_masks, 16)

            def scaled_queries(i, b):
                for d in range(2):
                    dve.wait_ge(s_dec, 4 * i + 2 * b + d + 2)
                    q = q_sb[:, d:d + 1, b * P:(b + 1) * P].broadcast_to([P, 8, P])
                    ins = dve.tensor_tensor(qdec[:, d], dec[:, d], q, ALU.mult)
                ins.then_inc(s_qd, 1)

            def masked(i, b, dst):
                dve.wait_ge(s_sc, 2 * i + b + 1)
                tmp = sq_a.rearrange("p a (l n) -> p (a l) n", l=2)
                dve.tensor_tensor(tmp, ps[:, 6:8, :].rearrange("p a (l n) -> p (a l) n", l=4),
                                  masks, ALU.mult).then_inc(s_msk, 1)
                dve.wait_ge(s_msk, 2 * i + b + 1)
                return dve.tensor_reduce(dst, tmp.rearrange("p l n -> p n l"), AX.X, ALU.add)

            def masked_second(i):
                masked(i, 1, att[:, S:3 * P])
                dve.tensor_copy(att[:, P:S], ps[:, 4, 0:P]).then_inc(s_att, 1)

            def values(i):
                g, cc = G_GLA + i * 6, C_GLA + i * 6
                for c in range(2):
                    sum_group(g + 2 + c, cc + 2 + c, c)
                    dve.wait_ge(s_read, g + 2 + c + 3)
                    for b in range(TB):
                        ins = dve.tensor_scalar(v_sb[:, b, c * HC:(c + 1) * HC], total[:, c, b, :],
                                                rstd[:, S + b:S + b + 1], None, ALU.mult)
                    ins.then_inc(s_v, 1)

            def output_gates(i):
                g, cc = G_GLA + i * 6, C_GLA + i * 6
                for c in range(2):
                    sum_group(g + 4 + c, cc + 4 + c, c)
                    dve.wait_ge(s_read, g + 4 + c + 3)
                    dve.tensor_tensor(r_sb[:, 2 * c:2 * c + 2, :], total[:, c], per_token(2),
                                      ALU.mult).then_inc(s_r, 1)

            def gating(h, i):
                lows(h, 2, 4)
                dve.wait_ge(s_tanh, i)
                dve.scalar_tensor_tensor(out=r_sb, in0=e_sb, scalar=1.0, in1=r_sb, op0=ALU.add,
                                         op1=ALU.mult).then_inc(s_silu, 1)
                dve.wait_ge(s_oroot, i)
                dve.reciprocal(rstd_o, root_o).then_inc(s_orstd, 1)
                dve.wait_ge(s_silu, i)
                dve.wait_ge(s_orstd, i)
                dve.tensor_tensor(r_sb, r_sb, per_token(4, rstd_o), ALU.mult).then_inc(s_scaled, 1)
                dve.wait_ge(s_scaled, i)
                dve.wait_ge(s_ocp, i + 1)
                dve.tensor_tensor(o_sb, o_sb, r_sb, ALU.mult).then_inc(s_full, 1)
                lows(h, 4, 6)
                dve.wait_ge(s_fullhi, i)
                head = xb[:, bass.ds(4 * i - 4, 4)]
                dve.tensor_tensor(head[:, :, 1, :], o_sb, head[:, :, 0, :].bitcast(F32),
                                  ALU.subtract).then_inc(s_gated, 1)

            lows(H_GLA, 4, 10)
            queries_keys(0)
            lows(H_GLA, 10, 12)
            gates()
            lows(H_GLA, 12, 14)
            split_gates()
            lows(H_GLA, 14, 18)
            values(0)
            lows(H_GLA, 18, 20)
            scaled_queries(0, 0)
            lows(H_GLA, 20, 23)
            masked(0, 0, att[:, 0:P]).then_inc(s_att, 1)
            scaled_queries(0, 1)
            lows(H_GLA, 23, 26)
            output_gates(0)
            masked_second(0)

            with dve.Fori(1, GH) as i:
                h = H_GLA + i * HEAD_HALVES
                gating(h, i)
                lows(h, 6, 10)
                queries_keys(i)
                scale_queries_keys(i)
                scaled_queries(i, 0)
                lows(h, 10, 16)
                masked(i, 0, att[:, 0:P]).then_inc(s_att, 1)
                lows(h, 16, 18)
                values(i)
                scaled_queries(i, 1)
                lows(h, 18, 22)
                masked_second(i)
                lows(h, 22, 26)
                output_gates(i)

            gating(H_OUT, GH)
            lows(H_OUT, 6, PANEL + 2)
            down(H_OUT, 0, R_OUT)
            down_panels(H_OUT, R_OUT, PANELS - 1, 1)
            last_panel(H_OUT + (PANELS - 1) * PANEL, PANELS - 1, R_OUT + 2 * (PANELS - 1), N_MLP0,
                       X_MLP0)
            mlp(H_MLP0, G_MLP0, 0, C_MLP0, R_MLP0, X_MLP0, N_MLP0, ST_MLP0,
                lambda h, r: last_panel(h, PANELS - 1, r, N_KVIN, X_KV))

            def queries_in(j):
                if j >= 5:
                    convert(resid, N_MIX1, xb, X_Q, 4 * (j - 5), min(4 * (j - 5) + 4, KT))

            first_panel(H_DKV, N_KVIN, X_KV, queries_in)
            factors(ST_MIX1, columns=True)

            def latent(g, cc, n):
                for c in range(2):
                    sum_group(g + c, cc + c, c)
                    dve.wait_ge(s_read, g + c + 3)
                    dve.tensor_tensor(lat[:, 2 * c:2 * c + 2, :], total[:, c], per_token(2),
                                      ALU.mult).then_inc(s_lat, 1)
                    dve.wait_ge(s_lat, n + c + 1)

            def normed(st, gain, dst, x0, n):
                factors(st, dst=rstd_c)
                for c in range(LT):
                    ins = dve.scalar_tensor_tensor(out=lat[:, c, :], in0=lat[:, c, :],
                                                   scalar=gains[:, gain + c:gain + c + 1],
                                                   in1=rstd_c, op0=ALU.mult, op1=ALU.mult)
                ins.then_inc(s_laty, 1)
                dve.wait_ge(s_laty, n)
                for c in range(LT):
                    dve.wait_ge(s_xhi, x0 + c + 1)
                    dve.tensor_tensor(dst[:, c, 1, :], lat[:, c, :], dst[:, c, 0, :].bitcast(F32),
                                      ALU.subtract).then_inc(s_x, 1)

            latent(G_DKV, C_DKV, 0)
            dve.wait_ge(s_sidehi, 2)
            dve.tensor_tensor(side1[:, 1, :], side_in1, side1[:, 0, :].bitcast(F32), ALU.subtract)\
                .then_inc(s_sidelo, 1)
            lows(H_DQ, 2, 8)
            normed(ST_C, N_C, xc, X_C, 1)
            lows(H_DQ, 8, PANEL + 2)
            dve.wait_ge(s_x, X_C + LT)
            latent(G_DQ, C_DQ, 2)
            dve.wait_ge(s_low, 2)
            step(dve.tensor_copy(kr_tmp, ps[:, 4:6, ROPE:2 * ROPE]))
            step(dve.tensor_tensor(kr_tmp, ps[:, 4:6, 0:ROPE], kr_tmp, ALU.add))
            for b in range(TB):
                for n in range(2):
                    ins = dve.tensor_scalar(kr_nat[:, b, n * ROPE:(n + 1) * ROPE], kr_tmp[:, b, :],
                                            rstd[:, S + b:S + b + 1], None, ALU.mult)
            ins.then_inc(s_krn, 1)
            dve.wait_ge(s_freqs, 16)
            dve.wait_ge(s_pos, 16)
            step(dve.tensor_copy(ang, pos_i))
            step(dve.tensor_scalar(ang, ang, freqs[:, 0:1], None, ALU.mult))
            step(dve.tensor_scalar(turns, ang, 1.0 / (2.0 * np.pi), ROUND, ALU.mult, ALU.add))
            step(dve.tensor_scalar(turns, turns, ROUND, None, ALU.subtract))
            for part in TWO_PI:
                step(dve.scalar_tensor_tensor(out=ang, in0=turns, scalar=-part, in1=ang,
                                              op0=ALU.mult, op1=ALU.add))
            step(dve.tensor_scalar(sin, ang, float(np.float32(np.pi)), -float(np.float32(np.pi)),
                                   ALU.min, ALU.max))
            step(dve.scalar_tensor_tensor(out=cos, in0=sin, scalar=-1.0, in1=sin, op0=ALU.mult,
                                          op1=ALU.max))
            dve.tensor_scalar(cos, cos, -1.0, float(np.pi / 2), ALU.mult, ALU.add)\
                .then_inc(s_ang, 2)
            normed(ST_CQ, N_CQ, xq, X_CQ, 2)
            dve.wait_ge(s_krt, 1)
            dve.tensor_copy(raw_r, ps[:, 6, 0:S]).then_inc(s_krc, 1)
            dve.wait_ge(s_trig, 2)
            dve.wait_ge(s_krc, 1)
            step(dve.tensor_tensor(cos_r, raw_r, cos, ALU.mult))
            dve.wait_ge(s_krot, 1)
            step(dve.tensor_tensor(sin_r, ps[:, 7, 0:S], sin, ALU.mult))
            dve.wait_ge(s_krz, 1)
            for n in range(2):
                rows = slice(n * ROPE, (n + 1) * ROPE)
                dve.tensor_tensor(keys_r[rows, n, :], cos_r[rows, :], sin_r[rows, :], ALU.add)\
                    .then_inc(s_keysr, 1)
            dve.wait_ge(s_keysr, 2)
            dve.wait_ge(s_causal, 16)

            def slot(i, b, proj=True, attn=True):
                h, g, cc = H_PAIR + i * 4, G_PAIR + i * 4, C_PAIR + i * 4
                if proj:
                    low(h, 2)
                    sum_group(g, cc, 0, dst=kt_sb[:, b])
                if attn:
                    dve.wait_ge(s_dots, i)
                    mask = causal.rearrange("p (o n) -> p o n", o=1).broadcast_to([P, 2, 3 * P])
                    dve.tensor_tensor(sc_sb, ps[:, 4:6, 0:3 * P], mask, ALU.add).then_inc(s_ms, 1)
                    dve.wait_ge(s_ms, i)
                    dve.tensor_reduce(mx[:, 0:2], sc_sb[:, :, 0:P], AX.X, ALU.max)
                    dve.tensor_reduce(mx[:, 2:4], sc_sb[:, :, P:3 * P], AX.X, ALU.max)\
                        .then_inc(s_max, 1)
                    dve.wait_ge(s_max, i)
                    dve.tensor_scalar(nmx, mx, -MLA_SCALE, None, ALU.mult).then_inc(s_nmx, 1)
                if proj:
                    low(h, 3, n=HF // 2)
                    sum_group(g + 1, cc + 1, 1, dst=vt_sb[:, b])
                    low(h, 4)
                if attn:
                    dve.wait_ge(s_exp, i)
                    dve.wait_ge(s_pr, i)
                    dve.reciprocal(rden, den).then_inc(s_rden, 1)
                if proj:
                    sum_group(g + 2, cc + 2, 0, dst=qn_sb[:, b])
                    low(h, 5)
                    dve.wait_ge(s_qr, i)
                    sum_group(g + 3, cc + 3, 1, dst=raw_r.rearrange("p (o s) -> p o s", o=1),
                              banks=1)
                    dve.wait_ge(s_read, g + 3 + 3)
                    dve.sem_inc(s_raw, 1)
                if attn:
                    dve.wait_ge(s_ohi, i)
                    pair = xb[:, bass.ds(2 * i - 2, 2)]
                    dve.tensor_tensor(pair[:, :, 1, :],
                                      ps[:, 6, :].rearrange("p (h s) -> p h s", h=2),
                                      pair[:, :, 0, :].bitcast(F32), ALU.subtract).then_inc(s_ox, 1)
                if proj:
                    dve.wait_ge(s_rot, i + 1)
                    dve.tensor_tensor(sin_r, ps[:, 7, 0:S], sin, ALU.mult).then_inc(s_sinr, 1)

            slot(0, 0, attn=False)
            with dve.Fori(0, PAIRS // 2 - 1) as m:
                slot(m * 2 + 1, 1)
                slot(m * 2 + 2, 0)
            slot(PAIRS - 1, 1)
            slot(PAIRS, 0, proj=False)

            down_panels(H_WO, R_WO, PANELS - 1)
            last_panel(H_WO + (PANELS - 1) * PANEL, PANELS - 1, R_WO + 2 * (PANELS - 1), N_MLP1,
                       X_MLP1)

            def end(h, r):
                lows(h, 2, PANEL)
                down(h, PANELS - 1, r)

            mlp(H_MLP1, G_MLP1, UP_GROUPS, C_MLP1, R_MLP1, X_MLP1, N_MLP1, ST_MLP1, end)
            dve.wait_ge(s_root, ST_FIN + 1)
            dve.reciprocal(rstd[:, S:S + TB], root[:, S:S + TB]).then_inc(s_rstd, 1)
            dve.wait_ge(s_rstd, ST_FIN + 1)
            for n in range(8):
                b, c = n // 4, n % 4
                dve.wait_ge(s_fin, n + 1)
                dve.tensor_scalar(o_nat[:, b, c * 512:(c + 1) * 512], ps[:, n, :],
                                  rstd[:, S + b:S + b + 1], None, ALU.mult).then_inc(s_finc, 1)


_INS = ["x", "positions", "norm_mix", "norm_mlp", "gla_w_in", "gla_w_gate_up", "gla_b_gate",
        "gla_norm", "gla_w_out", "kv_norm_in", "mla_w_dkv", "mla_kv_norm", "mla_w_uk", "mla_w_uv",
        "mla_w_dq", "mla_q_norm", "mla_w_uq", "mla_w_o", "mlp_w1", "mlp_w2", "final_norm"]


def kernel(**inputs):
    import concourse.bacc as bacc
    from concourse.bass_utils import run_bass_kernel_spmd

    nc = bacc.Bacc("TRN2", target_bir_lowering=False, num_devices=1)
    arrays, tensors = {}, {}
    given = {name: inputs[name] for name in _INS}
    for name, a in (*given.items(), *constants().items()):
        a = np.ascontiguousarray(a)
        arrays[f"in_{name}"] = a
        tensors[name] = nc.dram_tensor(f"in_{name}", a.shape, mybir.dt.from_np(a.dtype),
                                       kind="ExternalInput").ap()
    out = nc.dram_tensor("out", (1, S, D), F32, kind="ExternalOutput").ap()
    build(nc, tensors, out)
    return run_bass_kernel_spmd(nc, [arrays], core_ids=[0]).results[0]["out"]
```

```python
from contextlib import ExitStack

import numpy as np

import concourse.bass as bass
from concourse import mybir

F32 = mybir.dt.float32
F32R = mybir.dt.float32r
I32 = mybir.dt.int32
ALU = mybir.AluOpType
ACT = mybir.ActivationFunctionType
AX = mybir.AxisListType

P = 128
S = 256
TB = S // P
D = 2048
KT = D // P
EPS = 1e-6

GH = 4
GK = D // 2
HK = GK // GH
HV = D // GH
RANK = 16
TAU = 16.0
LEVELS = [64, 32, 16, 8, 4, 2, 1]

MH = 16
LORA = 512
LT = LORA // P
NOPE = 128
ROPE = 64
QH = NOPE + ROPE
PAIRS = MH // 2
THETA = 10000.0
MLA_SCALE = float(QH) ** -0.5
MASKED = -1e30

D_FF = 4 * D
SLAB = 2048
SLABS = D_FF // SLAB

ROUND = 1.5 * 2.0 ** 23
TWO_PI = [6.28125, 0.0019350051879882812, 2.0 * np.pi - 6.28125 - 0.0019350051879882812]

HC = 256
HK4 = 4
HF = HK4 * HC
RING = 4
UNITS = KT // HK4
PANEL = 2 * UNITS
PANELS = D // (2 * HC)
HEAD_HALVES = 3 * PANEL
H_GLA, G_GLA = 0, 0
H_OUT, G_OUT = H_GLA + GH * HEAD_HALVES, G_GLA + GH * 6
H_MLP0, G_MLP0 = H_OUT + PANELS * PANEL, G_OUT + PANELS * 2
SLAB_HALVES, SLAB_GROUPS = 2 * PANELS * PANEL, 4 * PANELS
H_DKV, G_DKV = H_MLP0 + SLABS * SLAB_HALVES, G_MLP0 + SLABS * SLAB_GROUPS
H_DQ, G_DQ = H_DKV + PANEL, G_DKV + 2
H_PAIR, G_PAIR = H_DQ + PANEL, G_DQ + 2
H_WO, G_WO = H_PAIR + PAIRS * 4, G_PAIR + PAIRS * 4
H_MLP1, G_MLP1 = H_WO + PANELS * PANEL, G_WO + PANELS * 2
H_END, G_END = H_MLP1 + SLABS * SLAB_HALVES, G_MLP1 + SLABS * SLAB_GROUPS
C_GLA = 0
C_MLP0 = C_GLA + GH * 6
UP_GROUPS = SLABS * PANELS * 2
C_DKV = C_MLP0 + UP_GROUPS
C_DQ = C_DKV + 2
C_PAIR = C_DQ + 2
C_MLP1 = C_PAIR + PAIRS * 4
X_GLA, X_MLP0, X_KV, X_Q, X_C, X_CQ, X_MLP1 = 0, 16, 32, 48, 64, 68, 72
N_MIX0, N_MIX1, N_MLP0, N_MLP1, N_KVIN, N_FIN, N_GLA, N_C, N_CQ = 0, 16, 32, 48, 64, 80, 96, 100, 104
N_GAINS = 108
R_OUT, R_MLP0 = 0, 2 * PANELS
R_WO = R_MLP0 + SLABS * PANELS * 2
R_MLP1 = R_WO + 2 * PANELS
(ST_MIX0, ST_MLP0, ST_MIX1, ST_C, ST_CQ, ST_MLP1, ST_FIN) = range(7)
PLACES = [[0, 1, 2, 3, 5, 6, 7], [0, 1, 2, 3, 4, 5, 6]]
SUFFIX, PREFIX = 4, 7


RESULT = [(0, 0, 4), (0, 1, 5), (0, 2, 6), (1, 0, 0), (1, 1, 1), (1, 2, 2), (0, 3, 3), (1, 3, 4)]


def constants():
    s, t = np.arange(P)[:, None], np.arange(P)[None, :]
    sums = {}
    masks = []
    for m in LEVELS:
        mid = (t // (2 * m)) * 2 * m + m
        upper = (t % (2 * m)) >= m
        sums[m] = np.where(upper, (s >= mid) & (s <= t), (s > t) & (s < mid))
        same = (s // (2 * m)) == (t // (2 * m))
        masks.append(same & ((t % (2 * m)) >= m) & ((s % (2 * m)) < m))
    masks.append(s == t)
    suffix, prefix = s > t, s <= t
    order = [sums[m] for m in LEVELS[:4]] + [suffix] + [sums[m] for m in LEVELS[4:]] + [prefix]
    rot = np.zeros((P, P))
    half = ROPE // 2
    for b in range(0, P, ROPE):
        for d in range(half):
            rot[b + d + half, b + d] = -1.0
            rot[b + d, b + d + half] = 1.0
    causal = np.zeros((P, 3 * P))
    later = np.where(t > s, MASKED, 0.0)
    causal[:, 0:P] = later
    causal[:, 2 * P:] = later
    freqs = (THETA ** (-np.arange(0, ROPE, 2, dtype=np.float64) / ROPE)).astype(np.float32)
    pad = np.zeros((P, P))
    pad[:, RANK] = 1.0
    return {
        "c_sums": np.stack(order, 1).reshape(P, 9 * P).astype(np.float32),
        "c_masks": np.stack(masks, 1).reshape(P, 8 * P).astype(np.float32),
        "c_ident": np.eye(P, dtype=np.float32),
        "c_rot": rot.astype(np.float32),
        "c_causal": causal.astype(np.float32),
        "c_freqs": np.tile(freqs, P // half)[:, None].copy(),
        "c_bias_row": pad.astype(np.float32),
    }


def build(nc, t, out):
    ctx = ExitStack()
    with ctx:
        def sb(name, shape, dt=F32):
            return ctx.enter_context(nc.sbuf_tensor(name, shape, dt))

        def sem(name):
            return ctx.enter_context(nc.semaphore(name))

        resid = sb("resid", [P, KT, S])
        xa = sb("xa", [P, KT, 2, S], F32R)
        xb = sb("xb", [P, KT, 2, S], F32R)
        stage = sb("stage", [P, RING, HF])
        wts = sb("wts", [P, RING, HK4, 2, HC], F32R)
        temps = sb("temps", [P, 16 * S])
        sqs = sb("sqs", [P, S + TB])
        rstd = sb("rstd", [P, S + TB])
        ident = sb("ident", [P, P])
        ones = sb("ones", [P, P])
        gains = sb("gains", [P, N_GAINS])
        eps = sb("eps", [P, 2])
        scratch = sb("scratch", [P, 11136])
        scratch_r = sb("scratch_r", [P, 4096], F32R)

        def carve(tensor, at=0):
            end = [at]

            def take(*dims):
                n = int(np.prod(dims))
                v = tensor[:, end[0]:end[0] + n]
                end[0] += n
                assert end[0] <= tensor.shape[1]
                if len(dims) == 1:
                    return v
                names = "abcd"[:len(dims)]
                return v.rearrange(f"p ({' '.join(names)}) -> p {' '.join(names)}",
                                   **dict(zip(names, dims)))

            return take

        root = sqs
        take = carve(temps)
        corr, total = take(2, 2, S), take(2, 2, S)
        sq_a, sq_b = take(4, S), take(4, S)
        x_nat = temps[:, :].rearrange("p (b d) -> p b d", b=TB)

        take = carve(scratch)
        dec = take(2, 8, P)
        qdec = take(2, 8, P)
        q_sb, k_sb = take(2, S), take(2, S)
        v_sb = take(TB, HV)
        r_sb, e_sb, o_sb = take(4, S), take(4, S), take(4, S)
        masks = take(8, P)
        kx = take(2, P)
        att = take(3 * P)
        rstd_o, root_o = take(S), root[:, 0:S]
        w_up = scratch[:, 0:GK]
        z_sb = scratch[:, 2048:2048 + TB * GK]
        g_sb = scratch[:, 0:TB * GK]
        sums_in = scratch[:, 4096:4096 + 9 * P]
        low_nat = r_sb[:, 0, :].rearrange("p (b c) -> p b c", b=TB)
        low_t = r_sb[:, 1, :]
        side_in0 = r_sb[:, 2, :]
        low_tmp = r_sb[:, 3, :]
        gains_in = e_sb[:, 0, 0:P]
        take = carve(scratch_r)
        gate = take(TB, 2, HK)
        sums = take(9, P)
        side0 = take(2, KT * RANK)

        take = carve(scratch)
        kt_sb, vt_sb = take(2, 2, S), take(2, TB, S)
        cos, sin = take(S), take(S)
        causal = take(3 * P)
        rot = take(P)
        lat = take(LT, S)
        keys_r = take(2, S)
        qn_sb = take(2, 2, S)
        qr_sb = take(2, S)
        raw_r, cos_r, sin_r = take(S), take(S), take(S)
        sc_sb, pr_sb, pt_sb = take(2, 3 * P), take(2, 3 * P), take(2, 3 * P)
        mx, nmx, den, rden = take(4), take(4), take(4), take(4)
        freqs = take(2)
        rstd_c = take(S)
        side_in1 = take(KT * ROPE)
        kr_nat = sc_sb[:, 0, 0:TB * P].rearrange("p (b c) -> p b c", b=TB)
        kr_tmp = pr_sb[:, 0, 0:TB * ROPE].rearrange("p (b c) -> p b c", b=TB)
        ang, turns, pos_i = pt_sb[:, 0, 0:S], pt_sb[:, 1, 0:S], cos.bitcast(I32)
        take = carve(scratch_r)
        xc, xq = take(LT, 2, S), take(LT, 2, S)
        side1 = scratch_r[:, 2048:4096].rearrange("p (h n) -> p h n", h=2)

        take = carve(scratch)
        act, sq_h = take(2, 2, S), take(2, 2, S)
        o_nat = take(TB, D)
        y_sb = scratch[:, 6144:6144 + KT * S].rearrange("p (t s) -> p t s", t=KT)

        ps = ctx.enter_context(nc.psum_tensor("ps", [P, 8, 512], F32))

        s_ident, s_xin = sem("s_ident"), [sem(f"s_xin{i}") for i in range(4)]
        s_gin, s_side0, s_up, s_masks, s_sums = (
            sem(n) for n in ("s_gin", "s_side0", "s_up", "s_masks", "s_sums"))
        s_side1, s_causal, s_rotm, s_freqs, s_pos = (
            sem(n) for n in ("s_side1", "s_causal", "s_rotm", "s_freqs", "s_pos"))
        s_landed = [sem(f"s_landed{i}") for i in range(RING)]
        s_high = sem("s_high")
        s_split = sem("s_split")
        s_mult = sem("s_mult")
        s_read = sem("s_read")
        s_corr = sem("s_corr")
        s_main = sem("s_main")
        s_xhi, s_x = sem("s_xhi"), sem("s_x")
        s_sqs = sem("s_sqs")
        s_stat = sem("s_stat")
        s_root = sem("s_root")
        s_rstd = sem("s_rstd")
        s_act, s_acthi, s_acts = sem("s_act"), sem("s_acthi"), sem("s_acts")
        s_hid = sem("s_hid")
        s_dve, s_pool = sem("s_dve"), sem("s_pool")
        s_ones, s_eps, s_pad, s_tr, s_trc, s_gtr, s_gains = (
            sem(n) for n in ("s_ones", "s_eps", "s_pad", "s_tr", "s_trc", "s_gtr", "s_gains"))
        s_sidehi, s_sidelo, s_low, s_lownat, s_lowt, s_lowtc = (
            sem(n) for n in ("s_sidehi", "s_sidelo", "s_low", "s_lownat", "s_lowt", "s_lowtc"))
        s_z, s_zact, s_g, s_ghi, s_glo, s_sumsr = (
            sem(n) for n in ("s_z", "s_zact", "s_g", "s_ghi", "s_glo", "s_sumsr"))
        s_y, s_ysq, s_fin, s_out = (sem(n) for n in ("s_y", "s_ysq", "s_fin", "s_out"))
        s_finc = [sem("s_finc0"), sem("s_finc1")]
        s_gcur = sem("s_gcur")
        s_sum = sem("s_sum")
        s_dec = sem("s_dec")
        s_q, s_k, s_r = sem("s_q"), sem("s_k"), sem("s_r")
        s_v = sem("s_v")
        s_qd, s_kd = sem("s_qd"), sem("s_kd")
        s_kx = sem("s_kx")
        s_sc = sem("s_sc")
        s_msk = sem("s_msk")
        s_att = sem("s_att")
        s_o, s_osq, s_ocp, s_ost, s_oroot, s_orstd = (
            sem(n) for n in ("s_o", "s_osq", "s_ocp", "s_ost", "s_oroot", "s_orstd"))
        s_tanh, s_silu, s_scaled, s_full, s_fullhi = (
            sem(n) for n in ("s_tanh", "s_silu", "s_scaled", "s_full", "s_fullhi"))
        s_gated = sem("s_gated")
        s_lat, s_latsq, s_laty, s_krn, s_krt, s_krc, s_krot, s_krz = (
            sem(n) for n in ("s_lat", "s_latsq", "s_laty", "s_krn", "s_krt", "s_krc", "s_krot",
                              "s_krz"))
        s_ang, s_trig, s_keysr = sem("s_ang"), sem("s_trig"), sem("s_keysr")
        s_raw, s_rot, s_cosr, s_sinr, s_qr = (
            sem(n) for n in ("s_raw", "s_rot", "s_cosr", "s_sinr", "s_qr"))
        s_dots, s_ms, s_max, s_nmx, s_exp, s_rden, s_pr = (
            sem(n) for n in ("s_dots", "s_ms", "s_max", "s_nmx", "s_exp", "s_rden", "s_pr"))
        s_pt, s_ptc, s_ov, s_ohi, s_ox = (
            sem(n) for n in ("s_pt", "s_ptc", "s_ov", "s_ohi", "s_ox"))

        def by_chunk(w):
            return w.rearrange("(t p) n -> p t n", p=P)

        w_in, w_out = by_chunk(t["gla_w_in"][0]), by_chunk(t["gla_w_out"][0])
        w1 = [by_chunk(t["mlp_w1"][i]) for i in range(2)]
        w2 = [by_chunk(t["mlp_w2"][i]) for i in range(2)]
        w_dkv, w_dq = by_chunk(t["mla_w_dkv"]), by_chunk(t["mla_w_dq"][0])
        w_uk, w_uv, w_o = by_chunk(t["mla_w_uk"]), by_chunk(t["mla_w_uv"]), by_chunk(t["mla_w_o"][0])
        w_uq = t["mla_w_uq"][0].rearrange("(t p) (h c) -> p t h c", p=P, c=QH)
        x_dram = t["x"][0].rearrange("(b p) d -> p b d", p=P)
        out_dram = out[0].rearrange("(b p) d -> p b d", p=P)

        block = ctx.enter_context(nc.Block())

        @block.sync
        def _(sp):
            def load(h, j, src, n=HF):
                slot = j % RING
                sp.wait_ge(s_split, h + j + 1)
                dst = stage[:, slot, 0:n]
                if len(src.shape) == 3:
                    dst = dst.rearrange("p (t n) -> p t n", t=src.shape[1])
                    sp.dma_start(dst, src).then_inc(s_landed[slot], 16)
                else:
                    dst = dst.rearrange("p (t h n) -> p t h n", t=src.shape[1], h=src.shape[2])
                    for hd in range(2):
                        sp.dma_start(dst[:, :, hd], src[:, :, hd]).then_inc(s_landed[slot], 16)

            def panel(h, w, row, col0, col1):
                for u in range(UNITS):
                    for c, col in enumerate((col0, col1)):
                        load(h, 2 * u + c, w[:, bass.ds(row + HK4 * u, HK4), bass.ds(col, HC)])

            def plain_panels(h, w):
                with sp.Fori(0, PANELS) as p:
                    panel(h + p * PANEL, w, 0, p * 2 * HC, p * 2 * HC + HC)

            def mlp(layer, h0):
                with sp.Fori(0, SLABS) as s:
                    h = h0 + s * SLAB_HALVES
                    with sp.Fori(0, PANELS) as p:
                        col = s * SLAB + p * 2 * HC
                        panel(h + p * PANEL, w1[layer], 0, col, col + HC)
                    with sp.Fori(0, PANELS) as p:
                        panel(h + PANELS * PANEL + p * PANEL, w2[layer], s * KT,
                              p * 2 * HC, p * 2 * HC + HC)

            with sp.Fori(0, GH) as i:
                h = H_GLA + i * HEAD_HALVES
                panel(h, w_in, 0, i * HK, GK + i * HK)
                v0 = 2 * GK + i * HV
                panel(h + PANEL, w_in, 0, v0, v0 + HC)
                r0 = 2 * GK + D + i * HV
                panel(h + 2 * PANEL, w_in, 0, r0, r0 + HC)
            plain_panels(H_OUT, w_out)
            sp.wait_ge(s_gated, GH)
            sp.dma_start(side_in1.rearrange("p (t n) -> p t n", t=KT),
                         w_dkv[:, :, LORA:LORA + ROPE]).then_inc(s_side1, 16)
            sp.dma_start(causal, t["c_causal"]).then_inc(s_causal, 16)
            sp.dma_start(rot, t["c_rot"]).then_inc(s_rotm, 16)
            sp.dma_start(freqs[:, 0:1], t["c_freqs"]).then_inc(s_freqs, 16)
            sp.dma_start(pos_i, t["positions"][0:1, :].broadcast_to([P, S])).then_inc(s_pos, 16)
            mlp(0, H_MLP0)
            panel(H_DKV, w_dkv, 0, 0, HC)
            panel(H_DQ, w_dq, 0, 0, HC)
            with sp.Fori(0, PAIRS) as i:
                h = H_PAIR + i * 4
                load(h, 0, w_uk[:, :, bass.ds(i * HC, HC)])
                load(h, 1, w_uv[:, :, bass.ds(i * HC, HC)])
                load(h, 2, w_uq[:, :, bass.ds(i * 2, 2), 0:NOPE])
                load(h, 3, w_uq[:, :, bass.ds(i * 2, 2), NOPE:QH], n=HF // 2)
            plain_panels(H_WO, w_o)
            mlp(1, H_MLP1)
            for n, (b, c, _) in enumerate(RESULT):
                sp.wait_ge(s_finc[n % 2], n // 2 + 1)
                sp.dma_start(out_dram[:, b, c * 512:(c + 1) * 512],
                             o_nat[:, b, c * 512:(c + 1) * 512]).then_inc(s_out, 16)
            sp.wait_ge(s_out, 8 * 16)

        @block.gpsimd
        def _(pool):
            steps = [0]

            def step(ins):
                steps[0] += 1
                ins.then_inc(s_pool, 1)
                pool.wait_ge(s_pool, steps[0])

            def squares(st, src, chunks, ready=None):
                for c in range(0, chunks, 4):
                    if ready:
                        ready(c)
                    part = src[:, c:c + 4, :]
                    step(pool.tensor_tensor(sq_b if c else sq_a, part, part, ALU.mult))
                    if c:
                        step(pool.tensor_tensor(sq_a, sq_a, sq_b, ALU.add))
                step(pool.tensor_tensor(sq_a[:, 0:2, :], sq_a[:, 0:2, :], sq_a[:, 2:4, :], ALU.add))
                if st:
                    pool.wait_ge(s_rstd, st)
                pool.tensor_tensor(sqs[:, 0:S], sq_a[:, 0, :], sq_a[:, 1, :], ALU.add)\
                    .then_inc(s_sqs, 1)

            def final(g):
                return lambda c: pool.wait_ge(s_read, g + c // 2 + 2 + 2)

            def mlp(k0):
                with pool.Fori(0, SLABS) as s:
                    with pool.Fori(0, PANELS) as p:
                        for c in range(2):
                            k = k0 + s * (PANELS * 2) + p * 2 + c
                            pool.wait_ge(s_act, k + 1)
                            pool.wait_ge(s_hid, k + 1)
                            pool.tensor_tensor(sq_h[:, c], act[:, c], act[:, c], ALU.mult)\
                                .then_inc(s_acts, 1)
                            pool.wait_ge(s_acts, k + 1)
                            pool.wait_ge(s_acthi, k + 1)
                            hid = xb[:, bass.ds(p * 4 + 2 * c, 2)]
                            pool.tensor_tensor(hid[:, :, 1, :], sq_h[:, c],
                                               hid[:, :, 0, :].bitcast(F32), ALU.subtract)\
                                .then_inc(s_hid, 1)

            pool.sem_inc(s_hid, 2)
            pool.sem_inc(s_pr, 1)
            for n in range(2):
                pool.memset(eps[:, n:n + 1], (1.0, 4.0)[n] * EPS).then_inc(s_eps, 1)
            pool.memset(ones[:, :], 1.0).then_inc(s_ones, 1)
            step(pool.memset(low_nat, 0.0))
            step(pool.memset(low_nat[:, :, RANK:RANK + 1], 1.0))
            pool.memset(w_up, 0.0).then_inc(s_pad, 1)
            pool.wait_ge(s_trc, 8)
            squares(ST_MIX0, resid, KT)

            with pool.Fori(0, GH) as i:
                for b in range(TB):
                    pool.wait_ge(s_dec, 4 * i + 2 * b + 3)
                    pool.wait_ge(s_k, i + 1)
                    if b == 0:
                        pool.tensor_tensor(kx, dec[:, :, SUFFIX, :], k_sb[:, :, 0:P], ALU.mult)\
                            .then_inc(s_kx, 1)
                        pool.wait_ge(s_kx, i + 1)
                    pool.wait_ge(s_qd, 4 * i + 2 * b + 1)
                    keys = k_sb[:, 0:1, b * P:(b + 1) * P].broadcast_to([P, 8, P])
                    pool.tensor_tensor(dec[:, 0], dec[:, 0], keys, ALU.mult).then_inc(s_kd, 1)

            squares(ST_MLP0, resid, KT, final(G_OUT))
            mlp(0)
            squares(ST_MIX1, resid, KT, final(G_DKV - 2 * PANELS))
            pool.memset(keys_r, 0.0).then_inc(s_krz, 1)
            for n in range(4):
                pool.wait_ge(s_lat, n + 1)
                if n == 2:
                    pool.wait_ge(s_stat, ST_C + 1)
                two = slice(2 * (n % 2), 2 * (n % 2) + 2)
                pool.tensor_tensor(sq_a[:, two, :], lat[:, two, :], lat[:, two, :], ALU.mult)\
                    .then_inc(s_latsq, 1)
            pool.sem_inc(s_sqs, 2)

            def normalised(i):
                pool.wait_ge(s_rden, i + 1)
                for h in range(2):
                    for blk in range(2):
                        part = pr_sb[:, h, 0:P] if blk == 0 else pr_sb[:, h, P:3 * P]
                        col = 2 * blk + h
                        by = rden[:, col:col + 1].broadcast_to(list(part.shape))
                        ins = pool.tensor_tensor(part, part, by, ALU.mult)
                ins.then_inc(s_pr, 1)

            def rotary_queries(i, b):
                pool.wait_ge(s_raw, i + 1)
                if not isinstance(i, int) or i:
                    pool.wait_ge(s_qr, i)
                pool.tensor_tensor(cos_r, raw_r, cos, ALU.mult).then_inc(s_cosr, 1)
                pool.wait_ge(s_cosr, i + 1)
                pool.wait_ge(s_sinr, i + 1)
                pool.tensor_tensor(qr_sb[:, b, :], cos_r, sin_r, ALU.add).then_inc(s_qr, 1)

            rotary_queries(0, 0)
            with pool.Fori(0, PAIRS // 2 - 1) as m:
                for b in range(2):
                    normalised(m * 2 + b)
                    rotary_queries(m * 2 + (b + 1), 1 - b)
            normalised(PAIRS - 2)
            rotary_queries(PAIRS - 1, 1)
            normalised(PAIRS - 1)

            squares(ST_MLP1, resid, KT, final(G_WO))
            mlp(UP_GROUPS)
            squares(ST_FIN, resid, KT - 4, final(G_END - 2 * PANELS))

        @block.scalar
        def _(act_e):
            sc = act_e

            pair_loads = [0]

            def high(h, j, n=HF, pairs=None):
                slot = j % RING
                more = 16 * (pair_loads[0] if pairs is None else pairs) if slot >= 2 else 0
                sc.wait_ge(s_landed[slot], h * (16 // RING) + (16 * (j // RING + 1) + more))
                sc.wait_ge(s_mult, h + j + 1)
                src = stage[:, slot, 0:n].rearrange("p (t n) -> p t n", n=HC)
                sc.activation(wts[:, slot, 0:n // HC, 0, :], src, ACT.Copy).then_inc(s_high, 1)

            def copy_corr(h, j, c, banks=2):
                sc.wait_ge(s_mult, h + j + 1 + RING)
                sc.activation(corr[:, c, 0:banks, :], ps[:, 2 * c:2 * c + banks, S:2 * S], ACT.Copy)\
                    .then_inc(s_corr, 1)

            def convert(src, gain, dst, c0, c1):
                for c in range(c0, c1):
                    sc.activation(dst[:, c, 0, :], src[:, c, :], ACT.Copy,
                                  scale=gains[:, gain + c:gain + c + 1]).then_inc(s_xhi, 1)

            def last_panel(h, g, gain, start=4):
                for j in range(4, PANEL + 4):
                    if j >= start:
                        high(h, j)
                    if j < PANEL + 2:
                        c = 2 * (j - 4)
                        sc.wait_ge(s_read, g + c // 2 + 1 + 2)
                        convert(resid, gain, xa, c, c + 2)

            def take_root(st, features, columns=False):
                sc.wait_ge(s_stat, st + 1)
                if st:
                    sc.wait_ge(s_rstd, st)
                n = S + TB if columns else S
                sc.activation(root[:, 0:n], ps[:, 7, 0:n], ACT.Sqrt, scale=1.0 / features,
                              bias=eps[:, 0:1]).then_inc(s_root, 1)

            def first_panel(h, g, gain, st, columns=False, more=None):
                for n in range(2):
                    c = KT - 4 + 2 * n
                    sc.wait_ge(s_read, g - 2 + n + 1 + 2)
                    convert(resid, gain, xa, c, c + 2)
                for j in range(4, PANEL + 2):
                    high(h, j)
                    if more:
                        more(j)
                    if j == 8:
                        take_root(st, D, columns)

            def highs(h, j0, j1):
                for j in range(j0, j1):
                    high(h, j)

            def up_tail(h, p, k):
                for c in range(2):
                    copy_corr(h, PANEL - 2 + c, c)
                    high(h, PANEL + 2 + c)
                    sc.wait_ge(s_act, k + c + 1)
                    hid = xb[:, bass.ds(p * 4 + 2 * c, 2), 0, :]
                    sc.activation(hid, act[:, c], ACT.Square).then_inc(s_acthi, 1)

            def up(h, p, k):
                highs(h, 4, PANEL + 2)
                up_tail(h, p, k)

            def mlp(h0, g0, k0, gain, st, end):
                first_panel(h0, g0, gain, st)
                up_tail(h0, 0, k0)
                with sc.Fori(1, PANELS) as p:
                    up(h0 + p * PANEL, p, k0 + p * 2)
                with sc.Fori(PANELS, 2 * PANELS) as p:
                    highs(h0 + p * PANEL, 4, PANEL + 4)
                with sc.Fori(1, SLABS - 1) as s:
                    h = h0 + s * SLAB_HALVES
                    k = k0 + s * (2 * PANELS)
                    with sc.Fori(0, PANELS) as p:
                        up(h + p * PANEL, p, k + p * 2)
                    with sc.Fori(PANELS, 2 * PANELS) as p:
                        highs(h + p * PANEL, 4, PANEL + 4)
                h = h0 + (SLABS - 1) * SLAB_HALVES
                k = k0 + (SLABS - 1) * (2 * PANELS)
                with sc.Fori(0, PANELS) as p:
                    up(h + p * PANEL, p, k + p * 2)
                with sc.Fori(PANELS, 2 * PANELS - 1) as p:
                    highs(h + p * PANEL, 4, PANEL + 4)
                end(h + (2 * PANELS - 1) * PANEL, g0 + SLABS * SLAB_GROUPS - 2 * PANELS)

            for free in (s_dec, s_ocp, s_ptc):
                sc.sem_inc(free, 1)
            sc.dma_start(ident[:, :], t["c_ident"]).then_inc(s_ident, 16)

            def x_in(n):
                cols = slice(n * 512, (n + 1) * 512)
                sc.dma_start(x_nat[:, :, cols], x_dram[:, :, cols]).then_inc(s_xin[n], 16)

            x_in(0)
            row = 0
            for w in (t["norm_mix"], t["norm_mlp"], t["kv_norm_in"], t["final_norm"], t["gla_norm"],
                      t["mla_kv_norm"], t["mla_q_norm"]):
                flat = w if len(w.shape) == 1 else w.rearrange("a b -> (a b)")
                n = flat.shape[0] // P
                sc.dma_start(gains_in[row:row + n, :], flat.rearrange("(r c) -> r c", c=P))\
                    .then_inc(s_gin, 16)
                row += n
            for n in range(1, 4):
                x_in(n)
            sc.dma_start(side_in0.rearrange("p (t n) -> p t n", t=KT),
                         w_in[:, :, 2 * GK + 2 * D:]).then_inc(s_side0, 16)
            sc.dma_start(sums_in, t["c_sums"]).then_inc(s_sums, 16)
            sc.dma_start(masks, t["c_masks"].rearrange("p (l n) -> p l n", l=8))\
                .then_inc(s_masks, 16)
            sc.wait_ge(s_pad, 1)
            sc.dma_start(w_up[0:RANK, :], t["gla_w_gate_up"][0]).then_inc(s_up, 16)
            sc.dma_start(w_up[RANK:RANK + 1, :], t["gla_b_gate"]).then_inc(s_up, 16)

            def gates():
                sc.wait_ge(s_z, 1)
                z_ps = ps[:, 4:8, :].rearrange("p b n -> p (b n)")
                sc.activation(z_sb, z_ps, ACT.Abs).then_inc(s_zact, 1)
                high(H_GLA, 14)
                sc.wait_ge(s_zact, 1)
                sc.activation(z_sb, z_sb, ACT.Exp, scale=-1.0).then_inc(s_zact, 1)
                high(H_GLA, 15)
                sc.wait_ge(s_zact, 2)
                sc.activation(z_sb, z_sb, ACT.Ln, bias=1.0).then_inc(s_zact, 1)
                for c in range(2):
                    copy_corr(H_GLA, 14 + c, c)
                    high(H_GLA, 16 + c)
                high(H_GLA, 18)
                sc.wait_ge(s_g, 1)
                g_by_head = g_sb.rearrange("p (b h n) -> p h b n", b=TB, h=GH)
                for i in range(GH):
                    sc.activation(xb[:, 4 * i:4 * i + 2, 0, :], g_by_head[:, i], ACT.Copy)\
                        .then_inc(s_ghi, 1)
                    if i == 0:
                        sc.wait_ge(s_glo, 1)
                        head_gate(0)
                high(H_GLA, 19)
                sc.wait_ge(s_glo, GH)

            def head_gate(i):
                sc.activation(gate, xb[:, bass.ds(4 * i, 2)].bitcast(F32), ACT.Copy)\
                    .then_inc(s_gcur, 1)

            def decays(i, b, d):
                sc.wait_ge(s_sum, 4 * i + 2 * b + d + 1)
                sc.activation(dec[:, d].rearrange("p (g l) n -> p g (l n)", g=2), ps[:, 4:6, :],
                              ACT.Exp, scale=1.0 / TAU).then_inc(s_dec, 1)

            def head_output(i, first=False):
                sc.wait_ge(s_o, i + 1)
                o_ps = ps[:, 6:8, :].rearrange("p b (e s) -> p (b e) s", e=2)
                sc.activation(sq_b, o_ps, ACT.Square).then_inc(s_osq, 1)
                if not first:
                    sc.wait_ge(s_gated, i)
                for e in range(4):
                    ins = sc.activation(o_sb[:, e, :], o_ps[:, e, :], ACT.Copy,
                                        scale=gains[:, N_GLA + e:N_GLA + e + 1])
                ins.then_inc(s_ocp, 1)

            def gating(h, i):
                high(h, 3)
                sc.wait_ge(s_r, 2 * i)
                sc.activation(e_sb, r_sb, ACT.Tanh, scale=0.5).then_inc(s_tanh, 1)
                sc.wait_ge(s_ost, i)
                sc.activation(root_o, ps[:, 5, 0:S], ACT.Sqrt, scale=4.0 / HV, bias=eps[:, 1:2])\
                    .then_inc(s_oroot, 1)
                highs(h, 4, 6)
                sc.wait_ge(s_full, i)
                sc.activation(xb[:, bass.ds(4 * i - 4, 4), 0, :], o_sb, ACT.Copy)\
                    .then_inc(s_fullhi, 1)

            sc.wait_ge(s_gains, 1)
            for u in range(UNITS):
                sc.wait_ge(s_trc, 2 * u + 2)
                convert(resid, N_MIX0, xa, HK4 * u, HK4 * u + HK4)
                if u < 2:
                    highs(H_GLA, 2 * u, 2 * u + 2)
                if u in (1, 2):
                    high(H_GLA, u + 3)
            sc.wait_ge(s_side0, 16)
            sc.activation(side0[:, 0, :], side_in0, ACT.Copy).then_inc(s_sidehi, 1)
            sc.wait_ge(s_sums, 16)
            sc.activation(sums.rearrange("p a b -> p (a b)"), sums_in, ACT.Copy)\
                .then_inc(s_sumsr, 1)
            highs(H_GLA, 6, 10)
            copy_corr(H_GLA, 6, 0)
            copy_corr(H_GLA, 7, 1)
            sc.wait_ge(s_eps, 2)
            highs(H_GLA, 10, 12)
            take_root(ST_MIX0, D, True)
            highs(H_GLA, 12, 14)
            gates()
            highs(H_GLA, 20, 22)
            decays(0, 0, 0)
            high(H_GLA, 22)
            decays(0, 0, 1)
            highs(H_GLA, 23, 26)
            decays(0, 1, 0)
            decays(0, 1, 1)
            copy_corr(H_GLA, 22, 0)
            high(H_GLA, 26)
            copy_corr(H_GLA, 23, 1)
            head_output(0, True)

            with sc.Fori(1, GH) as i:
                h = H_GLA + i * HEAD_HALVES
                head_gate(i)
                gating(h, i)
                highs(h, 6, 8)
                decays(i, 0, 0)
                highs(h, 8, 10)
                decays(i, 0, 1)
                copy_corr(h, 6, 0)
                copy_corr(h, 7, 1)
                highs(h, 10, 18)
                decays(i, 1, 0)
                copy_corr(h, 14, 0)
                copy_corr(h, 15, 1)
                decays(i, 1, 1)
                highs(h, 18, 26)
                head_output(i)
                copy_corr(h, 22, 0)
                high(h, 26)
                copy_corr(h, 23, 1)

            gating(H_OUT, GH)
            highs(H_OUT, 6, PANEL + 4)
            with sc.Fori(1, PANELS - 1) as p:
                highs(H_OUT + p * PANEL, 4, PANEL + 4)
            last_panel(H_OUT + (PANELS - 1) * PANEL, G_OUT, N_MLP0)

            def end(h, g):
                high(h, 4)
                sc.wait_ge(s_ang, 2)
                sc.activation(sin, sin, ACT.Sin).then_inc(s_trig, 1)
                sc.activation(cos, cos, ACT.Sin).then_inc(s_trig, 1)
                last_panel(h, g, N_KVIN, 5)

            mlp(H_MLP0, G_MLP0, 0, N_MLP0, ST_MLP0, end)

            def queries_in(j):
                if 4 <= j < 8:
                    convert(resid, N_MIX1, xb, 2 * (j - 4), 2 * (j - 4) + 2)

            first_panel(H_DKV, G_DKV, N_KVIN, ST_MIX1, True, queries_in)
            copy_corr(H_DKV, PANEL - 2, 0)
            copy_corr(H_DKV, PANEL - 1, 1)
            sc.wait_ge(s_side1, 16)
            sc.activation(side1[:, 0, :], side_in1, ACT.Copy).then_inc(s_sidehi, 1)
            for j in range(2, 8):
                high(H_DQ, j)
                if j < 6:
                    convert(resid, N_MIX1, xb, 2 * j + 4, 2 * j + 6)
            take_root(ST_C, LORA)

            def convert_lat(n, dst):
                sc.wait_ge(s_laty, n)
                for c in range(LT):
                    sc.activation(dst[:, c, 0, :], lat[:, c, :], ACT.Copy).then_inc(s_xhi, 1)

            convert_lat(1, xc)
            highs(H_DQ, 8, PANEL + 2)
            copy_corr(H_DQ, PANEL - 2, 0)
            copy_corr(H_DQ, PANEL - 1, 1)

            def turned(i):
                sc.wait_ge(s_pt, i + 1)
                sc.activation(pt_sb, ps[:, 4:6, 0:3 * P], ACT.Copy).then_inc(s_ptc, 1)

            def exponentials(i):
                sc.wait_ge(s_nmx, i + 1)
                for hd in range(2):
                    for blk in range(2):
                        col = 2 * blk + hd
                        a, z = (0, P) if blk == 0 else (P, 3 * P)
                        ins = sc.activation(pr_sb[:, hd, a:z], sc_sb[:, hd, a:z], ACT.Exp,
                                            bias=nmx[:, col:col + 1], scale=MLA_SCALE,
                                            accum_out=den[:, col:col + 1])
                ins.then_inc(s_exp, 1)

            def attended(i):
                sc.wait_ge(s_ov, i + 1)
                sc.activation(xb[:, bass.ds(2 * i, 2), 0, :],
                              ps[:, 6, :].rearrange("p (h s) -> p h s", h=2), ACT.Copy)\
                    .then_inc(s_ohi, 1)

            def slot(i, dotted, weighed):
                h = H_PAIR + i * 4
                if weighed:
                    turned(i - 2)
                high(h, 2, pairs=i + 1)
                copy_corr(h, 0, 0)
                high(h, 3, n=HF // 2, pairs=i + 1)
                high(h, 4, pairs=i + 1)
                if weighed:
                    attended(i - 2)
                if dotted:
                    exponentials(i - 1)
                copy_corr(h, 1, 1)
                high(h, 5, pairs=i + 1)
                copy_corr(h, 2, 0)
                copy_corr(h, 3, 1, banks=1)

            high(H_PAIR, 2, pairs=1)
            high(H_PAIR, 3, n=HF // 2, pairs=1)
            take_root(ST_CQ, LORA)
            copy_corr(H_PAIR, 0, 0)
            high(H_PAIR, 4, pairs=1)
            convert_lat(2, xq)
            copy_corr(H_PAIR, 1, 1)
            high(H_PAIR, 5, pairs=1)
            copy_corr(H_PAIR, 2, 0)
            copy_corr(H_PAIR, 3, 1, banks=1)
            slot(1, True, False)
            with sc.Fori(2, PAIRS) as i:
                slot(i, True, True)
            pair_loads[0] = PAIRS
            turned(PAIRS - 2)
            highs(H_WO, 2, 4)
            attended(PAIRS - 2)
            exponentials(PAIRS - 1)
            highs(H_WO, 4, 8)
            turned(PAIRS - 1)
            high(H_WO, 8)
            attended(PAIRS - 1)
            highs(H_WO, 9, PANEL + 4)
            with sc.Fori(1, PANELS - 1) as p:
                highs(H_WO + p * PANEL, 4, PANEL + 4)
            last_panel(H_WO + (PANELS - 1) * PANEL, G_WO, N_MLP1)

            def result(c0, c1):
                for c in range(c0, c1, 2):
                    sc.wait_ge(s_read, G_END - 2 * PANELS + c // 2 + 1 + 2)
                    for n in range(c, c + 2):
                        sc.activation(y_sb[:, n, :], resid[:, n, :], ACT.Copy,
                                      scale=gains[:, N_FIN + n:N_FIN + n + 1]).then_inc(s_y, 1)

            def end(h, g):
                for j in range(4, 10):
                    if j < PANEL:
                        high(h, j)
                    result(2 * (j - 4), 2 * (j - 4) + 2)

            mlp(H_MLP1, G_MLP1, UP_GROUPS, N_MLP1, ST_MLP1, end)
            sc.wait_ge(s_read, G_END + 2)
            sc.wait_ge(s_sqs, ST_FIN + 1)
            sc.activation(sq_b, resid[:, KT - 4:KT, :], ACT.Square).then_inc(s_ysq, 1)
            result(KT - 4, KT)
            sc.wait_ge(s_stat, ST_FIN + 1)
            sc.wait_ge(s_rstd, ST_FIN)
            sc.activation(root[:, S:S + TB], ps[:, 7, S:S + TB], ACT.Sqrt, scale=1.0 / D,
                          bias=eps[:, 0:1]).then_inc(s_root, 1)
            sc.wait_ge(s_rstd, ST_FIN + 1)
            for n, (b, c, bank) in enumerate(RESULT):
                if n % 2:
                    sc.wait_ge(s_fin, n + 1)
                    sc.activation(o_nat[:, b, c * 512:(c + 1) * 512], ps[:, bank, :], ACT.Copy,
                                  scale=rstd[:, S + b:S + b + 1]).then_inc(s_finc[1], 1)

        @block.tensor
        def _(pe):
            def begin(h, j, g=None):
                pe.wait_ge(s_split, h + j + 1 + RING)
                if g is not None:
                    pe.wait_ge(s_read, g + 1)

            def weights(j, c, part, col):
                return wts[:, j % RING, c, part, col:col + P]

            def products(bank, n, main, rest, first, last):
                corr_at = slice(n // 2, n)
                if last:
                    pe.matmul(bank[:, corr_at], *rest, start=False, stop=False)
                ins = pe.matmul(bank[:, 0:n], *main, start=first, stop=last)
                if not last:
                    ins = pe.matmul(bank[:, corr_at], *rest, start=False, stop=False)
                return ins

            def half_t(j, c2, x, x0, first, last):
                for n in range(2):
                    for c in range(HK4):
                        ins = products(ps[:, 2 * c2 + n], 2 * S,
                                       (weights(j, c, 0, n * P), x[:, x0 + c]),
                                       (weights(j, c, 1, n * P), x[:, x0 + c, 0, :]),
                                       first and c == 0, last and c == HK4 - 1)
                ins.then_inc(s_mult, 1)

            def half_n(j, c2, x, x0, first, last):
                for b in range(TB):
                    tok = slice(b * P, (b + 1) * P)
                    for c in range(HK4):
                        ins = products(ps[:, 2 * c2 + b], 2 * HC,
                                       (x[:, x0 + c, 0, tok], wts[:, j % RING, c]),
                                       (x[:, x0 + c, 1, tok], wts[:, j % RING, c, 0, :]),
                                       first and c == 0, last and c == HK4 - 1)
                ins.then_inc(s_mult, 1)

            def panel(h, g, x, ready=None, half=half_t, after=None):
                for u in range(UNITS):
                    if ready:
                        ready(u)
                    for c2 in range(2):
                        j = 2 * u + c2
                        begin(h, j, g + c2 if u == 0 else None)
                        half(j, c2, x, HK4 * u, u == 0, u == UNITS - 1)
                        if after and j in after:
                            after[j]()

            def stat(st, columns):
                pe.wait_ge(s_sqs, st + 1)
                if st:
                    pe.wait_ge(s_rstd, st)
                ins = pe.matmul(ps[:, 7, 0:S], ones[:, :], sqs[:, 0:S], start=True, stop=True)
                for b in range(TB if columns else 0):
                    ins = pe.matmul(ps[:, 7, S + b:S + b + 1], sqs[:, b * P:(b + 1) * P],
                                    ones[:, 0:1], start=True, stop=True)
                ins.then_inc(s_stat, 1)

            def stat_latent(st, n):
                pe.wait_ge(s_latsq, n)
                pe.wait_ge(s_rstd, st)
                for c in range(LT):
                    ins = pe.matmul(ps[:, 7, 0:S], ones[:, :], sq_a[:, c, :], start=c == 0,
                                    stop=c == LT - 1)
                ins.then_inc(s_stat, 1)

            def inputs(x0):
                return lambda u: pe.wait_ge(s_x, x0 + HK4 * (u + 1))

            def hidden(k):
                return lambda u: pe.wait_ge(s_hid, k + 2 * (u + 1) + 2)

            def mlp(h0, g0, k0, x0, st, after=None):
                panel(h0, g0, xa, inputs(x0), after={4: lambda: stat(st, False)})
                with pe.Fori(1, PANELS) as p:
                    panel(h0 + p * PANEL, g0 + p * 2, xa)
                with pe.Fori(PANELS, 2 * PANELS) as p:
                    panel(h0 + p * PANEL, g0 + p * 2, xb, hidden(k0))
                with pe.Fori(1, SLABS - 1) as s:
                    h = h0 + s * SLAB_HALVES
                    g = g0 + s * SLAB_GROUPS
                    with pe.Fori(0, PANELS) as p:
                        panel(h + p * PANEL, g + p * 2, xa)
                    with pe.Fori(PANELS, 2 * PANELS) as p:
                        panel(h + p * PANEL, g + p * 2, xb, hidden(k0 + s * (2 * PANELS)))
                h, g = h0 + (SLABS - 1) * SLAB_HALVES, g0 + (SLABS - 1) * SLAB_GROUPS
                with pe.Fori(0, PANELS) as p:
                    panel(h + p * PANEL, g + p * 2, xa)
                with pe.Fori(PANELS, 2 * PANELS - 1) as p:
                    panel(h + p * PANEL, g + p * 2, xb, hidden(k0 + (SLABS - 1) * (2 * PANELS)))
                p = 2 * PANELS - 1
                panel(h + p * PANEL, g + p * 2, xb, after=after)

            pe.sem_inc(s_mult, RING)
            pe.wait_ge(s_ident, 16)
            def x_transposed(n):
                pe.wait_ge(s_xin[n], 16)
                for m in range(2 * n, 2 * n + 2):
                    if n > 1:
                        pe.wait_ge(s_trc, m - 3)
                    for q in range(4):
                        c, b = 2 * m + q // 2, q % 2
                        ins = pe.transpose(ps[:, 4 + m % 4, q * P:(q + 1) * P],
                                           x_nat[:, b, c * P:(c + 1) * P], ident[:, :])
                    ins.then_inc(s_tr, 1)

            x_transposed(0)
            pe.wait_ge(s_gin, 16 * 7)
            pe.transpose(ps[:, 0, 0:N_GAINS], gains_in[0:N_GAINS, :], ident[0:N_GAINS, 0:N_GAINS])\
                .then_inc(s_gtr, 1)
            x_transposed(1)

            def low_rank():
                pe.wait_ge(s_sidelo, 1)
                pe.wait_ge(s_trc, 8)
                for b in range(TB):
                    for c in range(KT):
                        cols = slice(c * RANK, (c + 1) * RANK)
                        tok = slice(b * P, (b + 1) * P)
                        ins = products(ps[:, 4 + b], 2 * RANK,
                                       (xa[:, c, 0, tok], side0[:, :, cols]),
                                       (xa[:, c, 1, tok], side0[:, 0, cols]), c == 0, c == KT - 1)
                ins.then_inc(s_low, 1)
                pe.wait_ge(s_ones, 1)
                stat(ST_MIX0, True)

            def low_transposed():
                pe.wait_ge(s_lownat, 1)
                for b in range(TB):
                    ins = pe.transpose(ps[:, 6, b * P:(b + 1) * P], low_nat[:, b, :], ident[:, :])
                ins.then_inc(s_lowt, 1)

            def gates_in():
                pe.wait_ge(s_lowtc, 1)
                pe.wait_ge(s_rstd, ST_MIX0 + 1)
                pe.wait_ge(s_up, 32)
                for b in range(TB):
                    for n in range(2):
                        ins = pe.matmul(ps[:, 4 + 2 * b + n, :], low_t[:, b * P:(b + 1) * P],
                                        w_up[:, n * 512:(n + 1) * 512], start=True, stop=True)
                ins.then_inc(s_z, 1)

            def gate_sums(i, b, d):
                r = 2 * b + d
                if r == 0:
                    pe.wait_ge(s_gcur, i + 1)
                    if not isinstance(i, int):
                        pe.wait_ge(s_oroot, i)
                pe.wait_ge(s_dec, 4 * i + r + 1)
                for n in range(2):
                    at = 4 * n + (b if n else 0)
                    for part in range(2):
                        ins = pe.matmul(ps[:, 4 + n, :], gate[:, b, part, d * P:(d + 1) * P],
                                        sums[:, at:at + 4, :], start=part == 0, stop=part == 1)
                ins.then_inc(s_sum, 1)

            def scores(i, b):
                pe.wait_ge(s_qd, 4 * i + 2 * b + 2)
                pe.wait_ge(s_kd, 4 * i + 2 * b + 2)
                if b == 0:
                    pe.wait_ge(s_ocp, i + 1)
                else:
                    pe.wait_ge(s_att, 2 * i + 1)
                tok = slice(b * P, (b + 1) * P)
                for n in range(8):
                    at = PLACES[b][n] if n < 7 else None
                    for d in range(2):
                        lhs = dec[:, d, at, :] if n < 7 else k_sb[:, d, tok]
                        rhs = qdec[:, d, at, :] if n < 7 else q_sb[:, d, tok]
                        ins = pe.matmul(ps[:, 6 + n // 4, (n % 4) * P:(n % 4 + 1) * P], lhs, rhs,
                                        start=d == 0, stop=d == 1)
                if b == 1:
                    for d in range(2):
                        ins = pe.matmul(ps[:, 4, 0:P], kx[:, d, :], qdec[:, d, PREFIX, :],
                                        start=d == 0, stop=d == 1)
                ins.then_inc(s_sc, 1)

            def output(i):
                pe.wait_ge(s_att, 2 * i + 2)
                pe.wait_ge(s_v, 2 * i + 2)
                for e in range(4):
                    bank, col = 6 + e // 2, (e % 2) * S
                    feat = slice(e * P, (e + 1) * P)
                    pe.matmul(ps[:, bank, col:col + P], v_sb[:, 0, feat], att[:, 0:P],
                              start=True, stop=True)
                    pe.matmul(ps[:, bank, col + P:col + S], v_sb[:, 0, feat], att[:, P:S],
                              start=True, stop=False)
                    ins = pe.matmul(ps[:, bank, col + P:col + S], v_sb[:, 1, feat],
                                    att[:, S:3 * P], start=False, stop=True)
                ins.then_inc(s_o, 1)

            def output_squares(i):
                pe.wait_ge(s_osq, i + 1)
                for e in range(4):
                    ins = pe.matmul(ps[:, 5, 0:S], ones[:, :], sq_b[:, e, :], start=e == 0,
                                    stop=e == 3)
                ins.then_inc(s_ost, 1)

            x_transposed(2)
            pe.wait_ge(s_gains, 1)
            panel(H_GLA, G_GLA, xa, inputs(X_GLA), after={0: lambda: x_transposed(3), 7: low_rank})
            pe.wait_ge(s_sumsr, 1)
            panel(H_GLA + PANEL, G_GLA + 2, xa, half=half_n,
                  after={1: low_transposed, 2: gates_in})
            panel(H_GLA + 2 * PANEL, G_GLA + 4, xa,
                  after={2: lambda: gate_sums(0, 0, 0), 3: lambda: gate_sums(0, 0, 1),
                         5: lambda: (scores(0, 0), gate_sums(0, 1, 0)),
                         6: lambda: gate_sums(0, 1, 1), 7: lambda: scores(0, 1)})
            output(0)
            output_squares(0)

            with pe.Fori(1, GH) as i:
                h = H_GLA + i * HEAD_HALVES
                g = G_GLA + i * 6
                panel(h, g, xa, after={3: lambda: gate_sums(i, 0, 0), 5: lambda: gate_sums(i, 0, 1)})
                panel(h + PANEL, g + 2, xa, half=half_n,
                      after={4: lambda: scores(i, 0), 5: lambda: gate_sums(i, 1, 0),
                             7: lambda: gate_sums(i, 1, 1)})
                panel(h + 2 * PANEL, g + 4, xa,
                      after={1: lambda: scores(i, 1), 5: lambda: output(i)})
                output_squares(i)

            with pe.Fori(0, PANELS) as p:
                panel(H_OUT + p * PANEL, G_OUT + p * 2, xb,
                      lambda u: pe.wait_ge(s_gated, u + 1))
            mlp(H_MLP0, G_MLP0, 0, X_MLP0, ST_MLP0)

            panel(H_DKV, G_DKV, xa, inputs(X_KV), after={4: lambda: stat(ST_MIX1, True)})
            panel(H_DQ, G_DQ, xb, inputs(X_Q), after={2: lambda: stat_latent(ST_C, 2)})
            pe.wait_ge(s_sidelo, 2)
            for b in range(TB):
                for c in range(KT):
                    cols = slice(c * ROPE, (c + 1) * ROPE)
                    tok = slice(b * P, (b + 1) * P)
                    ins = products(ps[:, 4 + b], 2 * ROPE, (xa[:, c, 0, tok], side1[:, :, cols]),
                                   (xa[:, c, 1, tok], side1[:, 0, cols]), c == 0, c == KT - 1)
            ins.then_inc(s_low, 1)

            def keys(i):
                h, g = H_PAIR + i * 4, G_PAIR + i * 4
                begin(h, 0, g)
                half_t(0, 0, xc, 0, True, True)

            def values(i):
                h, g = H_PAIR + i * 4, G_PAIR + i * 4
                begin(h, 1, g + 1)
                half_n(1, 1, xc, 0, True, True)

            def queries(i):
                h, g = H_PAIR + i * 4, G_PAIR + i * 4
                begin(h, 2, g + 2)
                half_t(2, 0, xq, 0, True, True)

            def rotary_queries(i):
                h, g = H_PAIR + i * 4, G_PAIR + i * 4
                begin(h, 3, g + 3)
                for c in range(LT):
                    cols = (c % 2) * P
                    ins = products(ps[:, 2], 2 * S, (weights(3, c // 2, 0, cols), xq[:, c]),
                                   (weights(3, c // 2, 1, cols), xq[:, c, 0, :]),
                                   c == 0, c == LT - 1)
                ins.then_inc(s_mult, 1)

            def rotate(i):
                pe.wait_ge(s_raw, i + 1)
                if not isinstance(i, int) or i:
                    pe.wait_ge(s_sinr, i)
                pe.matmul(ps[:, 7, 0:S], rot, raw_r, start=True, stop=True).then_inc(s_rot, 1)

            def dots(i, b):
                pe.wait_ge(s_read, G_PAIR + i * 4 + 4 + 2)
                pe.wait_ge(s_qr, i + 1)
                pe.wait_ge(s_ptc, i + 1)
                for hd in range(2):
                    for blk in range(2):
                        n = (blk + 1) * P
                        dst = ps[:, 4 + hd, blk * P:blk * P + n]
                        tok = slice(blk * P, (blk + 1) * P)
                        pe.matmul(dst, qn_sb[:, b, hd, tok], kt_sb[:, b, hd, 0:n], start=True,
                                  stop=False)
                        ins = pe.matmul(dst, qr_sb[:, b, tok], keys_r[:, hd, 0:n], start=False,
                                        stop=True)
                ins.then_inc(s_dots, 1)

            def turn(i):
                pe.wait_ge(s_pr, i + 2)
                for hd in range(2):
                    for n in range(3):
                        ins = pe.transpose(ps[:, 4 + hd, n * P:(n + 1) * P],
                                           pr_sb[:, hd, n * P:(n + 1) * P], ident[:, :])
                ins.then_inc(s_pt, 1)

            def weigh(i, b):
                pe.wait_ge(s_ptc, i + 2)
                pe.wait_ge(s_ox, i + 1)
                for hd in range(2):
                    feat = slice(hd * P, (hd + 1) * P)
                    at = hd * S
                    pe.matmul(ps[:, 6, at:at + P], vt_sb[:, b, 0, feat], pt_sb[:, hd, 0:P],
                              start=True, stop=True)
                    pe.matmul(ps[:, 6, at + P:at + S], vt_sb[:, b, 0, feat], pt_sb[:, hd, P:S],
                              start=True, stop=False)
                    ins = pe.matmul(ps[:, 6, at + P:at + S], vt_sb[:, b, 1, feat],
                                    pt_sb[:, hd, S:3 * P], start=False, stop=True)
                ins.then_inc(s_ov, 1)

            stat_latent(ST_CQ, 4)
            pe.wait_ge(s_krn, 1)
            for b in range(TB):
                ins = pe.transpose(ps[:, 6, b * P:(b + 1) * P], kr_nat[:, b, :], ident[:, :])
            ins.then_inc(s_krt, 1)
            pe.wait_ge(s_x, X_C + LT)
            keys(0)
            pe.wait_ge(s_krc, 1)
            pe.wait_ge(s_rotm, 16)
            pe.matmul(ps[:, 6, S:2 * S], rot, raw_r, start=True, stop=True).then_inc(s_krot, 1)
            values(0)
            pe.wait_ge(s_x, X_CQ + LT)
            queries(0)
            rotary_queries(0)
            pe.wait_ge(s_keysr, 2)

            def slot(i, b, weighed=True):
                if weighed:
                    turn(i - 2)
                rotate(i - 1)
                keys(i)
                dots(i - 1, 1 - b)
                if weighed:
                    weigh(i - 2, b)
                values(i)
                queries(i)
                rotary_queries(i)

            slot(1, 1, weighed=False)
            with pe.Fori(1, PAIRS // 2) as m:
                slot(m * 2, 0)
                slot(m * 2 + 1, 1)
            turn(PAIRS - 2)
            rotate(PAIRS - 1)

            def attention_in(u):
                pe.wait_ge(s_ox, 2 * (u + 1) + 1)

            panel(H_WO, G_WO, xb, attention_in,
                  after={0: lambda: (dots(PAIRS - 1, 1), weigh(PAIRS - 2, 0)),
                         3: lambda: turn(PAIRS - 1), 4: lambda: weigh(PAIRS - 1, 1)})
            with pe.Fori(1, PANELS) as p:
                panel(H_WO + p * PANEL, G_WO + p * 2, xb)
            def result(parts):
                for n in parts:
                    b, c0, bank = RESULT[n]
                    pe.wait_ge(s_y, KT if c0 == 3 else KT - 4)
                    if n == 7:
                        pe.wait_ge(s_finc[0], 1)
                    elif bank < 4:
                        pe.wait_ge(s_read, G_END + bank // 2 + 1)
                    for c in range(4):
                        ins = pe.transpose(ps[:, bank, c * P:(c + 1) * P],
                                           y_sb[:, 4 * c0 + c, b * P:(b + 1) * P], ident[:, :])
                    ins.then_inc(s_fin, 1)

            mlp(H_MLP1, G_MLP1, UP_GROUPS, X_MLP1, ST_MLP1, {5: lambda: result(range(3))})
            result(range(3, 5))
            pe.wait_ge(s_rstd, ST_FIN)
            pe.wait_ge(s_sqs, ST_FIN + 1)
            pe.wait_ge(s_ysq, 1)
            for b in range(TB):
                tok = slice(b * P, (b + 1) * P)
                pe.matmul(ps[:, 7, S + b:S + b + 1], sqs[:, tok], ones[:, 0:1], start=True,
                          stop=False)
                for c in range(4):
                    ins = pe.matmul(ps[:, 7, S + b:S + b + 1], sq_b[:, c, tok], ones[:, 0:1],
                                    start=False, stop=c == 3)
            ins.then_inc(s_stat, 1)
            result(range(5, 8))

        @block.vector
        def _(dve):
            steps = [0]

            def step(ins):
                steps[0] += 1
                ins.then_inc(s_dve, 1)
                dve.wait_ge(s_dve, steps[0])

            def low(h, j, n=HF):
                slot = j % RING
                dve.wait_ge(s_high, h + j + 1)
                src = stage[:, slot, 0:n].rearrange("p (t n) -> p t n", n=HC)
                dve.tensor_tensor(wts[:, slot, 0:n // HC, 1, :], src,
                                  wts[:, slot, 0:n // HC, 0, :].bitcast(F32), ALU.subtract)\
                    .then_inc(s_split, 1)

            def lows(h, j0, j1):
                for j in range(j0, j1):
                    low(h, j)

            def convert(src, gain, dst, x0, c0, c1):
                for c in range(c0, c1):
                    dve.wait_ge(s_xhi, x0 + c + 1)
                    dve.scalar_tensor_tensor(out=dst[:, c, 1, :], in0=src[:, c, :],
                                             scalar=gains[:, gain + c:gain + c + 1],
                                             in1=dst[:, c, 0, :].bitcast(F32),
                                             op0=ALU.mult, op1=ALU.subtract).then_inc(s_x, 1)

            def refined(to, root, sums, features):
                step(dve.reciprocal(to, root))
                step(dve.tensor_scalar(root, sums, -0.5 / features, -0.5 * EPS, ALU.mult, ALU.add))
                step(dve.tensor_tensor(root, root, to, ALU.mult))
                step(dve.tensor_tensor(root, root, to, ALU.mult))
                dve.scalar_tensor_tensor(out=to, in0=root, scalar=1.5, in1=to, op0=ALU.add,
                                         op1=ALU.mult).then_inc(s_rstd, 1)

            def factors(st, columns=False, dst=None):
                dve.wait_ge(s_root, st + 1)
                n = S + TB if columns else S
                refined(rstd[:, 0:n] if dst is None else dst, root[:, 0:n], ps[:, 7, 0:n],
                        LORA if dst is not None else D)
                dve.wait_ge(s_rstd, st + 1)

            def last_panel(h, p, r, gain, x0):
                for j in range(4, PANEL + 2):
                    low(h, j)
                    convert(resid, gain, xa, x0, 2 * (j - 4), 2 * (j - 4) + 2)
                down_tail(h, p, r)

            def first_panel(h, gain, st, x0, columns=False, more=None):
                convert(resid, gain, xa, x0, KT - 4, KT)
                for j in range(4, PANEL + 2):
                    low(h, j)
                    if more:
                        more(j)
                    if j == 8:
                        factors(st, columns)

            def sum_group(g, n, c, dst=None, banks=2):
                dve.wait_ge(s_corr, n + 1)
                to = total[:, c, 0:banks, :] if dst is None else dst
                dve.tensor_tensor(to, ps[:, 2 * c:2 * c + banks, 0:S], corr[:, c, 0:banks, :],
                                  ALU.add).then_inc(s_read, 1)

            def per_token(banks, factor=None):
                f = rstd[:, 0:S] if factor is None else factor
                return f.rearrange("p (o s) -> p o s", o=1).broadcast_to([P, banks, S])

            def up_tail(h, g, k, cc):
                for c in range(2):
                    dve.wait_ge(s_hid, k + c + 1)
                    sum_group(g + c, cc + c, c)
                    dve.wait_ge(s_read, g + c + 3)
                    dve.scalar_tensor_tensor(out=act[:, c], in0=total[:, c], scalar=0.0,
                                             in1=per_token(2), op0=ALU.max, op1=ALU.mult)\
                        .then_inc(s_act, 1)
                    low(h, PANEL + 2 + c)

            def down(h, p, r, c):
                dve.wait_ge(s_mult, h + PANEL - 2 + c + 1 + RING)
                to = resid[:, bass.ds(p * 4 + 2 * c, 2), :]
                banks = ps[:, 2 * c:2 * c + 2]
                dve.tensor_tensor(to, banks[:, :, 0:S], to, ALU.add).then_inc(s_main, 1)
                dve.wait_ge(s_main, r + c + 1)
                dve.tensor_tensor(to, banks[:, :, S:2 * S], to, ALU.add).then_inc(s_read, 1)

            def down_tail(h, p, r):
                for c in range(2):
                    down(h, p, r, c)
                    low(h, PANEL + 2 + c)

            def down_panels(h0, r0, count=PANELS, start=0):
                with dve.Fori(start, count) as p:
                    lows(h0 + p * PANEL, 4, PANEL + 2)
                    down_tail(h0 + p * PANEL, p, r0 + p * 2)

            def up_panels(h0, g0, k0, c0, start=0):
                with dve.Fori(start, PANELS) as p:
                    lows(h0 + p * PANEL, 4, PANEL + 2)
                    up_tail(h0 + p * PANEL, g0 + p * 2, k0 + p * 2, c0 + p * 2)

            def mlp(h0, g0, k0, c0, r0, x0, gain, st, end):
                first_panel(h0, gain, st, x0)
                up_tail(h0, g0, k0, c0)
                up_panels(h0, g0, k0, c0, 1)
                down_panels(h0 + PANELS * PANEL, r0)
                with dve.Fori(1, SLABS - 1) as s:
                    h, g, n = h0 + s * SLAB_HALVES, g0 + s * SLAB_GROUPS, s * (2 * PANELS)
                    up_panels(h, g, k0 + n, c0 + n)
                    down_panels(h + PANELS * PANEL, r0 + n)
                h, g = h0 + (SLABS - 1) * SLAB_HALVES, g0 + (SLABS - 1) * SLAB_GROUPS
                n = (SLABS - 1) * 2 * PANELS
                up_panels(h, g, k0 + n, c0 + n)
                down_panels(h + PANELS * PANEL, r0 + n, PANELS - 1)
                end(h + (2 * PANELS - 1) * PANEL, r0 + n + 2 * (PANELS - 1))

            dve.sem_inc(s_split, RING)
            dve.sem_inc(s_read, 2)
            dve.sem_inc(s_ox, 1)

            def x_copied(n):
                for m in range(2 * n, 2 * n + 2):
                    dve.wait_ge(s_tr, m + 1)
                    dve.tensor_copy(resid[:, 2 * m:2 * m + 2, :],
                                    ps[:, 4 + m % 4, :].rearrange("p (c s) -> p c s", c=2))\
                        .then_inc(s_trc, 1)

            x_copied(0)
            dve.wait_ge(s_gtr, 1)
            dve.tensor_copy(gains[:, :], ps[:, 0, 0:N_GAINS]).then_inc(s_gains, 1)
            dve.wait_ge(s_gains, 1)
            x_copied(1)
            for u in range(UNITS):
                convert(resid, N_MIX0, xa, X_GLA, HK4 * u, HK4 * u + HK4)
                if u < 2:
                    lows(H_GLA, 2 * u, 2 * u + 2)
                if u in (1, 2):
                    low(H_GLA, u + 3)
                if u < 2:
                    x_copied(u + 2)
            dve.wait_ge(s_sidehi, 1)
            dve.tensor_tensor(side0[:, 1, :], side_in0, side0[:, 0, :].bitcast(F32), ALU.subtract)\
                .then_inc(s_sidelo, 1)

            def queries_keys(i):
                for c in range(2):
                    sum_group(G_GLA + i * 6 + c, C_GLA + i * 6 + c, c)

            def scale_queries_keys(i):
                for c, (to, scale, done) in enumerate(((q_sb, float(HK) ** -0.5, s_q),
                                                       (k_sb, 1.0, s_k))):
                    dve.wait_ge(s_read, G_GLA + i * 6 + c + 3)
                    dve.scalar_tensor_tensor(out=to, in0=total[:, c], scalar=scale,
                                             in1=per_token(2), op0=ALU.mult, op1=ALU.mult)\
                        .then_inc(done, 1)
                dve.wait_ge(s_q, i + 1)

            def gates():
                dve.wait_ge(s_low, 1)
                lt = low_tmp[:, 0:TB * RANK].rearrange("p (b c) -> p b c", b=TB)
                step(dve.tensor_copy(lt, ps[:, 4:6, RANK:2 * RANK]))
                step(dve.tensor_tensor(lt, ps[:, 4:6, 0:RANK], lt, ALU.add))
                factors(ST_MIX0, columns=True)
                dve.wait_ge(s_pad, 1)
                for b in range(TB):
                    ins = dve.tensor_scalar(low_nat[:, b, 0:RANK], lt[:, b, :],
                                            rstd[:, S + b:S + b + 1], None, ALU.mult)
                ins.then_inc(s_lownat, 1)
                dve.wait_ge(s_sumsr, 1)
                scale_queries_keys(0)
                dve.wait_ge(s_lowt, 1)
                dve.tensor_copy(low_t, ps[:, 6, 0:S]).then_inc(s_lowtc, 1)

            def split_gates():
                dve.wait_ge(s_zact, 3)
                z_ps = ps[:, 4:8, :].rearrange("p b n -> p (b n)")
                dve.scalar_tensor_tensor(out=g_sb, in0=z_ps, scalar=0.0, in1=z_sb, op0=ALU.min,
                                         op1=ALU.subtract).then_inc(s_g, 1)
                g_by_head = g_sb.rearrange("p (b h n) -> p h b n", b=TB, h=GH)
                for i in range(GH):
                    dve.wait_ge(s_ghi, i + 1)
                    part = xb[:, 4 * i:4 * i + 2]
                    dve.tensor_tensor(part[:, :, 1, :], g_by_head[:, i],
                                      part[:, :, 0, :].bitcast(F32), ALU.subtract)\
                        .then_inc(s_glo, 1)
                dve.wait_ge(s_glo, GH)
                dve.wait_ge(s_masks, 16)

            def scaled_queries(i, b):
                for d in range(2):
                    dve.wait_ge(s_dec, 4 * i + 2 * b + d + 2)
                    q = q_sb[:, d:d + 1, b * P:(b + 1) * P].broadcast_to([P, 8, P])
                    dve.tensor_tensor(qdec[:, d], dec[:, d], q, ALU.mult).then_inc(s_qd, 1)
                dve.wait_ge(s_k, i + 1)
                dve.wait_ge(s_kx, i + 1)
                dve.wait_ge(s_qd, 4 * i + 2 * b + 2)
                keys = k_sb[:, 1:2, b * P:(b + 1) * P].broadcast_to([P, 8, P])
                dve.tensor_tensor(dec[:, 1], dec[:, 1], keys, ALU.mult).then_inc(s_kd, 1)

            def masked(i, b, dst):
                dve.wait_ge(s_sc, 2 * i + b + 1)
                tmp = sq_a.rearrange("p a (l n) -> p (a l) n", l=2)
                dve.tensor_tensor(tmp, ps[:, 6:8, :].rearrange("p a (l n) -> p (a l) n", l=4),
                                  masks, ALU.mult).then_inc(s_msk, 1)
                dve.wait_ge(s_msk, 2 * i + b + 1)
                return dve.tensor_reduce(dst, tmp.rearrange("p l n -> p n l"), AX.X, ALU.add)

            def masked_second(i):
                masked(i, 1, att[:, S:3 * P])
                dve.tensor_copy(att[:, P:S], ps[:, 4, 0:P]).then_inc(s_att, 1)

            def values(i, after=None):
                g, cc = G_GLA + i * 6, C_GLA + i * 6
                for c in range(2):
                    sum_group(g + 2 + c, cc + 2 + c, c)
                    dve.wait_ge(s_read, g + 2 + c + 3)
                    for b in range(TB):
                        ins = dve.tensor_scalar(v_sb[:, b, c * HC:(c + 1) * HC], total[:, c, b, :],
                                                rstd[:, S + b:S + b + 1], None, ALU.mult)
                    ins.then_inc(s_v, 1)
                    if after:
                        after(c)

            def output_gates(h, i, between=None):
                g, cc = G_GLA + i * 6, C_GLA + i * 6
                for c in range(2):
                    sum_group(g + 4 + c, cc + 4 + c, c)
                    dve.wait_ge(s_read, g + 4 + c + 3)
                    dve.tensor_tensor(r_sb[:, 2 * c:2 * c + 2, :], total[:, c], per_token(2),
                                      ALU.mult).then_inc(s_r, 1)
                    if c == 0:
                        low(h, 26)
                        if between:
                            between()

            def gating(h, i):
                low(h, 3)
                dve.wait_ge(s_tanh, i)
                dve.scalar_tensor_tensor(out=r_sb, in0=e_sb, scalar=1.0, in1=r_sb, op0=ALU.add,
                                         op1=ALU.mult).then_inc(s_silu, 1)
                dve.wait_ge(s_oroot, i)
                dve.reciprocal(rstd_o, root_o).then_inc(s_orstd, 1)
                dve.wait_ge(s_silu, i)
                dve.wait_ge(s_orstd, i)
                dve.tensor_tensor(r_sb, r_sb, per_token(4, rstd_o), ALU.mult).then_inc(s_scaled, 1)
                dve.wait_ge(s_scaled, i)
                dve.wait_ge(s_ocp, i + 1)
                dve.tensor_tensor(o_sb, o_sb, r_sb, ALU.mult).then_inc(s_full, 1)
                lows(h, 4, 6)
                dve.wait_ge(s_fullhi, i)
                head = xb[:, bass.ds(4 * i - 4, 4)]
                dve.tensor_tensor(head[:, :, 1, :], o_sb, head[:, :, 0, :].bitcast(F32),
                                  ALU.subtract).then_inc(s_gated, 1)

            lows(H_GLA, 6, 10)
            queries_keys(0)
            lows(H_GLA, 10, 12)
            gates()
            lows(H_GLA, 12, 17)
            values(0, lambda c: low(H_GLA, 17) if c == 0 else None)
            low(H_GLA, 18)
            split_gates()
            lows(H_GLA, 19, 22)
            scaled_queries(0, 0)
            lows(H_GLA, 22, 24)
            masked(0, 0, att[:, 0:P]).then_inc(s_att, 1)
            low(H_GLA, 24)
            scaled_queries(0, 1)
            low(H_GLA, 25)
            output_gates(H_GLA, 0, lambda: masked_second(0))

            with dve.Fori(1, GH) as i:
                h = H_GLA + i * HEAD_HALVES
                gating(h, i)
                lows(h, 6, 10)
                queries_keys(i)
                scale_queries_keys(i)
                lows(h, 10, 12)
                scaled_queries(i, 0)
                lows(h, 12, 16)
                masked(i, 0, att[:, 0:P]).then_inc(s_att, 1)
                lows(h, 16, 18)
                values(i)
                scaled_queries(i, 1)
                lows(h, 18, 22)
                masked_second(i)
                lows(h, 22, 26)
                output_gates(h, i)

            gating(H_OUT, GH)
            lows(H_OUT, 6, PANEL + 2)
            down_tail(H_OUT, 0, R_OUT)
            down_panels(H_OUT, R_OUT, PANELS - 1, 1)
            last_panel(H_OUT + (PANELS - 1) * PANEL, PANELS - 1, R_OUT + 2 * (PANELS - 1), N_MLP0,
                       X_MLP0)
            def angles():
                dve.wait_ge(s_freqs, 16)
                dve.wait_ge(s_pos, 16)
                step(dve.tensor_copy(ang, pos_i))
                step(dve.tensor_scalar(ang, ang, freqs[:, 0:1], None, ALU.mult))
                step(dve.tensor_scalar(turns, ang, 1.0 / (2.0 * np.pi), ROUND, ALU.mult, ALU.add))
                step(dve.tensor_scalar(turns, turns, ROUND, None, ALU.subtract))
                for part in TWO_PI:
                    step(dve.scalar_tensor_tensor(out=ang, in0=turns, scalar=-part, in1=ang,
                                                  op0=ALU.mult, op1=ALU.add))
                step(dve.tensor_scalar(sin, ang, float(np.float32(np.pi)), -float(np.float32(np.pi)),
                                       ALU.min, ALU.max))
                step(dve.scalar_tensor_tensor(out=cos, in0=sin, scalar=-1.0, in1=sin, op0=ALU.mult,
                                              op1=ALU.max))
                dve.tensor_scalar(cos, cos, -1.0, float(np.pi / 2), ALU.mult, ALU.add)\
                    .then_inc(s_ang, 2)

            def end(h, r):
                angles()
                last_panel(h, PANELS - 1, r, N_KVIN, X_KV)

            mlp(H_MLP0, G_MLP0, 0, C_MLP0, R_MLP0, X_MLP0, N_MLP0, ST_MLP0, end)

            def queries_in(j):
                if 4 <= j < 8:
                    convert(resid, N_MIX1, xb, X_Q, 2 * (j - 4), 2 * (j - 4) + 2)

            first_panel(H_DKV, N_KVIN, ST_MIX1, X_KV, True, queries_in)

            def latent(g, cc, n):
                for c in range(2):
                    sum_group(g + c, cc + c, c)
                    dve.wait_ge(s_read, g + c + 3)
                    dve.tensor_tensor(lat[:, 2 * c:2 * c + 2, :], total[:, c], per_token(2),
                                      ALU.mult).then_inc(s_lat, 1)
                    dve.wait_ge(s_lat, n + c + 1)

            def normed(st, gain, dst, x0, n, between=None):
                factors(st, dst=rstd_c)
                for c in range(LT):
                    ins = dve.scalar_tensor_tensor(out=lat[:, c, :], in0=lat[:, c, :],
                                                   scalar=gains[:, gain + c:gain + c + 1],
                                                   in1=rstd_c, op0=ALU.mult, op1=ALU.mult)
                ins.then_inc(s_laty, 1)
                if between:
                    between()
                dve.wait_ge(s_laty, n)
                for c in range(LT):
                    dve.wait_ge(s_xhi, x0 + c + 1)
                    dve.tensor_tensor(dst[:, c, 1, :], lat[:, c, :], dst[:, c, 0, :].bitcast(F32),
                                      ALU.subtract).then_inc(s_x, 1)

            latent(G_DKV, C_DKV, 0)
            dve.wait_ge(s_sidehi, 2)
            dve.tensor_tensor(side1[:, 1, :], side_in1, side1[:, 0, :].bitcast(F32), ALU.subtract)\
                .then_inc(s_sidelo, 1)
            for j in range(2, 8):
                low(H_DQ, j)
                if j < 6:
                    convert(resid, N_MIX1, xb, X_Q, 2 * j + 4, 2 * j + 6)
            normed(ST_C, N_C, xc, X_C, 1)
            lows(H_DQ, 8, PANEL + 2)
            dve.wait_ge(s_x, X_C + LT)
            latent(G_DQ, C_DQ, 2)
            dve.wait_ge(s_low, 2)
            step(dve.tensor_copy(kr_tmp, ps[:, 4:6, ROPE:2 * ROPE]))
            step(dve.tensor_tensor(kr_tmp, ps[:, 4:6, 0:ROPE], kr_tmp, ALU.add))
            for b in range(TB):
                for n in range(2):
                    ins = dve.tensor_scalar(kr_nat[:, b, n * ROPE:(n + 1) * ROPE], kr_tmp[:, b, :],
                                            rstd[:, S + b:S + b + 1], None, ALU.mult)
            ins.then_inc(s_krn, 1)
            dve.wait_ge(s_krt, 1)
            dve.tensor_copy(raw_r, ps[:, 6, 0:S]).then_inc(s_krc, 1)
            dve.wait_ge(s_trig, 2)
            dve.wait_ge(s_krc, 1)
            step(dve.tensor_tensor(cos_r, raw_r, cos, ALU.mult))
            low(H_PAIR, 2)
            low(H_PAIR, 3, n=HF // 2)
            normed(ST_CQ, N_CQ, xq, X_CQ, 2,
                   lambda: sum_group(G_PAIR, C_PAIR, 0, dst=kt_sb[:, 0]))
            dve.wait_ge(s_krot, 1)
            step(dve.tensor_tensor(sin_r, ps[:, 6, S:2 * S], sin, ALU.mult))
            dve.wait_ge(s_krz, 1)
            for n in range(2):
                rows = slice(n * ROPE, (n + 1) * ROPE)
                dve.tensor_tensor(keys_r[rows, n, :], cos_r[rows, :], sin_r[rows, :], ALU.add)\
                    .then_inc(s_keysr, 1)
            dve.wait_ge(s_keysr, 2)
            dve.wait_ge(s_causal, 16)

            def rotated(i):
                dve.wait_ge(s_rot, i + 1)
                dve.tensor_tensor(sin_r, ps[:, 7, 0:S], sin, ALU.mult).then_inc(s_sinr, 1)

            def maxima(i):
                dve.wait_ge(s_dots, i + 1)
                mask = causal.rearrange("p (o n) -> p o n", o=1).broadcast_to([P, 2, 3 * P])
                dve.tensor_tensor(sc_sb, ps[:, 4:6, 0:3 * P], mask, ALU.add).then_inc(s_ms, 1)
                dve.wait_ge(s_ms, i + 1)
                dve.tensor_reduce(mx[:, 0:2], sc_sb[:, :, 0:P], AX.X, ALU.max)
                dve.tensor_reduce(mx[:, 2:4], sc_sb[:, :, P:3 * P], AX.X, ALU.max)\
                    .then_inc(s_max, 1)
                dve.wait_ge(s_max, i + 1)
                dve.tensor_scalar(nmx, mx, -MLA_SCALE, None, ALU.mult).then_inc(s_nmx, 1)

            def denominators(i):
                dve.wait_ge(s_exp, i + 1)
                dve.wait_ge(s_pr, i + 1)
                dve.reciprocal(rden, den).then_inc(s_rden, 1)

            def attended(i):
                dve.wait_ge(s_ohi, i + 1)
                pair = xb[:, bass.ds(2 * i, 2)]
                dve.tensor_tensor(pair[:, :, 1, :], ps[:, 6, :].rearrange("p (h s) -> p h s", h=2),
                                  pair[:, :, 0, :].bitcast(F32), ALU.subtract).then_inc(s_ox, 1)

            def slot(i, b, dotted=True, weighed=True):
                h, g, cc = H_PAIR + i * 4, G_PAIR + i * 4, C_PAIR + i * 4
                if dotted:
                    rotated(i - 1)
                    low(h, 2)
                    sum_group(g, cc, 0, dst=kt_sb[:, b])
                    low(h, 3, n=HF // 2)
                if dotted:
                    maxima(i - 1)
                low(h, 4)
                if weighed:
                    attended(i - 2)
                if dotted:
                    denominators(i - 1)
                sum_group(g + 1, cc + 1, 1, dst=vt_sb[:, b])
                low(h, 5)
                sum_group(g + 2, cc + 2, 0, dst=qn_sb[:, b])
                if dotted:
                    dve.wait_ge(s_qr, i)
                sum_group(g + 3, cc + 3, 1, dst=raw_r.rearrange("p (o s) -> p o s", o=1), banks=1)
                dve.wait_ge(s_read, g + 3 + 3)
                dve.sem_inc(s_raw, 1)

            slot(0, 0, dotted=False, weighed=False)
            slot(1, 1, weighed=False)
            with dve.Fori(1, PAIRS // 2) as m:
                slot(m * 2, 0)
                slot(m * 2 + 1, 1)
            rotated(PAIRS - 1)
            lows(H_WO, 2, 4)
            maxima(PAIRS - 1)
            attended(PAIRS - 2)
            denominators(PAIRS - 1)
            lows(H_WO, 4, 9)
            attended(PAIRS - 1)
            low(H_WO, 9)
            down_tail(H_WO, 0, R_WO)
            down_panels(H_WO, R_WO, PANELS - 1, 1)
            last_panel(H_WO + (PANELS - 1) * PANEL, PANELS - 1, R_WO + 2 * (PANELS - 1), N_MLP1,
                       X_MLP1)

            def end(h, r):
                lows(h, 4, PANEL)
                for c in range(2):
                    down(h, PANELS - 1, r, c)

            mlp(H_MLP1, G_MLP1, UP_GROUPS, C_MLP1, R_MLP1, X_MLP1, N_MLP1, ST_MLP1, end)
            dve.wait_ge(s_root, ST_FIN + 1)
            refined(rstd[:, S:S + TB], root[:, S:S + TB], ps[:, 7, S:S + TB], D)
            dve.wait_ge(s_rstd, ST_FIN + 1)
            for n, (b, c, bank) in enumerate(RESULT):
                if n % 2 == 0:
                    dve.wait_ge(s_fin, n + 1)
                    dve.tensor_scalar(o_nat[:, b, c * 512:(c + 1) * 512], ps[:, bank, :],
                                      rstd[:, S + b:S + b + 1], None, ALU.mult)\
                        .then_inc(s_finc[0], 1)


_INS = ["x", "positions", "norm_mix", "norm_mlp", "gla_w_in", "gla_w_gate_up", "gla_b_gate",
        "gla_norm", "gla_w_out", "kv_norm_in", "mla_w_dkv", "mla_kv_norm", "mla_w_uk", "mla_w_uv",
        "mla_w_dq", "mla_q_norm", "mla_w_uq", "mla_w_o", "mlp_w1", "mlp_w2", "final_norm"]


def kernel(**inputs):
    import concourse.bacc as bacc
    from concourse.bass_utils import run_bass_kernel_spmd

    nc = bacc.Bacc("TRN2", target_bir_lowering=False, num_devices=1)
    arrays, tensors = {}, {}
    given = {name: inputs[name] for name in _INS}
    for name, a in (*given.items(), *constants().items()):
        a = np.ascontiguousarray(a)
        arrays[f"in_{name}"] = a
        tensors[name] = nc.dram_tensor(f"in_{name}", a.shape, mybir.dt.from_np(a.dtype),
                                       kind="ExternalInput").ap()
    out = nc.dram_tensor("out", (1, S, D), F32, kind="ExternalOutput").ap()
    build(nc, tensors, out)
    return run_bass_kernel_spmd(nc, [arrays], core_ids=[0]).results[0]["out"]
```
